# Optimizing a Trainium2 kernel written in Bass

```python
import math
import jax, jax.numpy as jnp
from jax import lax
import numpy as np

D_MODEL = 1024
BATCH = 1
SEQ = 256
DEPTH = 2

D_SSD = D_MODEL
SSD_HEAD_DIM = 64
SSD_HEADS = D_SSD // SSD_HEAD_DIM
SSD_GROUPS = 4
SSD_HPG = SSD_HEADS // SSD_GROUPS
SSD_STATE = 128
CONV_K = 4
SSD_CHUNK = 128
CONV_CH = D_SSD + 2 * SSD_GROUPS * SSD_STATE

D_GMLP = D_MODEL
GMLP_CHUNK = 128
GMLP_HEADS = 8
GMLP_HEAD_DIM = D_GMLP // GMLP_HEADS

D_MIX = D_SSD + D_GMLP
D_IN = 2 * D_SSD + 2 * SSD_GROUPS * SSD_STATE + SSD_HEADS + 2 * D_GMLP

D_FF = 2816
N_EXPERTS = 8
TOP_K = 2

NORM_EPS = 1e-6

kernel_name = "hybrid_ssd_gmlp_moe_adaln_block"

def rms_norm(x, eps=NORM_EPS):
    x32 = x.astype(jnp.float32)
    y = x32 * lax.rsqrt(jnp.mean(x32 * x32, axis=-1, keepdims=True) + eps)
    return y.astype(x.dtype)

def causal_dwconv(u, w, bias):
    ch = u.shape[-1]
    out = lax.conv_general_dilated(
        u, w[:, None, :].astype(u.dtype), window_strides=(1,), padding=[(CONV_K - 1, 0)],
        dimension_numbers=("NWC", "WIO", "NWC"), feature_group_count=ch)
    return out + bias

def ssd_mixer(z, xs, bm, cm, dt_raw, conv_w, conv_b, dt_bias, a_log, d_skip, norm_w):
    b, l, _ = xs.shape
    nc = l // SSD_CHUNK
    xbc = jax.nn.silu(causal_dwconv(jnp.concatenate([xs, bm, cm], axis=-1), conv_w, conv_b))
    xs, bm, cm = jnp.split(xbc, [D_SSD, D_SSD + SSD_GROUPS * SSD_STATE], axis=-1)

    xh = xs.reshape(b, nc, SSD_CHUNK, SSD_GROUPS, SSD_HPG, SSD_HEAD_DIM)
    bc = bm.reshape(b, nc, SSD_CHUNK, SSD_GROUPS, SSD_STATE).astype(jnp.float32)
    cc = cm.reshape(b, nc, SSD_CHUNK, SSD_GROUPS, SSD_STATE).astype(jnp.float32)
    dt = jax.nn.softplus((dt_raw + dt_bias).astype(jnp.float32))
    dt = dt.reshape(b, nc, SSD_CHUNK, SSD_GROUPS, SSD_HPG)
    a = -jnp.exp(a_log.astype(jnp.float32)).reshape(SSD_GROUPS, SSD_HPG)
    a_cs = jnp.cumsum(dt * a, axis=2)
    xdt = xh.astype(jnp.float32) * dt[..., None]

    causal = jnp.tril(jnp.ones((SSD_CHUNK, SSD_CHUNK), dtype=bool))
    seg = a_cs[:, :, :, None] - a_cs[:, :, None]
    decay = jnp.exp(jnp.where(causal[None, None, :, :, None, None], seg, -jnp.inf))
    cb = jnp.einsum("bcqgn,bcsgn->bcqsg", cc, bc)
    y_diag = jnp.einsum("bcqsg,bcqsge,bcsgep->bcqgep", cb, decay, xdt)

    decay_states = jnp.exp(a_cs[:, :, -1:] - a_cs)
    states = jnp.einsum("bcsgn,bcsge,bcsgep->bcgepn", bc, decay_states, xdt)
    chunk_decay = jnp.exp(a_cs[:, :, -1])

    def step(h, inp):
        s_c, d_c = inp
        return d_c[..., None, None] * h + s_c, h

    h0 = jnp.zeros((b, SSD_GROUPS, SSD_HPG, SSD_HEAD_DIM, SSD_STATE), jnp.float32)
    _, prev = lax.scan(step, h0, (jnp.moveaxis(states, 1, 0), jnp.moveaxis(chunk_decay, 1, 0)))
    prev = jnp.moveaxis(prev, 0, 1)
    y_off = jnp.einsum("bcqgn,bcgepn,bcqge->bcqgep", cc, prev, jnp.exp(a_cs))

    y = y_diag + y_off + xh.astype(jnp.float32) * d_skip.reshape(SSD_GROUPS, SSD_HPG)[:, :, None]
    y = y.reshape(b, l, D_SSD).astype(z.dtype)
    return rms_norm(y * jax.nn.silu(z)) * norm_w

def gmlp_mixer(u, v, ws, bs, v_norm_w, out_norm_w):
    b, l, _ = u.shape
    nc = l // GMLP_CHUNK
    u = jax.nn.gelu(u).reshape(b, nc, GMLP_CHUNK, GMLP_HEADS, GMLP_HEAD_DIM)
    v = jax.nn.gelu(v).reshape(b, nc, GMLP_CHUNK, GMLP_HEADS, GMLP_HEAD_DIM)
    v = rms_norm(v) * v_norm_w.reshape(GMLP_HEADS, GMLP_HEAD_DIM)
    causal = jnp.tril(jnp.ones((GMLP_CHUNK, GMLP_CHUNK), dtype=bool))
    ws_m = jnp.where(causal[None], ws, jnp.zeros_like(ws))
    sv = jnp.einsum("hts,bcshd->bcthd", ws_m, v) + bs.T[None, None, :, :, None]
    y = (u * sv).reshape(b, l, D_GMLP)
    return rms_norm(y) * out_norm_w

def swiglu(h, w_gate, w_up, w_down):
    return (jax.nn.silu(h @ w_gate) * (h @ w_up)) @ w_down

def moe_swiglu(h, router_w, router_b, w_gate, w_up, w_down):
    logits = (h @ router_w + router_b).astype(jnp.float32)
    top_vals, top_idx = lax.top_k(logits, TOP_K)
    probs = jax.nn.softmax(top_vals, axis=-1)
    gates = jnp.sum(jax.nn.one_hot(top_idx, N_EXPERTS, dtype=probs.dtype) * probs[..., None], axis=-2)
    out = jnp.zeros(h.shape, jnp.float32)
    for e in range(N_EXPERTS):
        out = out + gates[..., e:e + 1] * swiglu(h, w_gate[e], w_up[e], w_down[e])
    return out.astype(h.dtype)

def setup_inputs(seed: int = 0) -> dict:
    key = jax.random.key(seed)
    ks = iter(jax.random.split(key, 40))
    n_dense = (DEPTH + 1) // 2
    n_moe = DEPTH // 2

    def nrm(shape, scale):
        return jax.random.normal(next(ks), shape, jnp.float32) * scale

    x = nrm((BATCH, SEQ, D_MODEL), 1.0)
    c = nrm((BATCH, D_MODEL), 1.0)
    ada_w = nrm((DEPTH, D_MODEL, 6 * D_MODEL), 0.5 * D_MODEL ** -0.5)
    ada_b = nrm((DEPTH, 6 * D_MODEL), 0.02)
    w_in = nrm((DEPTH, D_MODEL, D_IN), D_MODEL ** -0.5)
    conv_w = nrm((DEPTH, CONV_K, CONV_CH), CONV_K ** -0.5)
    conv_b = nrm((DEPTH, CONV_CH), 0.02)
    dt0 = jnp.exp(jax.random.uniform(next(ks), (DEPTH, SSD_HEADS), jnp.float32,
                                     math.log(1e-3), math.log(1e-1)))
    dt_bias = dt0 + jnp.log(-jnp.expm1(-dt0))
    a_log = jnp.log(jax.random.uniform(next(ks), (DEPTH, SSD_HEADS), jnp.float32, 1.0, 16.0))
    d_skip = 1.0 + nrm((DEPTH, SSD_HEADS), 0.1)
    ssd_norm_w = 1.0 + nrm((DEPTH, D_SSD), 0.05)
    gmlp_v_norm_w = 1.0 + nrm((DEPTH, D_GMLP), 0.05)
    gmlp_ws = nrm((DEPTH, GMLP_HEADS, GMLP_CHUNK, GMLP_CHUNK), GMLP_CHUNK ** -0.5)
    gmlp_bs = nrm((DEPTH, GMLP_HEADS, GMLP_CHUNK), 0.02)
    gmlp_out_norm_w = 1.0 + nrm((DEPTH, D_GMLP), 0.05)
    w_out = nrm((DEPTH, D_MIX, D_MODEL), D_MIX ** -0.5)
    dense_w_gate = nrm((n_dense, D_MODEL, D_FF), D_MODEL ** -0.5)
    dense_w_up = nrm((n_dense, D_MODEL, D_FF), D_MODEL ** -0.5)
    dense_w_down = nrm((n_dense, D_FF, D_MODEL), D_FF ** -0.5)
    router_w = nrm((n_moe, D_MODEL, N_EXPERTS), D_MODEL ** -0.5)
    router_b = nrm((n_moe, N_EXPERTS), 0.01)
    moe_w_gate = nrm((n_moe, N_EXPERTS, D_MODEL, D_FF), D_MODEL ** -0.5)
    moe_w_up = nrm((n_moe, N_EXPERTS, D_MODEL, D_FF), D_MODEL ** -0.5)
    moe_w_down = nrm((n_moe, N_EXPERTS, D_FF, D_MODEL), D_FF ** -0.5)
    final_norm_w = 1.0 + nrm((D_MODEL,), 0.05)
    return {"x": x, "c": c, "ada_w": ada_w, "ada_b": ada_b, "w_in": w_in,
            "conv_w": conv_w, "conv_b": conv_b, "dt_bias": dt_bias, "a_log": a_log,
            "d_skip": d_skip, "ssd_norm_w": ssd_norm_w, "gmlp_v_norm_w": gmlp_v_norm_w,
            "gmlp_ws": gmlp_ws, "gmlp_bs": gmlp_bs, "gmlp_out_norm_w": gmlp_out_norm_w,
            "w_out": w_out, "dense_w_gate": dense_w_gate, "dense_w_up": dense_w_up,
            "dense_w_down": dense_w_down, "router_w": router_w, "router_b": router_b,
            "moe_w_gate": moe_w_gate, "moe_w_up": moe_w_up, "moe_w_down": moe_w_down,
            "final_norm_w": final_norm_w}

def reference(x, c, ada_w, ada_b, w_in, conv_w, conv_b, dt_bias, a_log, d_skip, ssd_norm_w,
              gmlp_v_norm_w, gmlp_ws, gmlp_bs, gmlp_out_norm_w, w_out, dense_w_gate, dense_w_up,
              dense_w_down, router_w, router_b, moe_w_gate, moe_w_up, moe_w_down, final_norm_w):
    gs = SSD_GROUPS * SSD_STATE
    splits = list(np.cumsum([D_SSD, D_SSD, gs, gs, SSD_HEADS, D_GMLP]))
    cond = jax.nn.silu(c)
    for i in range(DEPTH):
        mod = (cond @ ada_w[i] + ada_b[i])[:, None, :]
        sh1, sc1, g1, sh2, sc2, g2 = jnp.split(mod, 6, axis=-1)

        h = rms_norm(x) * (1.0 + sc1) + sh1
        proj = h @ w_in[i]
        z, xs, bm, cm, dt_raw, u, v = jnp.split(proj, splits, axis=-1)
        y_ssd = ssd_mixer(z, xs, bm, cm, dt_raw, conv_w[i], conv_b[i], dt_bias[i], a_log[i],
                          d_skip[i], ssd_norm_w[i])
        y_gmlp = gmlp_mixer(u, v, gmlp_ws[i], gmlp_bs[i], gmlp_v_norm_w[i], gmlp_out_norm_w[i])
        mix = jnp.concatenate([y_ssd, y_gmlp], axis=-1) @ w_out[i]
        x = x + (1.0 + g1) * mix

        h = rms_norm(x) * (1.0 + sc2) + sh2
        j = i // 2
        if i % 2 == 0:
            f = swiglu(h, dense_w_gate[j], dense_w_up[j], dense_w_down[j])
        else:
            f = moe_swiglu(h, router_w[j], router_b[j], moe_w_gate[j], moe_w_up[j], moe_w_down[j])
        x = x + (1.0 + g2) * f
    return rms_norm(x) * final_norm_w


_drawn_inputs = setup_inputs


def setup_inputs(seed=0):
    import zlib

    import numpy as np

    out = dict(_drawn_inputs(seed))
    spreads = {}
    factors = {'router_b': 3.662}
    for name, (base, spread) in spreads.items():
        noise = np.random.default_rng([zlib.crc32(name.encode()), seed]).standard_normal(out[name].shape)
        drawn = base * np.exp(spread * noise) if base else spread * noise
        out[name] = __import__('jax').numpy.asarray(drawn.astype(out[name].dtype))
    for name, factor in factors.items():
        out[name] = (out[name] * factor).astype(out[name].dtype)
    return out
```

```python
from contextlib import ExitStack

import concourse.bass as bass
from concourse import mybir

F32 = mybir.dt.float32
F32R = mybir.dt.float32r
BF16 = mybir.dt.bfloat16
I32 = mybir.dt.int32
U32 = mybir.dt.uint32
ALU = mybir.AluOpType
ACT = mybir.ActivationFunctionType
AX_X = mybir.AxisListType.X

P = 128
D = 1024
KD = D // P
SEQ = 256
NT = SEQ // P
LAYERS = 2
HEADS = 16
HD = 64
GROUPS = 4
HPG = HEADS // GROUPS
STATE = 128
CONV_K = 4
PAD = CONV_K - 1
XBC = D + 2 * GROUPS * STATE
CX = XBC // P
GH = 8
FF = 2816
EXPERTS = 8
EPS = 1e-6
D_IN = 2 * D + 2 * GROUPS * STATE + HEADS + 2 * D
COL_Z, COL_XBC = 0, D
COL_DT = COL_XBC + XBC
COL_U = COL_DT + HEADS
COL_V = COL_U + D

UNIT = 2048
PANEL = UNIT // KD
RING = 6
NJ = FF // PANEL
KK = UNIT // D
SEG = 6
JOBS = 14
SMALL = 112
CONVB, SSDW, VNW, ONW, COND = 64, 80, 88, 96, 104
SH1, SC1, G1, SH2, SC2, G2 = range(6)
WIN = 4 * (D // PANEL) + (XBC - D) // PANEL
WOUT = 2 * D // (KK * P)


class Order:

    def __init__(self, eng, sem):
        self.eng, self.sem, self.n = eng, sem, 0

    def step(self, ins):
        ins.then_inc(self.sem, 1)
        self.n = self.n + 1

    def link(self, ins):
        self.step(ins)
        self.eng.wait_ge(self.sem, self.n)


def hybrid_trunk(nc, x_in, c_in, ada_w, ada_b, w_in, conv_w, conv_b, dt_bias, a_log, d_skip, ssd_norm_w,
                 gmlp_v_norm_w, gmlp_ws, gmlp_bs, gmlp_out_norm_w, w_out, dense_w_gate, dense_w_up,
                 dense_w_down, router_w, router_b, moe_w_gate, moe_w_up, moe_w_down, final_norm_w, out):
    with ExitStack() as ctx:
        free = [(nc.sbuf_base + 63) // 64 * 64]

        def place(name, shape, dt=F32, at=None):
            size = 1
            for s in shape[1:]:
                size *= s
            size = (size * (2 if dt == BF16 else 4) + 31) // 32 * 32
            if at is None:
                at = free[0]
                free[0] += size
                assert free[0] <= nc.sbuf_usable_end, (name, free[0])
            return nc.alloc_sbuf_tensor_at(name, shape, dt, offset=at), at

        raw, _ = place("raw", [P, RING, UNIT])
        wh, _ = place("wh", [P, 2, UNIT], F32R)
        wl, _ = place("wl", [P, 2, UNIT], F32R)
        adaw, _ = place("adaw", [P, 2, D])
        acc, _ = place("acc", [P, D])
        x, _ = place("x", [P, NT, D])
        xn, at_xn = place("xn", [P, NT, D])
        y, _ = place("y", [P, NT, D], at=at_xn)
        hTh, at_hTh = place("hTh", [P, KD, SEQ], F32R)
        hTl, at_hTl = place("hTl", [P, KD, SEQ], F32R)
        z, at_z = place("z", [P, NT, D])
        v, at_v = place("v", [P, NT, D])
        u, at_u = place("u", [P, KD, SEQ])
        padded, at_pad = place("padded", [P, CX, PAD + SEQ])
        xbc, at_xbc = place("xbc", [P, CX, SEQ])
        bmN, _ = place("bmN", [P, GROUPS, STATE])
        dec_in, at_a = place("dec_in", [P, 2, HPG, P])
        dec, at_e = place("dec", [P, 2, HPG, P])
        wsT, at_wsT = place("wsT", [P, GH, P])
        bsb, at_bs = place("bsb", [P, GH, P])
        xs, _ = place("xs", [P, NT, D], at=at_v)
        wsraw, _ = place("wsraw", [P, GH, P], at=at_a)
        sq, _ = place("sq", [P, KD, SEQ], at=at_a)
        gbc, _ = place("gbc", [P, D], at=at_a)
        diag, _ = place("diag", [P, KD, P], at=at_e)
        state, _ = place("state", [P, GROUPS, HPG * HD], at=at_bs)
        xdec, _ = place("xdec", [P, D], at=at_wsT)
        mgh, _ = place("mgh", [P, KD, SEQ], F32R, at=at_pad)
        mgl, _ = place("mgl", [P, KD, SEQ], F32R, at=at_pad + KD * SEQ * 4)
        msh, _ = place("msh", [P, KD, SEQ], F32R, at=at_xbc)
        msl, _ = place("msl", [P, KD, SEQ], F32R, at=at_xbc + KD * SEQ * 4)
        hT, _ = place("hT", [P, KD, SEQ], at=at_xbc)
        cbm, _ = place("cbm", [P, NT, GROUPS, P], at=at_hTh)
        yoff, _ = place("yoff", [P, HPG * HD], at=at_hTh + 4096)
        rroot, _ = place("rroot", [P, SEQ], at=at_hTh + 5120)
        gtmp, _ = place("gtmp", [P, 2, SEQ], at=at_hTh + 6144)
        gate, _ = place("gate", [P, NT, PANEL], at=at_u)
        actn, _ = place("actn", [P, NT, PANEL], at=at_u + 2048)
        actTh, _ = place("actTh", [P, KK, SEQ], F32R, at=at_u + 4096)
        actTl, _ = place("actTl", [P, KK, SEQ], F32R, at=at_u + 6144)
        mixed, _ = place("mixed", [P, NT, D], at=at_z)
        yh, _ = place("yh", [P, D], F32R, at=at_v)
        yl, _ = place("yl", [P, D], F32R, at=at_v + 4096)
        jobh = [place(f"jobh{b}", [P, KD, P], F32R, at=a)[0] for b, a in enumerate((at_hTh, at_hTl))]
        jobl = [place(f"jobl{b}", [P, KD, P], F32R, at=a + 4096)[0] for b, a in enumerate((at_hTh, at_hTl))]
        h32, _ = place("h32", [P, KD, P], at=at_xbc + 8192)
        pick, _ = place("pick", [P, NT, P], at=at_pad)
        put = [place(f"put{b}", [P, NT, P], F32R, at=at_pad + 1024 * (1 + b))[0] for b in range(2)]
        rt, _ = place("rt", [P, 256], at=at_pad + 3072)
        table, _ = place("table", [P, 16], I32, at=at_pad + 4096)
        tix, _ = place("tix", [P, NT, 8], U32, at=at_pad + 4160)
        fnw, _ = place("fnw", [P, D], at=at_e)

        ident, _ = place("ident", [P, P])
        upper, _ = place("upper", [P, P])
        strict, _ = place("strict", [P, P])
        ones, _ = place("ones", [P, P])
        slots, _ = place("slots", [P, P])
        small, _ = place("small", [P, P])
        pcol, _ = place("pcol", [P, LAYERS, SMALL])
        abcol, _ = place("abcol", [P, LAYERS, SEG * KD])
        mod, _ = place("mod", [P, LAYERS * SEG, KD])
        cond, _ = place("cond", [P, KD])
        hv, _ = place("hv", [P, 3, HEADS])
        dtw, _ = place("dtw", [P, KD, HEADS])
        rw, _ = place("rw", [P, KD, EXPERTS])
        rb, _ = place("rb", [P, EXPERTS])
        i8, _ = place("i8", [P, EXPERTS])
        epsb, _ = place("epsb", [P, 1])
        ss, _ = place("ss", [P, 8])
        vs, _ = place("vs", [P, NT * GH])
        dtt, _ = place("dtt", [P, 10, NT * HEADS])
        zeros, _ = place("zeros", [P, 512], BF16)

        B = [ctx.enter_context(nc.psum_tensor(f"bank{b}", [P, 512], F32)) for b in range(8)]

        def sem(name):
            return ctx.enter_context(nc.semaphore(name))

        landed = [sem(f"landed{s}") for s in range(RING)]
        ada_landed = [sem(f"ada_landed{s}") for s in range(2)]
        (hi_done, split_done, gemm_done, ada_used, mod_ps, mod_done, consts, small_landed, small_ps, small_used,
         cond_ready, x_landed, rms_done, xn_ready, xT_ps, hT_done, hTh_done, hTl_done, ws_landed, wsT_ps,
         wsT_done, dtw_landed, hv_landed, dt_ps, dt_abs, dt_exp, dA_done, acs_ps, acs_done, acs_exp, proj_evac,
         conv_done, silu_done, bs_landed, v_sq, v_sum, v_ms, v_done, sv_ps, gate_done, gsq_done, gss_ps, grms_done, u_done,
         mgh_done, mgl_done, xs_ps, xs_done, cb_ps, cb_done, skip_done, xdt_done, st_ps, st_done, decin_done,
         seg_ps, seg_done, decay_done, wdec_done, yd_ps, yo_ps, y_done, yz_done, yms_done, yn_done, yT_ps,
         msh_done, msl_done, diag_done, gb_ps, gb_done, x_done, act_order, dve_order, pool_order,
         sg_done, act_done, tp_ps, actTh_done, actT_done, r_landed, lg_ps, rdiff, rexp, mask_done, pos_ps,
         table_done, pick_done, gather_ps, h32_done, jobh_done, jobl_done, yh_done, yl_done, scat_ps, scat_done,
         fn_landed, out_done, stored) = [sem(n) for n in (
            "hi_done split_done gemm_done ada_used mod_ps mod_done consts small_landed small_ps small_used "
            "cond_ready x_landed rms_done xn_ready xT_ps hT_done hTh_done hTl_done ws_landed wsT_ps "
            "wsT_done dtw_landed hv_landed dt_ps dt_abs dt_exp dA_done acs_ps acs_done acs_exp proj_evac "
            "conv_done silu_done bs_landed v_sq v_sum v_ms v_done sv_ps gate_done gsq_done gss_ps grms_done u_done "
            "mgh_done mgl_done xs_ps xs_done cb_ps cb_done skip_done xdt_done st_ps st_done decin_done "
            "seg_ps seg_done decay_done wdec_done yd_ps yo_ps y_done yz_done yms_done yn_done yT_ps "
            "msh_done msl_done diag_done gb_ps gb_done x_done act_order dve_order pool_order "
            "sg_done act_done tp_ps actTh_done actT_done r_landed lg_ps rdiff rexp mask_done pos_ps "
            "table_done pick_done gather_ps h32_done jobh_done jobl_done yh_done yl_done scat_ps scat_done "
            "fn_landed out_done stored").split()]

        first_win = [0, WIN + WOUT + 3 * NJ]
        first_wout = [f + WIN for f in first_win]
        dense0 = first_wout[0] + WOUT
        moe0 = first_wout[1] + WOUT

        def win_col(i):
            for first, n in ((COL_XBC, XBC // PANEL), (COL_U, D // PANEL), (COL_V, D // PANEL), (COL_Z, D // PANEL)):
                if i < n:
                    return first + i * PANEL
                i -= n

        def panel(w, col):
            return w[:, bass.ds(col, PANEL)].rearrange("(k p) n -> p k n", p=P)

        def rows(w, row):
            return w[bass.ds(row, KK * P), :].rearrange("(k p) n -> p k n", p=P)

        block = ctx.enter_context(nc.Block())

        @block.sync
        def _(sp):
            def load(n, src, k, turn=0):
                if not (isinstance(turn, int) and n + RING * turn < RING):
                    sp.wait_ge(split_done, n + RING * turn - RING + 1)
                sp.dma_start(raw[:, n % RING].rearrange("p (k n) -> p k n", k=k), src).then_inc(landed[n % RING], 16)

            def load_ada(layer, seg, k):
                a = 8 * (SEG * layer + seg) + k
                if not (isinstance(a, int) and a < 2):
                    sp.wait_ge(ada_used, a - 1)
                sp.dma_start(adaw[:, k % 2], ada_w[layer, k * P:(k + 1) * P, bass.ds(seg * D, D)]).then_inc(ada_landed[k % 2], 16)

            for t in range(NT):
                sp.dma_start(x[:, t], x_in[0, t * P:(t + 1) * P, :]).then_inc(x_landed, 16)
            for k in range(KD):
                load_ada(0, SH1, k)
                if k == 1:
                    for layer in range(LAYERS):
                        if layer:
                            sp.wait_ge(small_used, 2)
                        for w, first in ((conv_w[layer].rearrange("j (c p) -> (j c) p", p=P), 0),
                                         (conv_b[layer].rearrange("(c p) -> c p", p=P), CONVB),
                                         (ssd_norm_w[layer].rearrange("(c p) -> c p", p=P), SSDW),
                                         (gmlp_v_norm_w[layer].rearrange("(c p) -> c p", p=P), VNW),
                                         (gmlp_out_norm_w[layer].rearrange("(c p) -> c p", p=P), ONW),
                                         (c_in[0].rearrange("(c p) -> c p", p=P), COND)):
                            sp.dma_start(small[first:first + w.shape[0], :], w).then_inc(small_landed, 16)
                        sp.wait_ge(small_used, 2 * layer + 1)
                        sp.dma_start(small[0:SEG * KD, :], ada_b[layer].rearrange("(c p) -> c p", p=P)).then_inc(small_landed, 16)
            for k in range(KD):
                load_ada(0, SC1, k)

            for layer in range(LAYERS):
                if layer:
                    sp.wait_ge(x_done, 2)
                sp.dma_start(wsraw[:], gmlp_ws[layer].rearrange("h t s -> t h s")).then_inc(ws_landed, 16)
                sp.dma_start(dtw[:], w_in[layer, :, COL_DT:COL_DT + HEADS].rearrange("(k p) n -> p k n", p=P)).then_inc(dtw_landed, 16)
                for n, w in enumerate((dt_bias, a_log, d_skip)):
                    sp.dma_start(hv[:, n], w[layer].partition_broadcast(P)).then_inc(hv_landed, 16)
                sp.dma_start(bsb[:].rearrange("p h t -> p (h t)"), gmlp_bs[layer].rearrange("h t -> (h t)").partition_broadcast(P)).then_inc(bs_landed, 16)
                for i in range(WIN):
                    load(first_win[layer] + i, panel(w_in[layer], win_col(i)), KD)
                    if layer == 0 and i < 16:
                        for k in (2 * i, 2 * i + 1):
                            load_ada(0, 2 + k // KD, k % KD)
                for i in range(WOUT):
                    load(first_wout[layer] + i, rows(w_out[layer], D * (1 - i // 4) + KK * P * (i % 4)), KK)
                    if layer == 0:
                        load_ada(1, 0, i)
                if layer == 0:
                    g, up, dn = dense_w_gate[0], dense_w_up[0], dense_w_down[0]
                    load(dense0, panel(g, 0), KD)
                    load(dense0 + 1, panel(up, 0), KD)
                    with sp.Fori(0, NJ // 2) as i:
                        for b in range(2):
                            n = dense0 + 2 + 3 * b
                            load(n, panel(g, (2 * i + b + 1) * PANEL), KD, i)
                            load(n + 1, panel(up, (2 * i + b + 1) * PANEL), KD, i)
                            load_ada(1, i + 1, 4 * b)
                            load_ada(1, i + 1, 4 * b + 1)
                            load(n + 2, rows(dn, (2 * i + b) * PANEL), KK, i)
                            load_ada(1, i + 1, 4 * b + 2)
                            load_ada(1, i + 1, 4 * b + 3)
                    load(dense0 + 3 * NJ - 1, rows(dn, (NJ - 1) * PANEL), KK)

            sp.dma_start(rw[:], router_w[0].rearrange("(k p) e -> p k e", p=P)).then_inc(r_landed, 16)
            sp.dma_start(rb[:], router_b[0].partition_broadcast(P)).then_inc(r_landed, 16)
            sp.wait_ge(table_done, 1)
            pairs = sp.value_load(table[0:1, 0:1], min_val=4, max_val=6)

            def experts(job):
                e = sp.value_load(table[0:1, bass.ds(job + 1, 1)], min_val=0, max_val=EXPERTS - 1)
                return [w[0, bass.ds(e, 1)].rearrange("e k n -> (e k) n") for w in (moe_w_gate, moe_w_up, moe_w_down)]

            g, up, dn = experts(0)
            load(moe0, panel(g, 0), KD)
            load(moe0 + 1, panel(up, 0), KD)
            with sp.Fori(0, pairs) as m:
                n0 = moe0 + 2
                g, up, dn = experts(2 * m)
                with sp.Fori(0, 5) as i:
                    for b in range(2):
                        load(n0 + 3 * b, panel(g, (2 * i + b + 1) * PANEL), KD, NJ * m + i)
                        load(n0 + 3 * b + 1, panel(up, (2 * i + b + 1) * PANEL), KD, NJ * m + i)
                        load(n0 + 3 * b + 2, rows(dn, (2 * i + b) * PANEL), KK, NJ * m + i)
                n0 += 30
                g2, up2, dn2 = experts(2 * m + 1)
                load(n0, panel(g2, 0), KD, NJ * m)
                load(n0 + 1, panel(up2, 0), KD, NJ * m)
                load(n0 + 2, rows(dn, (NJ - 1) * PANEL), KK, NJ * m)
                n0 += 3
                with sp.Fori(0, 5) as i:
                    for b in range(2):
                        load(n0 + 3 * b, panel(g2, (2 * i + b + 1) * PANEL), KD, NJ * m + i)
                        load(n0 + 3 * b + 1, panel(up2, (2 * i + b + 1) * PANEL), KD, NJ * m + i)
                        load(n0 + 3 * b + 2, rows(dn2, (2 * i + b) * PANEL), KK, NJ * m + i)
                n0 += 30
                g3, up3, _ = experts(2 * m + 2)
                load(n0, panel(g3, 0), KD, NJ * m)
                load(n0 + 1, panel(up3, 0), KD, NJ * m)
                load(n0 + 2, rows(dn2, (NJ - 1) * PANEL), KK, NJ * m)
            sp.wait_ge(x_done, 4)
            sp.dma_start(fnw[:], final_norm_w.partition_broadcast(P)).then_inc(fn_landed, 16)
            for t in range(NT):
                sp.wait_ge(out_done, t + 1)
                sp.dma_start(out[0, t * P:(t + 1) * P, :], xn[:, t]).then_inc(stored, 16)
            sp.wait_ge(stored, 16 * NT)

        @block.gpsimd
        def _(pool):
            o = Order(pool, pool_order)
            o.step(pool.memset(ones[:], 1.0))
            o.step(pool.memset(zeros[:], 0.0))
            o.step(pool.memset(epsb[:], EPS))
            o.step(pool.memset(ident[:], 0.0))
            o.step(pool.iota(slots[:], pattern=[[1, P]], base=0, channel_multiplier=0, allow_small_or_imprecise_dtypes=True))
            o.link(pool.iota(i8[:], pattern=[[1, EXPERTS]], base=0, channel_multiplier=0, allow_small_or_imprecise_dtypes=True))
            o.step(pool.affine_select(out=ident[:], in_=ident[:], compare_op=ALU.not_equal, fill=1.0, base=0,
                                      pattern=[[-1, P]], channel_multiplier=1))
            o.step(pool.affine_select(out=upper[:], in_=ones[:], compare_op=ALU.is_ge, fill=0.0, base=0,
                                      pattern=[[1, P]], channel_multiplier=-1))
            pool.affine_select(out=strict[:], in_=ones[:], compare_op=ALU.is_gt, fill=0.0, base=0,
                               pattern=[[1, P]], channel_multiplier=-1).then_inc(consts, 1)
            for layer in range(LAYERS):
                if layer:
                    pool.wait_ge(mgl_done, layer)
                    pool.wait_ge(x_done, 2 * layer)
                pool.memset(padded[:, :, 0:PAD], 0.0).then_inc(consts, 1)
                pool.wait_ge(xs_done, layer + 1)
                pool.wait_ge(hv_landed, 48 * (layer + 1))
                for t in range(NT):
                    ins = pool.tensor_tensor(y[:, t].rearrange("p (h d) -> p h d", h=HEADS), xs[:, t].rearrange("p (h d) -> p h d", h=HEADS),
                                             hv[:, 2].unsqueeze(2).broadcast_to([P, HEADS, HD]), ALU.mult)
                    if t == NT - 1:
                        ins.then_inc(skip_done, 1)
                pool.wait_ge(dA_done, layer + 1)
                pool.wait_ge(mgl_done, layer + 1)
                for i in range(2 * GROUPS):
                    c, g = divmod(i, GROUPS)
                    n = 8 * layer + i
                    if i >= 2:
                        pool.wait_ge(seg_ps, n - 1)
                    pool.tensor_tensor(dec_in[:, i % 2], upper[:].unsqueeze(1).broadcast_to([P, HPG, P]),
                                       dtt[:, 2, c * HEADS + HPG * g:c * HEADS + HPG * (g + 1)].unsqueeze(2).broadcast_to([P, HPG, P]),
                                       ALU.mult).then_inc(decin_done, 1)

        @block.scalar
        def _(act):
            o = Order(act, act_order)

            def hi(n, turn=0):
                act.wait_ge(landed[n % RING], 16 * (n // RING + 1) + 16 * turn)
                if not (isinstance(turn, int) and n < 2):
                    act.wait_ge(gemm_done, n - 1 + RING * turn)
                act.activation(wh[:, n % 2], raw[:, n % RING], ACT.Copy).then_inc(hi_done, 1)

            def root_mean(n):
                for t in range(NT):
                    o.step(act.activation(xn[:, t], x[:, t], ACT.Square, accum_out=ss[:, t:t + 1]))
                act.wait_ge(act_order, o.n)
                act.activation(ss[:, 2:4], ss[:, 0:2], ACT.Sqrt, bias=epsb[:, 0:1], scale=1.0 / D).then_inc(rms_done, 1)

            def turned_hi(n):
                for b in range(4):
                    act.wait_ge(hT_done, 4 * n + b + 1)
                    act.activation(hTh[:, 2 * b:2 * b + 2], hT[:, 2 * b:2 * b + 2], ACT.Copy).then_inc(hTh_done, 1)

            def gb_evac(n):
                act.wait_ge(gb_ps, n + 1)
                for half in range(2):
                    ins = act.activation(gbc[:, half * 512:half * 512 + 512], B[half][:], ACT.Copy)
                ins.then_inc(gb_done, 1)

            act.wait_ge(small_used, 1)
            act.activation(cond[:], pcol[:, 0, COND:COND + KD], ACT.Silu).then_inc(cond_ready, 1)
            act.wait_ge(consts, 1)
            act.wait_ge(x_landed, 16 * NT)
            norm = 0
            for layer in range(LAYERS):
                if layer:
                    act.wait_ge(x_done, 2 * layer)
                root_mean(norm)
                turned_hi(2 * layer)
                norm += 1
                act.wait_ge(dt_abs, layer + 1)
                act.activation(dtt[:, 1], dtt[:, 1], ACT.Exp, scale=-1.0).then_inc(dt_exp, 1)
                act.wait_ge(hv_landed, 48 * (layer + 1))
                act.activation(hv[:, 1], hv[:, 1], ACT.Exp).then_inc(dt_exp, 1)
                g0 = first_win[layer]
                hi(g0)
                hi(g0 + 1)
                for i in range(WIN):
                    act.wait_ge(gemm_done, g0 + i + 1)
                    ps = B[i % 2]
                    if i < 8:
                        if i == 0:
                            act.wait_ge(consts, 2 + layer)
                        ins = act.activation(padded[:, 2 * i:2 * i + 2, PAD:PAD + SEQ], ps[:].rearrange("p (c t) -> p c t", c=2), ACT.Copy)
                    elif i < 12:
                        ins = act.activation(u[:, 2 * (i - 8):2 * (i - 8) + 2], ps[:].rearrange("p (c t) -> p c t", c=2), ACT.Gelu_apprx_tanh)
                    elif i < 16:
                        ins = act.activation(v[:, :, PANEL * (i - 12):PANEL * (i - 11)], ps[:].rearrange("p (t n) -> p t n", t=NT), ACT.Gelu_apprx_tanh)
                    else:
                        ins = act.activation(z[:, :, PANEL * (i - 16):PANEL * (i - 15)], ps[:].rearrange("p (t n) -> p t n", t=NT), ACT.Silu)
                    ins.then_inc(proj_evac, 1)
                    if i + 2 < WIN:
                        hi(g0 + i + 2)
                    if i == 6:
                        act.wait_ge(acs_done, layer + 1)
                        act.activation(dtt[:, 5], dtt[:, 5], ACT.Exp).then_inc(acs_exp, 1)
                    if i >= 16:
                        for c in range(4 * (i - 16), 4 * (i - 15)):
                            act.wait_ge(conv_done, CX * layer + c + 1)
                            act.activation(xbc[:, c], xbc[:, c], ACT.Silu, bias=pcol[:, layer, CONVB + c:CONVB + c + 1]).then_inc(silu_done, 1)
                act.wait_ge(wsT_done, layer + 1)
                act.wait_ge(proj_evac, WIN * layer + 16)
                act.activation(sq[:].rearrange("p a b -> p (a b)"), v[:].rearrange("p a b -> p (a b)"), ACT.Square).then_inc(v_sq, 1)
                act.wait_ge(v_sum, layer + 1)
                act.activation(vs[:], vs[:], ACT.Sqrt, bias=epsb[:, 0:1], scale=1.0 / P).then_inc(v_ms, 1)
                for b in range(4):
                    act.wait_ge(gate_done, 4 * layer + b + 1)
                    act.activation(sq[:, 2 * b:2 * b + 2], u[:, 2 * b:2 * b + 2], ACT.Square).then_inc(gsq_done, 1)
                act.wait_ge(gss_ps, layer + 1)
                act.activation(B[0][:, 0:SEQ], B[0][:, 0:SEQ], ACT.Sqrt, bias=epsb[:, 0:1], scale=1.0 / D).then_inc(grms_done, 1)
                act.wait_ge(u_done, layer + 1)
                for h in range(GH):
                    act.activation(mgh[:, h], u[:, h], ACT.Copy, scale=pcol[:, layer, ONW + h:ONW + h + 1]).then_inc(mgh_done, 1)
                for n in range(4):
                    act.wait_ge(xs_ps, 5 * layer + n + 1)
                    t, half = divmod(n, 2)
                    act.activation(xs[:, t, half * 512:half * 512 + 512], B[4 + n][:], ACT.Copy)
                act.wait_ge(xs_ps, 5 * layer + 5)
                act.activation(bmN[:].rearrange("p g n -> p (g n)"), B[1][:], ACT.Copy).then_inc(xs_done, 1)
                act.wait_ge(st_ps, layer + 1)
                for b in range(2):
                    ins = act.activation(state[:, 2 * b:2 * b + 2].rearrange("p g n -> p (g n)"), B[2 + b][:], ACT.Copy)
                ins.then_inc(st_done, 1)
                for i in range(2 * GROUPS):
                    act.wait_ge(seg_done, 8 * layer + i + 1)
                    act.activation(dec[:, i % 2], dec[:, i % 2], ACT.Exp).then_inc(decay_done, 1)
                act.wait_ge(yz_done, layer + 1)
                for t in range(NT):
                    o.step(act.activation(z[:, t], y[:, t], ACT.Square, accum_out=ss[:, 4 + t:5 + t]))
                act.wait_ge(act_order, o.n)
                act.activation(ss[:, 6:8], ss[:, 4:6], ACT.Sqrt, bias=epsb[:, 0:1], scale=1.0 / D).then_inc(yms_done, 1)
                for k in range(KD):
                    act.wait_ge(yT_ps, 4 * layer + k // 2 + 1)
                    act.activation(msh[:, k], B[4 + k // 2][:, k % 2 * SEQ:k % 2 * SEQ + SEQ], ACT.Copy,
                                   scale=pcol[:, layer, SSDW + k:SSDW + k + 1]).then_inc(msh_done, 1)
                gb_evac(2 * layer)
                for i in range(WOUT):
                    hi(first_wout[layer] + i)
                act.wait_ge(x_done, 2 * layer + 1)
                root_mean(norm)
                norm += 1
                if layer == 0:
                    turned_hi(1)

                def silu_gate(n, F, turn, nt):
                    act.wait_ge(gemm_done, n + 1 + RING * turn)
                    act.wait_ge(act_done, F)
                    act.activation(gate[:, 0:nt], B[0][:].rearrange("p (t n) -> p t n", t=NT)[:, 0:nt], ACT.Silu).then_inc(sg_done, 1)

                def turned_product(F, nt):
                    act.wait_ge(tp_ps, F + 1)
                    act.activation(actTh[:, :, 0:nt * P], B[2][:].rearrange("p (k t) -> p k t", k=KK)[:, :, 0:nt * P], ACT.Copy).then_inc(actTh_done, 1)

                if layer == 0:
                    hi(dense0)
                    hi(dense0 + 1)
                    silu_gate(dense0, 0, 0, NT)
                    with act.Fori(0, NJ // 2) as i:
                        for b in range(2):
                            n, F = dense0 + 2 + 3 * b, 2 * i + b + 1
                            hi(n, i)
                            hi(n + 1, i)
                            silu_gate(n, F, i, NT)
                            turned_product(F - 1, NT)
                            hi(n + 2, i)
                    turned_product(NJ - 1, NT)
                    hi(dense0 + 3 * NJ - 1)
                    gb_evac(1)
            act.wait_ge(rdiff, 1)
            act.activation(rt[:, 0:2], rt[:, 0:2], ACT.Exp).then_inc(rexp, 1)
            act.wait_ge(table_done, 1)
            pairs = act.value_load(table[0:1, 0:1], min_val=4, max_val=6)

            def job_in(job, b):
                act.wait_ge(gather_ps, job + 1)
                act.activation(put[b][:].rearrange("p t n -> p (t n)"), B[3][:, 0:SEQ], ACT.Copy)
                act.wait_ge(h32_done, job + 1)
                act.activation(jobh[b][:], h32[:], ACT.Copy).then_inc(jobh_done, 1)

            def job_out(job, n, turn):
                act.wait_ge(gemm_done, n + 1 + RING * turn)
                act.wait_ge(scat_done, 2 * job + 1)
                for half in range(2):
                    ins = act.activation(yh[:, half * 512:half * 512 + 512], B[4 + half][:], ACT.Copy)
                ins.then_inc(yh_done, 1)

            def moe_iter(n, F, turn):
                hi(n, turn)
                hi(n + 1, turn)
                silu_gate(n, F, turn, 1)
                turned_product(F - 1, 1)
                hi(n + 2, turn)

            job_in(0, 0)
            hi(moe0)
            hi(moe0 + 1)
            silu_gate(moe0, NJ, 0, 1)
            with act.Fori(0, pairs) as m:
                n0, F0 = moe0 + 2, NJ + 22 * m
                job_in(2 * m + 1, 1)
                with act.Fori(0, 5) as i:
                    for b in range(2):
                        moe_iter(n0 + 3 * b, F0 + 2 * i + b + 1, NJ * m + i)
                n0 += 30
                moe_iter(n0, F0 + 11, NJ * m)
                job_out(2 * m, n0 + 2, NJ * m)
                job_in(2 * m + 2, 0)
                n0 += 3
                with act.Fori(0, 5) as i:
                    for b in range(2):
                        moe_iter(n0 + 3 * b, F0 + 2 * i + b + 12, NJ * m + i)
                n0 += 30
                moe_iter(n0, F0 + 22, NJ * m)
                job_out(2 * m + 1, n0 + 2, NJ * m)
            gb_evac(3)
            act.wait_ge(x_done, 4)
            root_mean(4)

        @block.tensor
        def _(pe):
            def three(ps, k, last, ah, al, bh, bl):
                pe.matmul(ps, ah, bh, start=(k == 0), stop=False, skip_group_check=True)
                pe.matmul(ps, ah, bl, start=False, stop=False, skip_group_check=True)
                return pe.matmul(ps, al, bh, start=False, stop=last, skip_group_check=True)

            def unit(n, turn):
                pe.wait_ge(split_done, n + 1 + RING * turn)

            def whl(n, k):
                return (w[:, n % 2].rearrange("p (k n) -> p k n", k=k) for w in (wh, wl))

            def natural(n, turn, ps_of, xh, xl, nt):
                unit(n, turn)
                h, l = whl(n, KD)
                for t in range(nt):
                    for k in range(KD):
                        ins = three(ps_of(t), k, k == KD - 1, xh[:, k, t * P:t * P + P], xl[:, k, t * P:t * P + P], h[:, k], l[:, k])
                ins.then_inc(gemm_done, 1)

            def turned(n, ps):
                unit(n, 0)
                h, l = whl(n, KD)
                for c in range(2):
                    for k in range(KD):
                        ins = three(ps[:, c * SEQ:c * SEQ + SEQ], k, k == KD - 1, h[:, k, c * P:c * P + P], l[:, k, c * P:c * P + P], hTh[:, k], hTl[:, k])
                ins.then_inc(gemm_done, 1)

            def deep(n, turn, xh, xl, k0, nt, start, last):
                unit(n, turn)
                h, l = whl(n, KK)
                for kk in range(KK):
                    for t in range(nt):
                        for half in range(2):
                            ps = B[4 + 2 * t + half][:]
                            ins = three(ps, 0 if start and kk == 0 else 1, last and kk == KK - 1, xh[:, k0 + kk, t * P:t * P + P],
                                        xl[:, k0 + kk, t * P:t * P + P], h[:, kk, half * 512:half * 512 + 512], l[:, kk, half * 512:half * 512 + 512])
                ins.then_inc(gemm_done, 1)

            def clear_acc(nt):
                for b in range(2 * nt):
                    pe.matmul(B[4 + b][:], zeros[0:1, 0:P], zeros[0:1, :], start=True, stop=False, skip_group_check=True)

            def mod_columns(s):
                pe.wait_ge(ada_used, 8 * (s + 1))
                if not (isinstance(s, int) and s == 0):
                    pe.wait_ge(mod_done, s)
                for k in range(KD):
                    ins = pe.matmul(B[3][:, k:k + 1], acc[:, k * P:k * P + P], ones[:, 0:1], start=True, stop=True, skip_group_check=True)
                ins.then_inc(mod_ps, 1)

            def turn_x(n):
                pe.wait_ge(xn_ready, n + 1)
                for b in range(4):
                    for c in range(4):
                        k, t = 2 * b + c // 2, c % 2
                        ins = pe.transpose(B[4 + b][:, c * P:c * P + P], xn[:, t, k * P:k * P + P], ident[:])
                    ins.then_inc(xT_ps, 1)

            def broadcast_gate(n):
                pe.wait_ge(diag_done, n + 1)
                for half in range(2):
                    ins = pe.matmul(B[half][:], ones[:], diag[:, 4 * half:4 * half + 4].rearrange("p k n -> p (k n)"), start=True, stop=True, skip_group_check=True)
                ins.then_inc(gb_ps, 1)

            pe.wait_ge(consts, 1)
            for i in range(2 * LAYERS):
                layer, b = divmod(i, 2)
                pe.wait_ge(small_landed, 16 * (7 * layer + (6, 7)[b]))
                rows_n = (SMALL, SEG * KD)[b]
                if i:
                    pe.wait_ge(small_used, i)
                pe.transpose(B[2][:, 0:rows_n], small[0:rows_n, :], ident[0:rows_n, 0:rows_n]).then_inc(small_ps, 1)
            mod_columns(SH1)
            mod_columns(SC1)

            for layer in range(LAYERS):
                pe.wait_ge(ws_landed, 16 * (layer + 1))
                if layer:
                    pe.wait_ge(x_done, 2 * layer)
                for h in range(GH):
                    ins = pe.transpose(B[h // 4][:, h % 4 * P:h % 4 * P + P], wsraw[:, h], ident[:])
                    if h % 4 == 3:
                        ins.then_inc(wsT_ps, 1)
                turn_x(2 * layer)
                pe.wait_ge(hT_done, 8 * layer + 4)
                pe.wait_ge(dtw_landed, 16 * (layer + 1))
                for t in range(NT):
                    for k in range(KD):
                        ins = pe.matmul(B[2][:, t * HEADS:(t + 1) * HEADS], hT[:, k, t * P:t * P + P], dtw[:, k], start=(k == 0), stop=(k == KD - 1), skip_group_check=True)
                ins.then_inc(dt_ps, 1)
                pe.wait_ge(hTl_done, 8 * layer + 4)
                pe.wait_ge(wsT_done, layer + 1)
                g0 = first_win[layer]
                for i in range(WIN):
                    if i >= 2:
                        pe.wait_ge(proj_evac, WIN * layer + i - 1)
                    if i < 12:
                        turned(g0 + i, B[i % 2])
                    else:
                        natural(g0 + i, 0, lambda t: B[i % 2][:, t * PANEL:(t + 1) * PANEL], hTh, hTl, NT)
                    if i == 3:
                        pe.wait_ge(dA_done, layer + 1)
                        for c in range(NT):
                            pe.matmul(B[2][:, c * HEADS:(c + 1) * HEADS], upper[:], dtt[:, 2, c * HEADS:(c + 1) * HEADS], start=True, stop=True, skip_group_check=True)
                        pe.matmul(B[2][:, 2 * HEADS:3 * HEADS], ones[:], dtt[:, 2, 0:HEADS], start=True, stop=True, skip_group_check=True).then_inc(acs_ps, 1)
                    if layer == 0 and i in (4, 8, 12, 16):
                        mod_columns(G1 + (i - 4) // 4)
                pe.wait_ge(v_done, layer + 1)
                for h in range(GH):
                    for c in range(NT):
                        ins = pe.matmul(B[4 + h // 2][:, (h % 2 * 2 + c) * P:(h % 2 * 2 + c + 1) * P], v[:, c, h * P:h * P + P], wsT[:, h], start=True, stop=True, skip_group_check=True)
                    if h % 2:
                        ins.then_inc(sv_ps, 1)
                pe.wait_ge(silu_done, CX * (layer + 1))
                pe.wait_ge(acs_done, layer + 1)
                pe.wait_ge(mod_done, SEG * (layer + 1))
                for c in range(NT):
                    for g in range(GROUPS):
                        ins = pe.matmul(B[2 + c][:, g * P:g * P + P], xbc[:, KD + g, c * P:c * P + P], xbc[:, KD + GROUPS + g, c * P:c * P + P], start=True, stop=True, skip_group_check=True)
                    ins.then_inc(cb_ps, 1)
                for n in range(4):
                    pe.wait_ge(gate_done, 4 * layer + n + 1)
                    t, half = divmod(n, 2)
                    for c in range(4):
                        ins = pe.transpose(B[4 + n][:, c * P:c * P + P], xbc[:, 4 * half + c, t * P:t * P + P], ident[:])
                    ins.then_inc(xs_ps, 1)
                pe.wait_ge(proj_evac, WIN * (layer + 1))
                for g in range(GROUPS):
                    ins = pe.transpose(B[1][:, g * P:g * P + P], xbc[:, KD + g, 0:P], ident[:])
                ins.then_inc(xs_ps, 1)
                for h in range(GH):
                    pe.wait_ge(gsq_done, 4 * layer + h // 2 + 1)
                    ins = pe.matmul(B[0][:, 0:SEQ], ones[:], sq[:, h], start=(h == 0), stop=(h == GH - 1), skip_group_check=True)
                ins.then_inc(gss_ps, 1)
                pe.wait_ge(xs_done, layer + 1)
                pe.wait_ge(xdt_done, layer + 1)
                pe.wait_ge(cb_done, 2 * layer + 2)
                for g in range(GROUPS):
                    ins = pe.matmul(B[2 + g // 2][:, g % 2 * 256:g % 2 * 256 + 256], bmN[:, g], xdec[:, g * 256:g * 256 + 256], start=True, stop=True, skip_group_check=True)
                ins.then_inc(st_ps, 1)
                pe.wait_ge(u_done, layer + 1)

                def segments(i):
                    if i >= 2:
                        pe.wait_ge(seg_done, 8 * layer + i - 1)
                    pe.wait_ge(decin_done, 8 * layer + i + 1)
                    pe.matmul(B[i % 2][:], ones[:], dec_in[:, i % 2].rearrange("p e q -> p (e q)"), start=True, stop=True, skip_group_check=True).then_inc(seg_ps, 1)

                def within(i):
                    c, g = divmod(i, GROUPS)
                    pe.wait_ge(wdec_done, 8 * layer + i + 1)
                    for e in range(HPG):
                        h = g * HPG + e
                        ins = pe.matmul(B[4 + i // 2][:, (i % 2 * HPG + e) * HD:(i % 2 * HPG + e + 1) * HD], dec[:, i % 2, e],
                                        xs[:, c, h * HD:(h + 1) * HD], start=True, stop=True, skip_group_check=True)
                    ins.then_inc(yd_ps, 1)

                segments(0)
                for i in range(2 * GROUPS):
                    if i + 1 < 2 * GROUPS:
                        segments(i + 1)
                    if i == 2:
                        pe.wait_ge(st_done, layer + 1)
                        for g in range(GROUPS):
                            ins = pe.matmul(B[2 + g // 2][:, g % 2 * 256:g % 2 * 256 + 256], xbc[:, KD + GROUPS + g, P:2 * P], state[:, g], start=True, stop=True, skip_group_check=True)
                        ins.then_inc(yo_ps, 1)
                    within(i)
                pe.wait_ge(yn_done, layer + 1)
                for b in range(4):
                    for c in range(4):
                        k, t = 2 * b + c // 2, c % 2
                        ins = pe.transpose(B[4 + b][:, c * P:c * P + P], y[:, t, k * P:k * P + P], ident[:])
                    ins.then_inc(yT_ps, 1)
                broadcast_gate(2 * layer)
                pe.wait_ge(mgl_done, layer + 1)
                pe.wait_ge(msl_done, layer + 1)
                for i in range(WOUT):
                    sh, sl = (mgh, mgl) if i < 4 else (msh, msl)
                    deep(first_wout[layer] + i, 0, sh, sl, KK * (i % 4), NT, i == 0, i == WOUT - 1)
                if layer == 0:
                    mod_columns(SEG)
                turn_x(2 * layer + 1)

                def turn_product(F, nt):
                    pe.wait_ge(act_done, F + 1)
                    if not (isinstance(F, int) and F == 0):
                        pe.wait_ge(actT_done, F)
                    for kk in range(KK):
                        for t in range(nt):
                            ins = pe.transpose(B[2][:, kk * SEQ + t * P:kk * SEQ + t * P + P], actn[:, t, kk * P:kk * P + P], ident[:])
                    ins.then_inc(tp_ps, 1)

                def gate_up(n, F, turn, xh, xl, nt, between):
                    pe.wait_ge(sg_done, F)
                    natural(n, turn, lambda t: B[0][:, t * PANEL:(t + 1) * PANEL], xh, xl, nt)
                    if between is not None:
                        turn_product(between, nt)
                    pe.wait_ge(act_done, F)
                    natural(n + 1, turn, lambda t: B[1][:, t * PANEL:(t + 1) * PANEL], xh, xl, nt)

                if layer == 0:
                    pe.wait_ge(hTl_done, 8)
                    clear_acc(NT)
                    gate_up(dense0, 0, 0, hTh, hTl, NT, None)
                    with pe.Fori(0, NJ // 2) as i:
                        for b in range(2):
                            n, F = dense0 + 2 + 3 * b, 2 * i + b + 1
                            gate_up(n, F, i, hTh, hTl, NT, F - 1)
                            pe.wait_ge(actT_done, F)
                            deep(n + 2, i, actTh, actTl, 0, NT, False, False)
                        mod_columns(SEG + 1 + i)
                    turn_product(NJ - 1, NT)
                    pe.wait_ge(actT_done, NJ)
                    deep(dense0 + 3 * NJ - 1, 0, actTh, actTl, 0, NT, False, True)
                    broadcast_gate(1)

            pe.wait_ge(hT_done, 16)
            pe.wait_ge(r_landed, 32)
            for t in range(NT):
                for k in range(KD):
                    ins = pe.matmul(B[2][:, t * EXPERTS:(t + 1) * EXPERTS], hT[:, k, t * P:t * P + P], rw[:, k], start=(k == 0), stop=(k == KD - 1), skip_group_check=True)
            ins.then_inc(lg_ps, 1)
            pe.wait_ge(mask_done, 1)
            mk = rt[:, 32:48]
            pe.matmul(B[2][:, 16:24], strict[:], mk[:, 0:8], start=True, stop=True, skip_group_check=True)
            pe.matmul(B[2][:, 24:32], strict[:], mk[:, 8:16], start=True, stop=False, skip_group_check=True)
            pe.matmul(B[2][:, 24:32], ones[:], mk[:, 0:8], start=False, stop=True, skip_group_check=True)
            pe.matmul(B[2][:, 32:40], ones[:], mk[:, 0:8], start=True, stop=False, skip_group_check=True)
            pe.matmul(B[2][:, 32:40], ones[:], mk[:, 8:16], start=False, stop=True, skip_group_check=True).then_inc(pos_ps, 1)
            pe.wait_ge(table_done, 1)
            pairs = pe.value_load(table[0:1, 0:1], min_val=4, max_val=6)

            def gather(job):
                pe.wait_ge(pick_done, job + 1)
                if not isinstance(job, int):
                    pe.wait_ge(scat_done, 2 * job - 1)
                    pe.wait_ge(jobh_done, job)
                for k in range(KD):
                    for t in range(NT):
                        pe.matmul(B[6 + k // 4][:, k % 4 * P:k % 4 * P + P], xn[:, t, k * P:k * P + P], pick[:, t], start=(t == 0), stop=(t == NT - 1), skip_group_check=True)
                for t in range(NT):
                    ins = pe.transpose(B[3][:, t * P:t * P + P], pick[:, t], ident[:])
                ins.then_inc(gather_ps, 1)

            def scatter(job, b):
                pe.wait_ge(yl_done, job + 1)
                pe.wait_ge(h32_done, job + 2)
                for t in range(NT):
                    pe.wait_ge(scat_done, 2 * job + t + 1)
                    for half in range(2):
                        for n, w in enumerate((yh, yl)):
                            ins = pe.matmul(B[6 + half][:], put[b][:, t], w[:, half * 512:half * 512 + 512], start=(n == 0), stop=(n == 1), skip_group_check=True)
                    ins.then_inc(scat_ps, 1)
                clear_acc(1)

            def moe_iter(n, F, turn, xb, last=False):
                gate_up(n, F, turn, jobh[xb], jobl[xb], 1, F - 1)
                pe.wait_ge(actT_done, F)
                deep(n + 2, turn, actTh, actTl, 0, 1, False, last)

            gather(0)
            pe.wait_ge(jobl_done, 1)
            clear_acc(1)
            gate_up(moe0, NJ, 0, jobh[0], jobl[0], 1, None)
            with pe.Fori(0, pairs) as m:
                n0, F0 = moe0 + 2, NJ + 22 * m
                gather(2 * m + 1)
                with pe.Fori(0, 5) as i:
                    for b in range(2):
                        moe_iter(n0 + 3 * b, F0 + 2 * i + b + 1, NJ * m + i, 0)
                n0 += 30
                pe.wait_ge(jobl_done, 2 * m + 2)
                moe_iter(n0, F0 + 11, NJ * m, 1, True)
                scatter(2 * m, 0)
                gather(2 * m + 2)
                n0 += 3
                with pe.Fori(0, 5) as i:
                    for b in range(2):
                        moe_iter(n0 + 3 * b, F0 + 2 * i + b + 12, NJ * m + i, 1)
                n0 += 30
                pe.wait_ge(jobl_done, 2 * m + 3)
                moe_iter(n0, F0 + 22, NJ * m, 0, True)
                scatter(2 * m + 1, 1)
            broadcast_gate(3)

        @block.vector
        def _(dve):
            o = Order(dve, dve_order)
            link, step = o.link, o.step

            def lo(n, turn=0):
                dve.wait_ge(hi_done, n + 1 + RING * turn)
                dve.tensor_tensor(wl[:, n % 2], raw[:, n % RING], wh[:, n % 2].bitcast(F32), ALU.subtract).then_inc(split_done, 1)

            def ada(layer, seg, k):
                a = 8 * (SEG * layer + seg) + k
                half = 4 * (SEG * layer + seg) + k // 2
                dve.wait_ge(ada_landed[k % 2], 16 * half + 16)
                if k == 0:
                    if not (isinstance(a, int) and a == 0):
                        dve.wait_ge(mod_ps, SEG * layer + seg)
                    dve.tensor_scalar(acc[:], adaw[:, 0], cond[:, 0:1], None, ALU.mult).then_inc(ada_used, 1)
                else:
                    dve.wait_ge(ada_used, a)
                    dve.scalar_tensor_tensor(acc[:], adaw[:, k % 2], cond[:, k:k + 1], acc[:], ALU.mult, ALU.add).then_inc(ada_used, 1)

            def mod_evac(layer, seg):
                s = SEG * layer + seg
                dve.wait_ge(mod_ps, s + 1)
                dve.tensor_tensor(mod[:, bass.ds(s, 1)].rearrange("p a k -> p (a k)"), B[3][:, 0:KD], abcol[:, layer, bass.ds(seg * KD, KD)], ALU.add).then_inc(mod_done, 1)

            def normalise(n):
                dve.wait_ge(rms_done, n + 1)
                link(dve.reciprocal(ss[:, 2:4], ss[:, 2:4]))
                for t in range(NT):
                    ins = dve.tensor_scalar(xn[:, t], x[:, t], ss[:, 2 + t:3 + t], None, ALU.mult)
                    if t < NT - 1:
                        step(ins)
                ins.then_inc(xn_ready, 1)

            def modulate(n, layer, shift, scale, low=True):
                dve.wait_ge(mod_done, SEG * layer + scale + 1)
                link(dve.tensor_scalar(mod[:, SEG * layer + scale], mod[:, SEG * layer + scale], 1.0, None, ALU.add))
                for b in range(4):
                    dve.wait_ge(xT_ps, 4 * n + b + 1)
                    for kk in range(2):
                        k = 2 * b + kk
                        ins = dve.tensor_scalar(hT[:, k], B[4 + b][:, kk * SEQ:kk * SEQ + SEQ], mod[:, SEG * layer + scale, k:k + 1],
                                                mod[:, SEG * layer + shift, k:k + 1], ALU.mult, ALU.add)
                    ins.then_inc(hT_done, 1)
                if low:
                    for b in range(4):
                        dve.wait_ge(hTh_done, 4 * n + b + 1)
                        dve.tensor_tensor(hTl[:, 2 * b:2 * b + 2], hT[:, 2 * b:2 * b + 2], hTh[:, 2 * b:2 * b + 2].bitcast(F32), ALU.subtract).then_inc(hTl_done, 1)

            def make_diag(n, layer, seg):
                dve.wait_ge(mod_done, SEG * layer + seg + 1)
                for k in range(KD):
                    ins = dve.tensor_scalar(diag[:, k], ident[:], mod[:, SEG * layer + seg, k:k + 1], None, ALU.mult)
                ins.then_inc(diag_done, 1)

            def residual(n, source, tmp):
                dve.wait_ge(gb_done, n + 1)
                for q in range(4):
                    t, half = divmod(q, 2)
                    link(dve.scalar_tensor_tensor(tmp(q), gbc[:, half * 512:half * 512 + 512], 1.0, source(q), ALU.add, ALU.mult))
                    ins = dve.tensor_tensor(x[:, t, half * 512:half * 512 + 512], x[:, t, half * 512:half * 512 + 512], tmp(q), ALU.add)
                    if q < 3:
                        step(ins)
                ins.then_inc(x_done, 1)

            def scratch(q):
                return diag[:, 4 * (q % 2):4 * (q % 2) + 4].rearrange("p k n -> p (k n)")

            dve.wait_ge(consts, 1)
            for i in range(2 * LAYERS):
                dve.wait_ge(small_ps, i + 1)
                layer, b = divmod(i, 2)
                if b == 0:
                    dve.tensor_copy(pcol[:, layer], B[2][:, 0:SMALL]).then_inc(small_used, 1)
                else:
                    dve.tensor_copy(abcol[:, layer], B[2][:, 0:SEG * KD]).then_inc(small_used, 1)
            dve.wait_ge(cond_ready, 1)
            for seg in (SH1, SC1):
                for k in range(KD):
                    ada(0, seg, k)
                if seg == SH1:
                    normalise(0)
                mod_evac(0, seg)

            norm = 0
            for layer in range(LAYERS):
                if layer:
                    normalise(2 * layer)
                for b in range(2):
                    dve.wait_ge(wsT_ps, 2 * layer + b + 1)
                    ins = dve.tensor_tensor(wsT[:, 4 * b:4 * b + 4], B[b][:].rearrange("p (h t) -> p h t", h=4), upper[:].unsqueeze(1).broadcast_to([P, 4, P]), ALU.mult)
                ins.then_inc(wsT_done, 1)
                modulate(2 * layer, layer, SH1, SC1)
                dve.wait_ge(dt_ps, layer + 1)
                dve.wait_ge(hv_landed, 48 * (layer + 1))
                T = [dtt[:, n] for n in range(10)]
                link(dve.tensor_tensor(T[0].rearrange("p (c h) -> p c h", c=NT), B[2][:, 0:NT * HEADS].rearrange("p (c h) -> p c h", c=NT),
                                       hv[:, 0].unsqueeze(1).broadcast_to([P, NT, HEADS]), ALU.add))
                link(dve.tensor_scalar(T[1], T[0], -1.0, None, ALU.mult))
                dve.tensor_tensor(T[1], T[0], T[1], ALU.max).then_inc(dt_abs, 1)
                g0 = first_win[layer]
                dve.wait_ge(dt_exp, 2 * layer + 2)
                link(dve.tensor_scalar(T[3], T[1], 2.0, None, ALU.add))
                link(dve.reciprocal(T[3], T[3]))
                link(dve.tensor_tensor(T[3], T[3], T[1], ALU.mult))
                link(dve.tensor_tensor(T[4], T[3], T[3], ALU.mult))
                link(dve.tensor_scalar(T[5], T[4], 1.0 / 15, 1.0 / 13, ALU.mult, ALU.add))
                for c in (11, 9, 7, 5, 3, 1):
                    link(dve.tensor_tensor(T[5], T[5], T[4], ALU.mult))
                    link(dve.tensor_scalar(T[5], T[5], 1.0 / c, None, ALU.add))
                link(dve.scalar_tensor_tensor(T[3], T[3], 2.0, T[5], ALU.mult, ALU.mult))
                link(dve.tensor_scalar(T[0], T[0], 0.0, None, ALU.max))
                link(dve.tensor_tensor(T[0], T[0], T[3], ALU.add))
                dve.scalar_tensor_tensor(T[2].rearrange("p (c h) -> p c h", c=NT), T[0].rearrange("p (c h) -> p c h", c=NT), -1.0,
                                         hv[:, 1].unsqueeze(1).broadcast_to([P, NT, HEADS]), ALU.mult, ALU.mult).then_inc(dA_done, 1)
                lo(g0)
                lo(g0 + 1)
                conv = 0
                for i in range(WIN):
                    if layer == 0 and i < 16:
                        ada(0, 2 + 2 * i // KD, 2 * i % KD)
                        ada(0, 2 + 2 * i // KD, 2 * i % KD + 1)
                    if i + 2 < WIN:
                        lo(g0 + i + 2)
                    if layer == 0 and i in (5, 9, 13, 17):
                        mod_evac(0, G1 + (i - 5) // 4)
                    if i == 5:
                        dve.wait_ge(acs_ps, layer + 1)
                        link(dve.tensor_copy(T[4], B[2][:, 0:NT * HEADS]))
                        step(dve.tensor_tensor(T[5][:, 0:HEADS], B[2][:, 2 * HEADS:3 * HEADS], T[4][:, 0:HEADS], ALU.subtract))
                        dve.tensor_copy(T[5][:, HEADS:2 * HEADS], T[4][:, HEADS:2 * HEADS]).then_inc(acs_done, 1)
                    if 3 <= i < 3 + CX:
                        c = i - 3
                        dve.wait_ge(proj_evac, WIN * layer + c // 2 + 1)
                        wc = pcol[:, layer]
                        link(dve.tensor_scalar(xbc[:, c], padded[:, c, 0:SEQ], wc[:, c:c + 1], None, ALU.mult))
                        for j in range(1, CONV_K):
                            ins = dve.scalar_tensor_tensor(xbc[:, c], padded[:, c, j:j + SEQ], wc[:, j * CX + c:j * CX + c + 1], xbc[:, c], ALU.mult, ALU.add)
                            if j < CONV_K - 1:
                                link(ins)
                        ins.then_inc(conv_done, 1)
                dve.wait_ge(v_sq, layer + 1)
                dve.tensor_reduce(vs[:], sq[:].rearrange("p a (h d) -> p (a h) d", d=P), AX_X, ALU.add).then_inc(v_sum, 1)
                dve.wait_ge(v_ms, layer + 1)
                link(dve.reciprocal(vs[:], vs[:]))
                vh = v[:].rearrange("p t (h d) -> p (t h) d", d=P)
                dve.tensor_tensor(vh, vh, vs[:].unsqueeze(2).broadcast_to([P, NT * GH, P]), ALU.mult).then_inc(v_done, 1)
                for c in range(NT):
                    dve.wait_ge(cb_ps, 2 * layer + c + 1)
                    dve.tensor_tensor(cbm[:, c], B[2 + c][:].rearrange("p (g q) -> p g q", g=GROUPS), upper[:].unsqueeze(1).broadcast_to([P, GROUPS, P]), ALU.mult).then_inc(cb_done, 1)
                dve.wait_ge(bs_landed, 16 * (layer + 1))
                for h in range(GH):
                    if h % 2 == 0:
                        dve.wait_ge(sv_ps, 4 * layer + h // 2 + 1)
                    tmp = gtmp[:, h % 2].rearrange("p (c t) -> p c t", c=NT)
                    link(dve.scalar_tensor_tensor(tmp, B[4 + h // 2][:, h % 2 * SEQ:h % 2 * SEQ + SEQ].rearrange("p (c t) -> p c t", c=NT),
                                                  pcol[:, layer, VNW + h:VNW + h + 1], bsb[:, h].unsqueeze(1).broadcast_to([P, NT, P]), ALU.mult, ALU.add))
                    ins = dve.tensor_tensor(u[:, h].rearrange("p (c t) -> p c t", c=NT), u[:, h].rearrange("p (c t) -> p c t", c=NT), tmp, ALU.mult)
                    if h % 2:
                        ins.then_inc(gate_done, 1)
                    else:
                        step(ins)
                dve.wait_ge(grms_done, layer + 1)
                link(dve.reciprocal(rroot[:], B[0][:, 0:SEQ]))
                dve.tensor_tensor(u[:], u[:], rroot[:].unsqueeze(1).broadcast_to([P, KD, SEQ]), ALU.mult).then_inc(u_done, 1)
                for h in range(GH):
                    dve.wait_ge(mgh_done, GH * layer + h + 1)
                    if h == 0:
                        dve.wait_ge(u_done, layer + 1)
                    ins = dve.scalar_tensor_tensor(mgl[:, h], u[:, h], pcol[:, layer, ONW + h:ONW + h + 1], mgh[:, h].bitcast(F32), ALU.mult, ALU.subtract)
                ins.then_inc(mgl_done, 1)
                dve.wait_ge(xs_done, layer + 1)
                dve.wait_ge(skip_done, layer + 1)
                dve.wait_ge(acs_exp, layer + 1)
                for t in range(NT):
                    xt = xs[:, t].rearrange("p (h d) -> p h d", h=HEADS)
                    link(dve.tensor_tensor(xt, xt, T[0][:, t * HEADS:(t + 1) * HEADS].unsqueeze(2).broadcast_to([P, HEADS, HD]), ALU.mult))
                dve.tensor_tensor(xdec[:].rearrange("p (h d) -> p h d", h=HEADS), xs[:, 0].rearrange("p (h d) -> p h d", h=HEADS),
                                  T[5][:, 0:HEADS].unsqueeze(2).broadcast_to([P, HEADS, HD]), ALU.mult).then_inc(xdt_done, 1)

                def gather_y(i):
                    c, g = divmod(i, GROUPS)
                    yt = y[:, c, g * 256:g * 256 + 256]
                    dve.wait_ge(yd_ps, 8 * layer + (i | 1) + 1)
                    link(dve.tensor_tensor(yt, yt, B[4 + i // 2][:, i % 2 * 256:i % 2 * 256 + 256], ALU.add))
                    if c:
                        dve.wait_ge(yo_ps, layer + 1)
                        link(dve.tensor_tensor(yoff[:].rearrange("p (e d) -> p e d", e=HPG), B[2 + g // 2][:, g % 2 * 256:g % 2 * 256 + 256].rearrange("p (e d) -> p e d", e=HPG),
                                               T[5][:, HEADS + g * HPG:HEADS + (g + 1) * HPG].unsqueeze(2).broadcast_to([P, HPG, HD]), ALU.mult))
                        step(dve.tensor_tensor(yt, yt, yoff[:], ALU.add))

                def segment(i):
                    c, g = divmod(i, GROUPS)
                    dve.wait_ge(seg_ps, 8 * layer + i + 1)
                    if i >= 2:
                        dve.wait_ge(yd_ps, 8 * layer + i - 1)
                    for e in range(HPG):
                        h = c * HEADS + g * HPG + e
                        ins = dve.tensor_scalar(dec[:, i % 2, e], B[i % 2][:, e * P:e * P + P], T[4][:, h:h + 1], 0.0, ALU.subtract, ALU.min)
                    ins.then_inc(seg_done, 1)

                segment(0)
                for i in range(2 * GROUPS):
                    c, g = divmod(i, GROUPS)
                    if i + 1 < 2 * GROUPS:
                        segment(i + 1)
                    if i % 2 == 0 and i:
                        gather_y(i - 2)
                        gather_y(i - 1)
                    dve.wait_ge(decay_done, 8 * layer + i + 1)
                    dve.tensor_tensor(dec[:, i % 2], dec[:, i % 2], cbm[:, c, g].unsqueeze(1).broadcast_to([P, HPG, P]), ALU.mult).then_inc(wdec_done, 1)
                gather_y(6)
                gather_y(7)
                dve.wait_ge(dve_order, o.n)
                dve.wait_ge(proj_evac, WIN * (layer + 1))
                for t in range(NT):
                    ins = dve.tensor_tensor(y[:, t], y[:, t], z[:, t], ALU.mult)
                    if t < NT - 1:
                        step(ins)
                ins.then_inc(yz_done, 1)
                dve.wait_ge(yms_done, layer + 1)
                link(dve.reciprocal(ss[:, 6:8], ss[:, 6:8]))
                for t in range(NT):
                    ins = dve.tensor_scalar(y[:, t], y[:, t], ss[:, 6 + t:7 + t], None, ALU.mult)
                    if t < NT - 1:
                        step(ins)
                ins.then_inc(yn_done, 1)
                make_diag(2 * layer, layer, G1)
                for k in range(KD):
                    dve.wait_ge(msh_done, KD * layer + k // 2 * 2 + 2)
                    ins = dve.scalar_tensor_tensor(msl[:, k], B[4 + k // 2][:, k % 2 * SEQ:k % 2 * SEQ + SEQ], pcol[:, layer, SSDW + k:SSDW + k + 1],
                                                   msh[:, k].bitcast(F32), ALU.mult, ALU.subtract)
                ins.then_inc(msl_done, 1)
                for i in range(WOUT):
                    lo(first_wout[layer] + i)
                    if layer == 0:
                        ada(1, 0, i)
                if layer == 0:
                    mod_evac(1, SH1)
                dve.wait_ge(gemm_done, first_wout[layer] + WOUT)
                residual(2 * layer, lambda q: B[4 + q][:], scratch)
                normalise(2 * layer + 1)
                modulate(2 * layer + 1, layer, SH2, SC2, low=(layer == 0))

                def product(n, F, turn, nt):
                    dve.wait_ge(sg_done, F + 1)
                    dve.wait_ge(gemm_done, n + 2 + RING * turn)
                    dve.tensor_tensor(actn[:, 0:nt], gate[:, 0:nt], B[1][:].rearrange("p (t n) -> p t n", t=NT)[:, 0:nt], ALU.mult).then_inc(act_done, 1)

                def turned_low(F, nt):
                    dve.wait_ge(actTh_done, F + 1)
                    dve.tensor_tensor(actTl[:, :, 0:nt * P], B[2][:].rearrange("p (k t) -> p k t", k=KK)[:, :, 0:nt * P],
                                      actTh[:, :, 0:nt * P].bitcast(F32), ALU.subtract).then_inc(actT_done, 1)

                if layer == 0:
                    lo(dense0)
                    lo(dense0 + 1)
                    product(dense0, 0, 0, NT)
                    with dve.Fori(0, NJ // 2) as i:
                        for b in range(2):
                            n, F = dense0 + 2 + 3 * b, 2 * i + b + 1
                            lo(n, i)
                            lo(n + 1, i)
                            ada(1, i + 1, 4 * b)
                            ada(1, i + 1, 4 * b + 1)
                            turned_low(F - 1, NT)
                            lo(n + 2, i)
                            product(n, F, i, NT)
                            ada(1, i + 1, 4 * b + 2)
                            ada(1, i + 1, 4 * b + 3)
                        mod_evac(1, i + 1)
                    turned_low(NJ - 1, NT)
                    lo(dense0 + 3 * NJ - 1)
                    make_diag(1, 0, G2)
                    dve.wait_ge(gemm_done, dense0 + 3 * NJ)
                    residual(1, lambda q: B[4 + q][:], scratch)

            DIFF, P1, MX, MASK, GATE, OH, POS, CNT, RANK, SEL = (rt[:, 0:2], rt[:, 2:4], rt[:, 16:32], rt[:, 32:48], rt[:, 48:64],
                                                               rt[:, 64:80], rt[:, 80:96], rt[:, 96:104], rt[:, 104:112], rt[:, 112:120])
            LG, IX, JP, JG, JE, CUR, TMP8, NOV = (rt[:, 120:136], rt[:, 136:152], rt[:, 152:180], rt[:, 180:208], rt[:, 208:224],
                                                  rt[:, 224:228], rt[:, 228:236], rt[:, 236:240])

            def v3(a):
                return a.rearrange("p (t e) -> p t e", t=NT)

            link(dve.memset(rt[:], 0.0))
            dve.wait_ge(lg_ps, 1)
            link(dve.tensor_tensor(v3(LG), B[2][:, 0:16].rearrange("p (t e) -> p t e", t=NT), rb[:].unsqueeze(1).broadcast_to([P, NT, EXPERTS]), ALU.add))
            for t in range(NT):
                link(dve.max(MX[:, 8 * t:8 * t + 8], LG[:, 8 * t:8 * t + 8]))
                link(dve.max_index(tix[:, t], MX[:, 8 * t:8 * t + 8], LG[:, 8 * t:8 * t + 8]))
            link(dve.tensor_copy(v3(IX), tix[:]))
            dve.tensor_tensor(DIFF, v3(MX)[:, :, 1], v3(MX)[:, :, 0], ALU.subtract).then_inc(rdiff, 1)
            dve.wait_ge(rexp, 1)
            link(dve.tensor_scalar(P1, DIFF, 1.0, None, ALU.add))
            link(dve.reciprocal(P1, P1))
            link(dve.tensor_tensor(DIFF, DIFF, P1, ALU.mult))
            for t in range(NT):
                e8 = slice(8 * t, 8 * t + 8)
                link(dve.tensor_scalar(MASK[:, e8], i8[:], IX[:, 8 * t:8 * t + 1], None, ALU.is_equal))
                link(dve.tensor_scalar(OH[:, e8], i8[:], IX[:, 8 * t + 1:8 * t + 2], None, ALU.is_equal))
                link(dve.tensor_scalar(GATE[:, e8], MASK[:, e8], P1[:, t:t + 1], None, ALU.mult))
                link(dve.scalar_tensor_tensor(GATE[:, e8], OH[:, e8], DIFF[:, t:t + 1], GATE[:, e8], ALU.mult, ALU.add))
                ins = dve.tensor_tensor(MASK[:, e8], MASK[:, e8], OH[:, e8], ALU.add)
                if t < NT - 1:
                    link(ins)
            ins.then_inc(mask_done, 1)
            dve.wait_ge(mask_done, 1)
            link(dve.memset(JP, -1.0))
            dve.wait_ge(pos_ps, 1)
            link(dve.scalar_tensor_tensor(POS, B[2][:, 16:32], 1.0, MASK, ALU.add, ALU.mult))
            link(dve.tensor_scalar(POS, POS, -1.0, None, ALU.add))
            link(dve.tensor_scalar(CNT, B[2][:, 32:40], float(P), None, ALU.is_gt))
            for e in range(1, EXPERTS):
                link(dve.tensor_tensor(RANK[:, e:e + 1], RANK[:, e - 1:e], CNT[:, e - 1:e], ALU.add))
            link(dve.tensor_tensor(NOV[:, 0:1], RANK[:, 7:8], CNT[:, 7:8], ALU.add))
            link(dve.tensor_scalar(NOV[:, 1:2], NOV[:, 0:1], 1.0, None, ALU.is_ge))
            link(dve.tensor_scalar(NOV[:, 2:3], NOV[:, 0:1], 3.0, 4.0, ALU.is_ge, ALU.add))
            link(dve.tensor_tensor(JE[:, 0:1], NOV[:, 1:2], NOV[:, 2:3], ALU.add))
            link(dve.tensor_copy(JE[:, 1:9], i8[:]))
            JP3, JG3 = (a.rearrange("p (t j) -> p t j", t=NT) for a in (JP, JG))
            link(dve.tensor_copy(JP3[:, :, 0:8], v3(POS)))
            link(dve.tensor_copy(JG3[:, :, 0:8], v3(GATE)))
            for k in range(4):
                link(dve.scalar_tensor_tensor(SEL, RANK, float(k), CNT, ALU.is_equal, ALU.mult))
                link(dve.scalar_tensor_tensor(TMP8, i8[:], 0.0, SEL, ALU.add, ALU.mult))
                link(dve.tensor_reduce(JE[:, 9 + k:10 + k], TMP8, AX_X, ALU.add))
                for t in range(NT):
                    e8 = slice(8 * t, 8 * t + 8)
                    link(dve.scalar_tensor_tensor(TMP8, POS[:, e8], 1.0 - P, SEL, ALU.add, ALU.mult))
                    link(dve.tensor_reduce(JP3[:, t, 8 + k:9 + k], TMP8, AX_X, ALU.add))
                    link(dve.tensor_scalar(JP3[:, t, 8 + k:9 + k], JP3[:, t, 8 + k:9 + k], -1.0, None, ALU.add))
                    link(dve.tensor_tensor(TMP8, GATE[:, e8], SEL, ALU.mult))
                    link(dve.tensor_reduce(JG3[:, t, 8 + k:9 + k], TMP8, AX_X, ALU.add))
            dve.memset(mixed[:], 0.0).then_inc(scat_done, 1)
            dve.wait_ge(scat_done, 1)
            dve.tensor_copy(table[:, 0:16], JE).then_inc(table_done, 1)
            dve.wait_ge(table_done, 1)
            pairs = dve.value_load(table[0:1, 0:1], min_val=4, max_val=6)

            def make_pick(job):
                link(dve.tensor_copy(CUR[:, 0:2].unsqueeze(2), JP3[:, :, bass.ds(job, 1)]))
                for t in range(NT):
                    ins = dve.tensor_scalar(pick[:, t], slots[:], CUR[:, t:t + 1], None, ALU.is_equal)
                    if t < NT - 1:
                        step(ins)
                ins.then_inc(pick_done, 1)

            def job_in(job, b):
                make_pick(job)
                dve.wait_ge(gather_ps, job + 1)
                for k in range(KD):
                    ins = dve.tensor_scalar(h32[:, k], B[6 + k // 4][:, k % 4 * P:k % 4 * P + P], mod[:, SEG + SC2, k:k + 1], mod[:, SEG + SH2, k:k + 1], ALU.mult, ALU.add)
                ins.then_inc(h32_done, 1)
                dve.wait_ge(jobh_done, job + 1)
                dve.tensor_tensor(jobl[b][:], h32[:], jobh[b][:].bitcast(F32), ALU.subtract).then_inc(jobl_done, 1)

            def job_out(job):
                dve.wait_ge(yh_done, job + 1)
                for half in range(2):
                    ins = dve.tensor_tensor(yl[:, half * 512:half * 512 + 512], B[4 + half][:], yh[:, half * 512:half * 512 + 512].bitcast(F32), ALU.subtract)
                ins.then_inc(yl_done, 1)
                link(dve.tensor_copy(CUR[:, 2:4].unsqueeze(2), JG3[:, :, bass.ds(job, 1)]))
                for t in range(NT):
                    dve.wait_ge(scat_ps, 2 * job + t + 1)
                    for half in range(2):
                        m_ = mixed[:, t, half * 512:half * 512 + 512]
                        ins = dve.scalar_tensor_tensor(m_, B[6 + half][:], CUR[:, 2 + t:3 + t], m_, ALU.mult, ALU.add)
                    ins.then_inc(scat_done, 1)

            def moe_iter(n, F, turn):
                lo(n, turn)
                lo(n + 1, turn)
                turned_low(F - 1, 1)
                lo(n + 2, turn)
                product(n, F, turn, 1)

            IN, OUT = 2, 1
            job_in(0, 0)
            lo(moe0)
            lo(moe0 + 1)
            product(moe0, NJ, 0, 1)
            done = o.n
            with dve.Fori(0, pairs) as m:
                o.n = done + 2 * (IN + OUT) * m
                n0, F0 = moe0 + 2, NJ + 22 * m
                job_in(2 * m + 1, 1)
                with dve.Fori(0, 5) as i:
                    for b in range(2):
                        moe_iter(n0 + 3 * b, F0 + 2 * i + b + 1, NJ * m + i)
                n0 += 30
                moe_iter(n0, F0 + 11, NJ * m)
                job_out(2 * m)
                job_in(2 * m + 2, 0)
                n0 += 3
                with dve.Fori(0, 5) as i:
                    for b in range(2):
                        moe_iter(n0 + 3 * b, F0 + 2 * i + b + 12, NJ * m + i)
                n0 += 30
                moe_iter(n0, F0 + 22, NJ * m)
                job_out(2 * m + 1)
            o.n = done + 2 * (IN + OUT) * pairs
            make_diag(3, 1, G2)
            residual(3, lambda q: mixed[:, q // 2, q % 2 * 512:q % 2 * 512 + 512], scratch)
            dve.wait_ge(fn_landed, 16)
            dve.wait_ge(rms_done, 5)
            link(dve.reciprocal(ss[:, 2:4], ss[:, 2:4]))
            for t in range(NT):
                dve.scalar_tensor_tensor(xn[:, t], x[:, t], ss[:, 2 + t:3 + t], fnw[:], ALU.mult, ALU.mult).then_inc(out_done, 1)


_INS = ["x", "c", "ada_w", "ada_b", "w_in", "conv_w", "conv_b", "dt_bias", "a_log", "d_skip", "ssd_norm_w",
        "gmlp_v_norm_w", "gmlp_ws", "gmlp_bs", "gmlp_out_norm_w", "w_out", "dense_w_gate", "dense_w_up",
        "dense_w_down", "router_w", "router_b", "moe_w_gate", "moe_w_up", "moe_w_down", "final_norm_w"]


def kernel(**inputs):
    import numpy as np
    import concourse.bacc as bacc
    from concourse.bass_utils import run_bass_kernel_spmd

    nc = bacc.Bacc("TRN2", target_bir_lowering=False, num_devices=1)
    arrays, args = {}, []
    for name in _INS:
        a = np.ascontiguousarray(inputs[name])
        arrays[f"in_{name}"] = a
        args.append(nc.dram_tensor(f"in_{name}", a.shape, mybir.dt.from_np(a.dtype), kind="ExternalInput").ap())
    out = nc.dram_tensor("out", (1, SEQ, D), F32, kind="ExternalOutput").ap()
    hybrid_trunk(nc, *args, out)
    r = run_bass_kernel_spmd(nc, [arrays], core_ids=[0])
    return r.results[0]["out"]
```

```python
from contextlib import ExitStack

import concourse.bass as bass
from concourse import mybir

F32 = mybir.dt.float32
F32R = mybir.dt.float32r
BF16 = mybir.dt.bfloat16
I32 = mybir.dt.int32
U32 = mybir.dt.uint32
ALU = mybir.AluOpType
ACT = mybir.ActivationFunctionType
AX_X = mybir.AxisListType.X

P = 128
D = 1024
KD = D // P
SEQ = 256
NT = SEQ // P
LAYERS = 2
HEADS = 16
HD = 64
GROUPS = 4
HPG = HEADS // GROUPS
STATE = 128
CONV_K = 4
PAD = CONV_K - 1
XBC = D + 2 * GROUPS * STATE
CX = XBC // P
GH = 8
FF = 2816
EXPERTS = 8
EPS = 1e-6
D_IN = 2 * D + 2 * GROUPS * STATE + HEADS + 2 * D
COL_Z, COL_XBC = 0, D
COL_DT = COL_XBC + XBC
COL_U = COL_DT + HEADS
COL_V = COL_U + D

UNIT = 2048
PANEL = UNIT // KD
RING = 6
LEAD = 3
NJ = FF // PANEL
KK = UNIT // D
SEG = 6
JOBS = 14
SMALL = 112
CONVB, SSDW, VNW, ONW, COND = 64, 80, 88, 96, 104
SH1, SC1, G1, SH2, SC2, G2 = range(6)
WIN = 4 * (D // PANEL) + (XBC - D) // PANEL
WOUT = 2 * D // (KK * P)


class Order:

    def __init__(self, eng, sem):
        self.eng, self.sem, self.n = eng, sem, 0

    def step(self, ins):
        ins.then_inc(self.sem, 1)
        self.n = self.n + 1

    def link(self, ins):
        self.step(ins)
        self.eng.wait_ge(self.sem, self.n)


def hybrid_trunk(nc, x_in, c_in, ada_w, ada_b, w_in, conv_w, conv_b, dt_bias, a_log, d_skip, ssd_norm_w,
                 gmlp_v_norm_w, gmlp_ws, gmlp_bs, gmlp_out_norm_w, w_out, dense_w_gate, dense_w_up,
                 dense_w_down, router_w, router_b, moe_w_gate, moe_w_up, moe_w_down, final_norm_w, out):
    with ExitStack() as ctx:
        free = [(nc.sbuf_base + 63) // 64 * 64]

        def place(name, shape, dt=F32, at=None):
            size = 1
            for s in shape[1:]:
                size *= s
            size = (size * (2 if dt == BF16 else 4) + 31) // 32 * 32
            if at is None:
                at = free[0]
                free[0] += size
                assert free[0] <= nc.sbuf_usable_end, (name, free[0])
            return nc.alloc_sbuf_tensor_at(name, shape, dt, offset=at), at

        raw, _ = place("raw", [P, RING, UNIT])
        wh, _ = place("wh", [P, 2, UNIT], F32R)
        wl, _ = place("wl", [P, 2, UNIT], F32R)
        adaw, _ = place("adaw", [P, 2, D])
        acc, _ = place("acc", [P, D])
        x, _ = place("x", [P, NT, D])
        xn, at_xn = place("xn", [P, NT, D])
        y, _ = place("y", [P, NT, D], at=at_xn)
        hTh, at_hTh = place("hTh", [P, KD, SEQ], F32R)
        hTl, at_hTl = place("hTl", [P, KD, SEQ], F32R)
        z, at_z = place("z", [P, NT, D])
        v, at_v = place("v", [P, NT, D])
        u, at_u = place("u", [P, KD, SEQ])
        padded, at_pad = place("padded", [P, CX, PAD + SEQ])
        xbc, at_xbc = place("xbc", [P, CX, SEQ])
        bmN, _ = place("bmN", [P, GROUPS, STATE])
        dec_in, at_a = place("dec_in", [P, 2, HPG, P])
        dec, at_e = place("dec", [P, 2, HPG, P])
        wsT, at_wsT = place("wsT", [P, GH, P])
        bsb, at_bs = place("bsb", [P, GH, P])
        xs, _ = place("xs", [P, NT, D], at=at_v)
        wsraw, _ = place("wsraw", [P, GH, P], at=at_a)
        sq, _ = place("sq", [P, KD, SEQ], at=at_a)
        gbc, _ = place("gbc", [P, D], at=at_a)
        diag, _ = place("diag", [P, KD, P], at=at_e)
        state, _ = place("state", [P, GROUPS, HPG * HD], at=at_bs)
        xdec, _ = place("xdec", [P, D], at=at_wsT)
        mgh, _ = place("mgh", [P, KD, SEQ], F32R, at=at_pad)
        mgl, _ = place("mgl", [P, KD, SEQ], F32R, at=at_pad + KD * SEQ * 4)
        msh, _ = place("msh", [P, KD, SEQ], F32R, at=at_xbc)
        msl, _ = place("msl", [P, KD, SEQ], F32R, at=at_xbc + KD * SEQ * 4)
        hT, _ = place("hT", [P, KD, SEQ], at=at_xbc)
        cbm, _ = place("cbm", [P, NT, GROUPS, P], at=at_hTh)
        yoff, _ = place("yoff", [P, HPG * HD], at=at_hTh + 4096)
        rroot, _ = place("rroot", [P, SEQ], at=at_hTh + 5120)
        gtmp, _ = place("gtmp", [P, 2, SEQ], at=at_hTh + 6144)
        gate, _ = place("gate", [P, NT, PANEL], at=at_u)
        actn, _ = place("actn", [P, NT, PANEL], at=at_u + 2048)
        actTh, _ = place("actTh", [P, KK, SEQ], F32R, at=at_u + 4096)
        actTl, _ = place("actTl", [P, KK, SEQ], F32R, at=at_u + 6144)
        mixed, _ = place("mixed", [P, NT, D], at=at_z)
        yh, _ = place("yh", [P, D], F32R, at=at_v)
        yl, _ = place("yl", [P, D], F32R, at=at_v + 4096)
        jobh = [place(f"jobh{b}", [P, KD, P], F32R, at=a)[0] for b, a in enumerate((at_hTh, at_hTl))]
        jobl = [place(f"jobl{b}", [P, KD, P], F32R, at=a + 4096)[0] for b, a in enumerate((at_hTh, at_hTl))]
        wh2, _ = place("wh2", [P, UNIT], F32R, at=at_xbc)
        wl2, _ = place("wl2", [P, UNIT], F32R, at=at_xbc + UNIT * 4)
        h32, _ = place("h32", [P, KD, P], at=at_pad + 8192)
        pick, _ = place("pick", [P, NT, P], at=at_pad)
        put = [place(f"put{b}", [P, NT, P], F32R, at=at_pad + 1024 * (1 + b))[0] for b in range(2)]
        rt, _ = place("rt", [P, 256], at=at_pad + 3072)
        table, _ = place("table", [P, 16], I32, at=at_pad + 4096)
        tix, _ = place("tix", [P, NT, 8], U32, at=at_pad + 4160)
        fnw, _ = place("fnw", [P, D], at=at_wsT)

        ident, _ = place("ident", [P, P])
        upper, _ = place("upper", [P, P])
        strict, _ = place("strict", [P, P])
        ones, _ = place("ones", [P, P])
        slots, _ = place("slots", [P, P])
        small, _ = place("small", [P, P])
        pcol, _ = place("pcol", [P, LAYERS, SMALL])
        abcol, _ = place("abcol", [P, LAYERS, SEG * KD])
        mod, _ = place("mod", [P, LAYERS * SEG, KD])
        cond, _ = place("cond", [P, KD])
        hv, _ = place("hv", [P, 3, HEADS])
        dtw, _ = place("dtw", [P, KD, HEADS])
        rw, _ = place("rw", [P, KD, EXPERTS])
        rb, _ = place("rb", [P, EXPERTS])
        i8, _ = place("i8", [P, EXPERTS])
        epsb, _ = place("epsb", [P, 1])
        ss, _ = place("ss", [P, 8])
        vs, _ = place("vs", [P, NT * GH])
        dtt, _ = place("dtt", [P, 10, NT * HEADS])
        zeros, _ = place("zeros", [P, 512], BF16)

        B = [ctx.enter_context(nc.psum_tensor(f"bank{b}", [P, 512], F32)) for b in range(8)]

        def sem(name):
            return ctx.enter_context(nc.semaphore(name))

        landed = [sem(f"landed{s}") for s in range(RING)]
        ada_landed = [sem(f"ada_landed{s}") for s in range(2)]
        (hi_done, split_done, gemm_done, ada_used, mod_ps, mod_done, consts, small_landed, small_ps, small_used,
         cond_ready, x_landed, rms_done, xn_ready, xT_ps, hT_done, hTh_done, hTl_done, ws_landed, wsT_ps,
         wsT_done, dtw_landed, hv_landed, dt_ps, dt_abs, dt_exp, dA_done, acs_ps, acs_done, acs_exp, proj_evac,
         conv_done, silu_done, bs_landed, v_sq, v_sum, v_ms, v_done, sv_ps, gate_done, gsq_done, gss_ps, grms_done, u_done,
         mgh_done, mgl_done, xs_ps, xs_done, cb_ps, cb_done, skip_done, xdt_done, st_ps, st_done, decin_done,
         seg_ps, seg_done, decay_done, wdec_done, yd_ps, yo_ps, y_done, yz_done, yms_done, yn_done, yT_ps,
         msh_done, msl_done, diag_done, gb_ps, gb_done, x_done, act_order, dve_order, pool_order,
         sg_done, act_done, tp_ps, actTh_done, actT_done, r_landed, lg_ps, rdiff, rexp, mask_done, pos_ps,
         put_cleared, table_done, pick_done, gather_ps, h32_done, jobh_done, jobl_done, yh_done, yl_done, scat_ps, scat_done,
         fn_landed, out_done, stored) = [sem(n) for n in (
            "hi_done split_done gemm_done ada_used mod_ps mod_done consts small_landed small_ps small_used "
            "cond_ready x_landed rms_done xn_ready xT_ps hT_done hTh_done hTl_done ws_landed wsT_ps "
            "wsT_done dtw_landed hv_landed dt_ps dt_abs dt_exp dA_done acs_ps acs_done acs_exp proj_evac "
            "conv_done silu_done bs_landed v_sq v_sum v_ms v_done sv_ps gate_done gsq_done gss_ps grms_done u_done "
            "mgh_done mgl_done xs_ps xs_done cb_ps cb_done skip_done xdt_done st_ps st_done decin_done "
            "seg_ps seg_done decay_done wdec_done yd_ps yo_ps y_done yz_done yms_done yn_done yT_ps "
            "msh_done msl_done diag_done gb_ps gb_done x_done act_order dve_order pool_order "
            "sg_done act_done tp_ps actTh_done actT_done r_landed lg_ps rdiff rexp mask_done pos_ps "
            "put_cleared table_done pick_done gather_ps h32_done jobh_done jobl_done yh_done yl_done scat_ps scat_done "
            "fn_landed out_done stored").split()]

        first_win = [0, WIN + WOUT + 3 * NJ]
        first_wout = [f + WIN for f in first_win]
        dense0 = first_wout[0] + WOUT
        moe0 = first_wout[1] + WOUT

        def splits(n):
            return 3 if dense0 <= n < dense0 + 3 * NJ or n >= moe0 else 2

        def first_of(n):
            return max(f for f in (first_win[0], dense0, first_win[1], moe0) if f <= n)

        def pair_of(n):
            slot = (n - first_of(n)) % splits(n)
            return (wh2[:], wl2[:]) if slot == 2 else (wh[:, slot], wl[:, slot])

        def win_col(i):
            for first, n in ((COL_XBC, XBC // PANEL), (COL_U, D // PANEL), (COL_V, D // PANEL), (COL_Z, D // PANEL)):
                if i < n:
                    return first + i * PANEL
                i -= n

        def panel(w, col):
            return w[:, bass.ds(col, PANEL)].rearrange("(k p) n -> p k n", p=P)

        def rows(w, row):
            return w[bass.ds(row, KK * P), :].rearrange("(k p) n -> p k n", p=P)

        block = ctx.enter_context(nc.Block())

        @block.sync
        def _(sp):
            def load(n, src, k, turn=0):
                if not (isinstance(turn, int) and n + RING * turn < RING):
                    sp.wait_ge(split_done, n + RING * turn - RING + 1)
                sp.dma_start(raw[:, n % RING].rearrange("p (k n) -> p k n", k=k), src).then_inc(landed[n % RING], 16)

            def load_ada(layer, seg, k):
                a = 8 * (SEG * layer + seg) + k
                if not (isinstance(a, int) and a < 2):
                    sp.wait_ge(ada_used, a - 1)
                sp.dma_start(adaw[:, k % 2], ada_w[layer, k * P:(k + 1) * P, bass.ds(seg * D, D)]).then_inc(ada_landed[k % 2], 16)

            for t in range(NT):
                sp.dma_start(x[:, t], x_in[0, t * P:(t + 1) * P, :]).then_inc(x_landed, 16)
            for k in range(KD):
                load_ada(0, SH1, k)
                if k == 1:
                    for layer in range(LAYERS):
                        if layer:
                            sp.wait_ge(small_used, 2)
                        for w, first in ((conv_w[layer].rearrange("j (c p) -> (j c) p", p=P), 0),
                                         (conv_b[layer].rearrange("(c p) -> c p", p=P), CONVB),
                                         (ssd_norm_w[layer].rearrange("(c p) -> c p", p=P), SSDW),
                                         (gmlp_v_norm_w[layer].rearrange("(c p) -> c p", p=P), VNW),
                                         (gmlp_out_norm_w[layer].rearrange("(c p) -> c p", p=P), ONW),
                                         (c_in[0].rearrange("(c p) -> c p", p=P), COND)):
                            sp.dma_start(small[first:first + w.shape[0], :], w).then_inc(small_landed, 16)
                        sp.wait_ge(small_used, 2 * layer + 1)
                        sp.dma_start(small[0:SEG * KD, :], ada_b[layer].rearrange("(c p) -> c p", p=P)).then_inc(small_landed, 16)
            for k in range(KD):
                load_ada(0, SC1, k)

            for layer in range(LAYERS):
                if layer:
                    sp.wait_ge(x_done, 2)
                sp.dma_start(wsraw[:], gmlp_ws[layer].rearrange("h t s -> t h s")).then_inc(ws_landed, 16)
                sp.dma_start(dtw[:], w_in[layer, :, COL_DT:COL_DT + HEADS].rearrange("(k p) n -> p k n", p=P)).then_inc(dtw_landed, 16)
                for n, w in enumerate((dt_bias, a_log, d_skip)):
                    sp.dma_start(hv[:, n], w[layer].partition_broadcast(P)).then_inc(hv_landed, 16)
                sp.dma_start(bsb[:].rearrange("p h t -> p (h t)"), gmlp_bs[layer].rearrange("h t -> (h t)").partition_broadcast(P)).then_inc(bs_landed, 16)
                for i in range(WIN + LEAD):
                    if i < WIN:
                        load(first_win[layer] + i, panel(w_in[layer], win_col(i)), KD)
                    if layer == 0 and 0 <= i - LEAD < 16:
                        for k in (2 * (i - LEAD), 2 * (i - LEAD) + 1):
                            load_ada(0, 2 + k // KD, k % KD)
                for i in range(WOUT):
                    load(first_wout[layer] + i, rows(w_out[layer], D * (1 - i // 4) + KK * P * (i % 4)), KK)
                    if layer == 0 and i >= 4:
                        load_ada(1, 0, i - 4)
                if layer == 0:
                    g, up, dn = dense_w_gate[0], dense_w_up[0], dense_w_down[0]
                    load(dense0, panel(g, 0), KD)
                    load(dense0 + 1, panel(up, 0), KD)
                    with sp.Fori(0, NJ // 2) as i:
                        for b in range(2):
                            n = dense0 + 2 + 3 * b
                            load(n, panel(g, (2 * i + b + 1) * PANEL), KD, i)
                            load(n + 1, panel(up, (2 * i + b + 1) * PANEL), KD, i)
                            load(n + 2, rows(dn, (2 * i + b) * PANEL), KK, i)
                            for k in range(4):
                                load_ada(1, i + b, 4 * (1 - b) + k)
                    load(dense0 + 3 * NJ - 1, rows(dn, (NJ - 1) * PANEL), KK)
                    for k in range(4, KD):
                        load_ada(1, SEG - 1, k)

            sp.dma_start(rw[:], router_w[0].rearrange("(k p) e -> p k e", p=P)).then_inc(r_landed, 16)
            sp.dma_start(rb[:], router_b[0].partition_broadcast(P)).then_inc(r_landed, 16)

            def expert(e):
                return [w[0, bass.ds(e, 1)].rearrange("e k n -> (e k) n") for w in (moe_w_gate, moe_w_up, moe_w_down)]

            def expert_of(job):
                return expert(sp.value_load(table[0:1, bass.ds(job + 1, 1)], min_val=0, max_val=EXPERTS - 1))

            def load_iter(n, turn, gate_up_of, down_of, F):
                load(n, panel(gate_up_of[0], F % NJ * PANEL if isinstance(F, int) else F * PANEL), KD, turn)
                load(n + 1, panel(gate_up_of[1], F % NJ * PANEL if isinstance(F, int) else F * PANEL), KD, turn)
                load(n + 2, rows(down_of[2], (F - 1) * PANEL), KK, turn)

            w0 = expert(0)
            load(moe0, panel(w0[0], 0), KD)
            load(moe0 + 1, panel(w0[1], 0), KD)
            load_iter(moe0 + 2, 0, w0, w0, 1)
            sp.dma_start(fnw[:], final_norm_w.partition_broadcast(P)).then_inc(fn_landed, 16)
            sp.wait_ge(table_done, 1)
            pairs = sp.value_load(table[0:1, 0:1], min_val=4, max_val=6)
            with sp.Fori(0, pairs) as m:
                n0, turn = moe0 + 5, NJ * m
                w0 = expert_of(2 * m)
                load_iter(n0, turn, w0, w0, 2)
                n0 += 3
                with sp.Fori(0, 4) as i:
                    for b in range(2):
                        load_iter(n0 + 3 * b, turn + i, w0, w0, 2 * i + b + 3)
                n0 += 24
                w1 = expert_of(2 * m + 1)
                load_iter(n0, turn, w1, w0, NJ)
                n0 += 3
                with sp.Fori(0, 5) as i:
                    for b in range(2):
                        load_iter(n0 + 3 * b, turn + i, w1, w1, 2 * i + b + 1)
                n0 += 30
                w2 = expert_of(2 * m + 2)
                load_iter(n0, turn, w2, w1, NJ)
                n0 += 3
                load_iter(n0, turn, w2, w2, 1)
            for n in range(moe0 + 68, moe0 + 71):
                sp.wait_ge(landed[n % RING], 16 * (n // RING + 1) + 16 * NJ * (pairs - 1))
            for t in range(NT):
                sp.wait_ge(out_done, t + 1)
                sp.dma_start(out[0, t * P:(t + 1) * P, :], xn[:, t]).then_inc(stored, 16)
            sp.wait_ge(stored, 16 * NT)

        @block.gpsimd
        def _(pool):
            o = Order(pool, pool_order)
            o.step(pool.memset(ones[:], 1.0))
            o.step(pool.memset(zeros[:], 0.0))
            o.step(pool.memset(epsb[:], EPS))
            o.step(pool.memset(ident[:], 0.0))
            o.step(pool.iota(slots[:], pattern=[[1, P]], base=0, channel_multiplier=0, allow_small_or_imprecise_dtypes=True))
            o.link(pool.iota(i8[:], pattern=[[1, EXPERTS]], base=0, channel_multiplier=0, allow_small_or_imprecise_dtypes=True))
            o.step(pool.affine_select(out=ident[:], in_=ident[:], compare_op=ALU.not_equal, fill=1.0, base=0,
                                      pattern=[[-1, P]], channel_multiplier=1))
            o.step(pool.affine_select(out=upper[:], in_=ones[:], compare_op=ALU.is_ge, fill=0.0, base=0,
                                      pattern=[[1, P]], channel_multiplier=-1))
            pool.affine_select(out=strict[:], in_=ones[:], compare_op=ALU.is_gt, fill=0.0, base=0,
                               pattern=[[1, P]], channel_multiplier=-1).then_inc(consts, 1)
            for layer in range(LAYERS):
                if layer:
                    pool.wait_ge(mgl_done, layer)
                    pool.wait_ge(x_done, 2 * layer)
                pool.memset(padded[:, :, 0:PAD], 0.0).then_inc(consts, 1)
                pool.wait_ge(xs_done, layer + 1)
                pool.wait_ge(hv_landed, 48 * (layer + 1))
                for t in range(NT):
                    ins = pool.tensor_tensor(y[:, t].rearrange("p (h d) -> p h d", h=HEADS), xs[:, t].rearrange("p (h d) -> p h d", h=HEADS),
                                             hv[:, 2].unsqueeze(2).broadcast_to([P, HEADS, HD]), ALU.mult)
                    if t == NT - 1:
                        ins.then_inc(skip_done, 1)
                pool.wait_ge(dA_done, layer + 1)
                pool.wait_ge(mgl_done, layer + 1)
                for i in range(2 * GROUPS):
                    c, g = divmod(i, GROUPS)
                    n = 8 * layer + i
                    if i >= 2:
                        pool.wait_ge(seg_ps, n - 1)
                    pool.tensor_tensor(dec_in[:, i % 2], upper[:].unsqueeze(1).broadcast_to([P, HPG, P]),
                                       dtt[:, 2, c * HEADS + HPG * g:c * HEADS + HPG * (g + 1)].unsqueeze(2).broadcast_to([P, HPG, P]),
                                       ALU.mult).then_inc(decin_done, 1)

        @block.scalar
        def _(act):
            o = Order(act, act_order)

            def hi(n, turn=0):
                act.wait_ge(landed[n % RING], 16 * (n // RING + 1) + 16 * turn)
                if isinstance(turn, int) and n - first_of(n) < splits(n):
                    if n >= dense0:
                        act.wait_ge(gemm_done, first_of(n))
                else:
                    act.wait_ge(gemm_done, n + 1 - splits(n) + RING * turn)
                if n == dense0 + 2:
                    act.wait_ge(hTl_done, 8)
                elif n == moe0 + 2:
                    act.wait_ge(lg_ps, 1)
                act.activation(pair_of(n)[0], raw[:, n % RING], ACT.Copy).then_inc(hi_done, 1)

            def root_mean(n):
                for t in range(NT):
                    o.step(act.activation(xn[:, t], x[:, t], ACT.Square, accum_out=ss[:, t:t + 1]))
                act.wait_ge(act_order, o.n)
                act.activation(ss[:, 2:4], ss[:, 0:2], ACT.Sqrt, bias=epsb[:, 0:1], scale=1.0 / D).then_inc(rms_done, 1)

            def turned_hi(n):
                for b in range(4):
                    act.wait_ge(hT_done, 4 * n + b + 1)
                    act.activation(hTh[:, 2 * b:2 * b + 2], hT[:, 2 * b:2 * b + 2], ACT.Copy).then_inc(hTh_done, 1)

            def gb_evac(n):
                act.wait_ge(gb_ps, n + 1)
                for half in range(2):
                    ins = act.activation(gbc[:, half * 512:half * 512 + 512], B[half][:], ACT.Copy)
                ins.then_inc(gb_done, 1)

            act.wait_ge(small_used, 1)
            act.activation(cond[:], pcol[:, 0, COND:COND + KD], ACT.Silu).then_inc(cond_ready, 1)
            act.wait_ge(consts, 1)
            act.wait_ge(x_landed, 16 * NT)
            norm = 0
            for layer in range(LAYERS):
                if layer:
                    act.wait_ge(x_done, 2 * layer)
                root_mean(norm)
                turned_hi(2 * layer)
                norm += 1
                act.wait_ge(dt_abs, layer + 1)
                act.activation(dtt[:, 1], dtt[:, 1], ACT.Exp, scale=-1.0).then_inc(dt_exp, 1)
                act.wait_ge(hv_landed, 48 * (layer + 1))
                act.activation(hv[:, 1], hv[:, 1], ACT.Exp).then_inc(dt_exp, 1)
                g0 = first_win[layer]
                hi(g0)
                hi(g0 + 1)
                for i in range(WIN):
                    act.wait_ge(gemm_done, g0 + i + 1)
                    ps = B[i % 2]
                    if i < 8:
                        if i == 0:
                            act.wait_ge(consts, 2 + layer)
                        ins = act.activation(padded[:, 2 * i:2 * i + 2, PAD:PAD + SEQ], ps[:].rearrange("p (c t) -> p c t", c=2), ACT.Copy)
                    elif i < 12:
                        ins = act.activation(u[:, 2 * (i - 8):2 * (i - 8) + 2], ps[:].rearrange("p (c t) -> p c t", c=2), ACT.Gelu_apprx_tanh)
                    elif i < 16:
                        ins = act.activation(v[:, :, PANEL * (i - 12):PANEL * (i - 11)], ps[:].rearrange("p (t n) -> p t n", t=NT), ACT.Gelu_apprx_tanh)
                    else:
                        ins = act.activation(z[:, :, PANEL * (i - 16):PANEL * (i - 15)], ps[:].rearrange("p (t n) -> p t n", t=NT), ACT.Silu)
                    ins.then_inc(proj_evac, 1)
                    if i + 2 < WIN:
                        hi(g0 + i + 2)
                    if i == 6:
                        act.wait_ge(acs_done, layer + 1)
                        act.activation(dtt[:, 5], dtt[:, 5], ACT.Exp).then_inc(acs_exp, 1)
                    if i >= 16:
                        for c in range(4 * (i - 16), 4 * (i - 15)):
                            act.wait_ge(conv_done, CX * layer + c + 1)
                            act.activation(xbc[:, c], xbc[:, c], ACT.Silu, bias=pcol[:, layer, CONVB + c:CONVB + c + 1]).then_inc(silu_done, 1)
                act.wait_ge(wsT_done, layer + 1)
                act.wait_ge(proj_evac, WIN * layer + 16)
                act.activation(sq[:].rearrange("p a b -> p (a b)"), v[:].rearrange("p a b -> p (a b)"), ACT.Square).then_inc(v_sq, 1)
                act.wait_ge(v_sum, layer + 1)
                act.activation(vs[:], vs[:], ACT.Sqrt, bias=epsb[:, 0:1], scale=1.0 / P).then_inc(v_ms, 1)
                for b in range(4):
                    act.wait_ge(gate_done, 4 * layer + b + 1)
                    act.activation(sq[:, 2 * b:2 * b + 2], u[:, 2 * b:2 * b + 2], ACT.Square).then_inc(gsq_done, 1)
                act.wait_ge(gss_ps, layer + 1)
                act.activation(B[0][:, 0:SEQ], B[0][:, 0:SEQ], ACT.Sqrt, bias=epsb[:, 0:1], scale=1.0 / D).then_inc(grms_done, 1)
                act.wait_ge(u_done, layer + 1)
                for h in range(GH):
                    act.activation(mgh[:, h], u[:, h], ACT.Copy, scale=pcol[:, layer, ONW + h:ONW + h + 1]).then_inc(mgh_done, 1)
                for n in range(4):
                    act.wait_ge(xs_ps, 5 * layer + n + 1)
                    t, half = divmod(n, 2)
                    act.activation(xs[:, t, half * 512:half * 512 + 512], B[4 + n][:], ACT.Copy)
                act.wait_ge(xs_ps, 5 * layer + 5)
                act.activation(bmN[:].rearrange("p g n -> p (g n)"), B[1][:], ACT.Copy).then_inc(xs_done, 1)
                act.wait_ge(st_ps, layer + 1)
                for b in range(2):
                    ins = act.activation(state[:, 2 * b:2 * b + 2].rearrange("p g n -> p (g n)"), B[2 + b][:], ACT.Copy)
                ins.then_inc(st_done, 1)
                for i in range(2 * GROUPS):
                    act.wait_ge(seg_done, 8 * layer + i + 1)
                    act.activation(dec[:, i % 2], dec[:, i % 2], ACT.Exp).then_inc(decay_done, 1)
                act.wait_ge(yz_done, layer + 1)
                for t in range(NT):
                    o.step(act.activation(z[:, t], y[:, t], ACT.Square, accum_out=ss[:, 4 + t:5 + t]))
                act.wait_ge(act_order, o.n)
                act.activation(ss[:, 6:8], ss[:, 4:6], ACT.Sqrt, bias=epsb[:, 0:1], scale=1.0 / D).then_inc(yms_done, 1)
                for k in range(KD):
                    act.wait_ge(yT_ps, 4 * layer + k // 2 + 1)
                    act.activation(msh[:, k], B[4 + k // 2][:, k % 2 * SEQ:k % 2 * SEQ + SEQ], ACT.Copy,
                                   scale=pcol[:, layer, SSDW + k:SSDW + k + 1]).then_inc(msh_done, 1)
                gb_evac(2 * layer)
                for i in range(WOUT):
                    hi(first_wout[layer] + i)
                act.wait_ge(x_done, 2 * layer + 1)
                root_mean(norm)
                norm += 1
                if layer == 0:
                    turned_hi(1)

                def silu_gate(n, F, turn, nt):
                    act.wait_ge(gemm_done, n + 1 + RING * turn)
                    act.wait_ge(act_done, F)
                    act.activation(gate[:, 0:nt], B[0][:].rearrange("p (t n) -> p t n", t=NT)[:, 0:nt], ACT.Silu).then_inc(sg_done, 1)

                def turned_product(F, nt):
                    act.wait_ge(tp_ps, F + 1)
                    act.activation(actTh[:, :, 0:nt * P], B[2][:].rearrange("p (k t) -> p k t", k=KK)[:, :, 0:nt * P], ACT.Copy).then_inc(actTh_done, 1)

                if layer == 0:
                    hi(dense0)
                    hi(dense0 + 1)
                    silu_gate(dense0, 0, 0, NT)
                    with act.Fori(0, NJ // 2) as i:
                        for b in range(2):
                            n, F = dense0 + 2 + 3 * b, 2 * i + b + 1
                            hi(n, i)
                            hi(n + 1, i)
                            hi(n + 2, i)
                            silu_gate(n, F, i, NT)
                            turned_product(F - 1, NT)
                    hi(dense0 + 3 * NJ - 1)
                    turned_product(NJ - 1, NT)
                    gb_evac(1)
            hi(moe0)
            hi(moe0 + 1)
            act.wait_ge(rdiff, 1)
            act.activation(rt[:, 0:2], rt[:, 0:2], ACT.Exp).then_inc(rexp, 1)
            act.wait_ge(table_done, 1)
            pairs = act.value_load(table[0:1, 0:1], min_val=4, max_val=6)

            def job_in(job, b):
                act.wait_ge(gather_ps, job + 1)
                if not isinstance(job, int):
                    act.wait_ge(jobl_done, job)
                act.activation(put[b][:].rearrange("p t n -> p (t n)"), B[3][:, 0:SEQ], ACT.Copy)
                for k in range(KD):
                    ins = act.activation(h32[:, k], B[6 + k // 4][:, k % 4 * P:k % 4 * P + P], ACT.Identity, scale=mod[:, SEG + SC2, k:k + 1], bias=mod[:, SEG + SH2, k:k + 1])
                ins.then_inc(h32_done, 1)
                act.wait_ge(h32_done, job + 1)
                act.activation(jobh[b][:], h32[:], ACT.Copy).then_inc(jobh_done, 1)

            def job_out(job, n, turn):
                act.wait_ge(gemm_done, n + RING * turn)
                act.wait_ge(scat_done, 2 * job + 3)
                for half in range(2):
                    ins = act.activation(yh[:, half * 512:half * 512 + 512], B[4 + half][:], ACT.Copy)
                ins.then_inc(yh_done, 1)

            def moe_iter(n, F, turn, ended=None):
                hi(n, turn)
                hi(n + 1, turn)
                if ended is not None:
                    job_out(ended, n, turn)
                hi(n + 2, turn)
                silu_gate(n, F, turn, 1)
                turned_product(F - 1, 1)

            job_in(0, 0)
            silu_gate(moe0, NJ, 0, 1)
            with act.Fori(0, pairs) as m:
                for b in range(2):
                    job, n0, F0, turn = 2 * m + b, moe0 + 2 + 33 * b, NJ + 22 * m + NJ * b, NJ * m
                    moe_iter(n0, F0 + 1, turn, job - 1)
                    moe_iter(n0 + 3, F0 + 2, turn)
                    job_in(job + 1, 1 - b)
                    n0 += 6
                    with act.Fori(0, 4) as i:
                        for c in range(2):
                            moe_iter(n0 + 3 * c, F0 + 2 * i + c + 3, turn + i)
                    moe_iter(n0 + 24, F0 + NJ, turn)
            job_out(2 * pairs - 1, moe0 + 68, NJ * (pairs - 1))
            gb_evac(3)
            act.wait_ge(x_done, 4)
            root_mean(4)

        @block.tensor
        def _(pe):
            def three(ps, k, last, ah, al, bh, bl):
                pe.matmul(ps, ah, bh, start=(k == 0), stop=False, skip_group_check=True)
                pe.matmul(ps, ah, bl, start=False, stop=False, skip_group_check=True)
                return pe.matmul(ps, al, bh, start=False, stop=last, skip_group_check=True)

            def unit(n, turn):
                pe.wait_ge(split_done, n + 1 + RING * turn)

            def whl(n, k):
                return (w.rearrange("p (k n) -> p k n", k=k) for w in pair_of(n))

            def natural(n, turn, ps_of, xh, xl, nt):
                unit(n, turn)
                h, l = whl(n, KD)
                for t in range(nt):
                    for k in range(KD):
                        ins = three(ps_of(t), k, k == KD - 1, xh[:, k, t * P:t * P + P], xl[:, k, t * P:t * P + P], h[:, k], l[:, k])
                ins.then_inc(gemm_done, 1)

            def turned(n, ps):
                unit(n, 0)
                h, l = whl(n, KD)
                for c in range(2):
                    for k in range(KD):
                        ins = three(ps[:, c * SEQ:c * SEQ + SEQ], k, k == KD - 1, h[:, k, c * P:c * P + P], l[:, k, c * P:c * P + P], hTh[:, k], hTl[:, k])
                ins.then_inc(gemm_done, 1)

            def deep(n, turn, xh, xl, k0, nt, start, last):
                unit(n, turn)
                h, l = whl(n, KK)
                for kk in range(KK):
                    for t in range(nt):
                        for half in range(2):
                            ps = B[4 + 2 * t + half][:]
                            ins = three(ps, 0 if start and kk == 0 else 1, last and kk == KK - 1, xh[:, k0 + kk, t * P:t * P + P],
                                        xl[:, k0 + kk, t * P:t * P + P], h[:, kk, half * 512:half * 512 + 512], l[:, kk, half * 512:half * 512 + 512])
                ins.then_inc(gemm_done, 1)

            def clear_acc(nt):
                for b in range(2 * nt):
                    pe.matmul(B[4 + b][:], zeros[0:1, 0:P], zeros[0:1, :], start=True, stop=False, skip_group_check=True)

            def mod_columns(s):
                pe.wait_ge(ada_used, 8 * (s + 1))
                if not (isinstance(s, int) and s == 0):
                    pe.wait_ge(mod_done, s)
                for k in range(KD):
                    ins = pe.matmul(B[3][:, k:k + 1], acc[:, k * P:k * P + P], ones[:, 0:1], start=True, stop=True, skip_group_check=True)
                ins.then_inc(mod_ps, 1)

            def turn_x(n):
                pe.wait_ge(xn_ready, n + 1)
                for b in range(4):
                    for c in range(4):
                        k, t = 2 * b + c // 2, c % 2
                        ins = pe.transpose(B[4 + b][:, c * P:c * P + P], xn[:, t, k * P:k * P + P], ident[:])
                    ins.then_inc(xT_ps, 1)

            def broadcast_gate(n):
                pe.wait_ge(diag_done, n + 1)
                for half in range(2):
                    ins = pe.matmul(B[half][:], ones[:], diag[:, 4 * half:4 * half + 4].rearrange("p k n -> p (k n)"), start=True, stop=True, skip_group_check=True)
                ins.then_inc(gb_ps, 1)

            pe.wait_ge(consts, 1)
            for i in range(2 * LAYERS):
                layer, b = divmod(i, 2)
                pe.wait_ge(small_landed, 16 * (7 * layer + (6, 7)[b]))
                rows_n = (SMALL, SEG * KD)[b]
                if i:
                    pe.wait_ge(small_used, i)
                pe.transpose(B[2][:, 0:rows_n], small[0:rows_n, :], ident[0:rows_n, 0:rows_n]).then_inc(small_ps, 1)
            mod_columns(SH1)
            mod_columns(SC1)

            for layer in range(LAYERS):
                pe.wait_ge(ws_landed, 16 * (layer + 1))
                if layer:
                    pe.wait_ge(x_done, 2 * layer)
                for h in range(GH):
                    ins = pe.transpose(B[h // 4][:, h % 4 * P:h % 4 * P + P], wsraw[:, h], ident[:])
                    if h % 4 == 3:
                        ins.then_inc(wsT_ps, 1)
                turn_x(2 * layer)
                pe.wait_ge(hT_done, 8 * layer + 4)
                pe.wait_ge(dtw_landed, 16 * (layer + 1))
                for t in range(NT):
                    for k in range(KD):
                        ins = pe.matmul(B[2][:, t * HEADS:(t + 1) * HEADS], hT[:, k, t * P:t * P + P], dtw[:, k], start=(k == 0), stop=(k == KD - 1), skip_group_check=True)
                ins.then_inc(dt_ps, 1)
                pe.wait_ge(hTl_done, 8 * layer + 4)
                pe.wait_ge(wsT_done, layer + 1)
                g0 = first_win[layer]
                for i in range(WIN):
                    if i >= 2:
                        pe.wait_ge(proj_evac, WIN * layer + i - 1)
                    if i < 12:
                        turned(g0 + i, B[i % 2])
                    else:
                        natural(g0 + i, 0, lambda t: B[i % 2][:, t * PANEL:(t + 1) * PANEL], hTh, hTl, NT)
                    if i == 3:
                        pe.wait_ge(dA_done, layer + 1)
                        for c in range(NT):
                            pe.matmul(B[2][:, c * HEADS:(c + 1) * HEADS], upper[:], dtt[:, 2, c * HEADS:(c + 1) * HEADS], start=True, stop=True, skip_group_check=True)
                        pe.matmul(B[2][:, 2 * HEADS:3 * HEADS], ones[:], dtt[:, 2, 0:HEADS], start=True, stop=True, skip_group_check=True).then_inc(acs_ps, 1)
                    if layer == 0 and i in (4, 8, 12, 16):
                        mod_columns(G1 + (i - 4) // 4)
                pe.wait_ge(v_done, layer + 1)
                for h in range(GH):
                    for c in range(NT):
                        ins = pe.matmul(B[4 + h // 2][:, (h % 2 * 2 + c) * P:(h % 2 * 2 + c + 1) * P], v[:, c, h * P:h * P + P], wsT[:, h], start=True, stop=True, skip_group_check=True)
                    if h % 2:
                        ins.then_inc(sv_ps, 1)
                pe.wait_ge(silu_done, CX * (layer + 1))
                pe.wait_ge(acs_done, layer + 1)
                pe.wait_ge(mod_done, SEG * (layer + 1))
                for c in range(NT):
                    for g in range(GROUPS):
                        ins = pe.matmul(B[2 + c][:, g * P:g * P + P], xbc[:, KD + g, c * P:c * P + P], xbc[:, KD + GROUPS + g, c * P:c * P + P], start=True, stop=True, skip_group_check=True)
                    ins.then_inc(cb_ps, 1)
                for n in range(4):
                    pe.wait_ge(gate_done, 4 * layer + n + 1)
                    t, half = divmod(n, 2)
                    for c in range(4):
                        ins = pe.transpose(B[4 + n][:, c * P:c * P + P], xbc[:, 4 * half + c, t * P:t * P + P], ident[:])
                    ins.then_inc(xs_ps, 1)
                pe.wait_ge(proj_evac, WIN * (layer + 1))
                for g in range(GROUPS):
                    ins = pe.transpose(B[1][:, g * P:g * P + P], xbc[:, KD + g, 0:P], ident[:])
                ins.then_inc(xs_ps, 1)
                for h in range(GH):
                    pe.wait_ge(gsq_done, 4 * layer + h // 2 + 1)
                    ins = pe.matmul(B[0][:, 0:SEQ], ones[:], sq[:, h], start=(h == 0), stop=(h == GH - 1), skip_group_check=True)
                ins.then_inc(gss_ps, 1)
                pe.wait_ge(xs_done, layer + 1)
                pe.wait_ge(xdt_done, layer + 1)
                pe.wait_ge(cb_done, 2 * layer + 2)
                for g in range(GROUPS):
                    ins = pe.matmul(B[2 + g // 2][:, g % 2 * 256:g % 2 * 256 + 256], bmN[:, g], xdec[:, g * 256:g * 256 + 256], start=True, stop=True, skip_group_check=True)
                ins.then_inc(st_ps, 1)
                pe.wait_ge(u_done, layer + 1)

                def segments(i):
                    if i >= 2:
                        pe.wait_ge(seg_done, 8 * layer + i - 1)
                    pe.wait_ge(decin_done, 8 * layer + i + 1)
                    pe.matmul(B[i % 2][:], ones[:], dec_in[:, i % 2].rearrange("p e q -> p (e q)"), start=True, stop=True, skip_group_check=True).then_inc(seg_ps, 1)

                def within(i):
                    c, g = divmod(i, GROUPS)
                    pe.wait_ge(wdec_done, 8 * layer + i + 1)
                    for e in range(HPG):
                        h = g * HPG + e
                        ins = pe.matmul(B[4 + i // 2][:, (i % 2 * HPG + e) * HD:(i % 2 * HPG + e + 1) * HD], dec[:, i % 2, e],
                                        xs[:, c, h * HD:(h + 1) * HD], start=True, stop=True, skip_group_check=True)
                    ins.then_inc(yd_ps, 1)

                segments(0)
                for i in range(2 * GROUPS):
                    if i + 1 < 2 * GROUPS:
                        segments(i + 1)
                    if i == 2:
                        pe.wait_ge(st_done, layer + 1)
                        for g in range(GROUPS):
                            ins = pe.matmul(B[2 + g // 2][:, g % 2 * 256:g % 2 * 256 + 256], xbc[:, KD + GROUPS + g, P:2 * P], state[:, g], start=True, stop=True, skip_group_check=True)
                        ins.then_inc(yo_ps, 1)
                    within(i)
                pe.wait_ge(yn_done, layer + 1)
                for b in range(4):
                    for c in range(4):
                        k, t = 2 * b + c // 2, c % 2
                        ins = pe.transpose(B[4 + b][:, c * P:c * P + P], y[:, t, k * P:k * P + P], ident[:])
                    ins.then_inc(yT_ps, 1)
                broadcast_gate(2 * layer)
                pe.wait_ge(mgl_done, layer + 1)
                pe.wait_ge(msl_done, layer + 1)
                for i in range(WOUT):
                    sh, sl = (mgh, mgl) if i < 4 else (msh, msl)
                    deep(first_wout[layer] + i, 0, sh, sl, KK * (i % 4), NT, i == 0, i == WOUT - 1)
                turn_x(2 * layer + 1)

                def turn_product(F, nt):
                    pe.wait_ge(act_done, F + 1)
                    if not (isinstance(F, int) and F == 0):
                        pe.wait_ge(actT_done, F)
                    for kk in range(KK):
                        for t in range(nt):
                            ins = pe.transpose(B[2][:, kk * SEQ + t * P:kk * SEQ + t * P + P], actn[:, t, kk * P:kk * P + P], ident[:])
                    ins.then_inc(tp_ps, 1)

                def gate_up(n, F, turn, xh, xl, nt, between, incoming=None):
                    pe.wait_ge(sg_done, F)
                    natural(n, turn, lambda t: B[0][:, t * PANEL:(t + 1) * PANEL], xh, xl, nt)
                    if between is not None:
                        turn_product(between, nt)
                    if incoming is not None:
                        gather(incoming)
                    pe.wait_ge(act_done, F)
                    natural(n + 1, turn, lambda t: B[1][:, t * PANEL:(t + 1) * PANEL], xh, xl, nt)

                if layer == 0:
                    pe.wait_ge(hTl_done, 8)
                    clear_acc(NT)
                    gate_up(dense0, 0, 0, hTh, hTl, NT, None)
                    with pe.Fori(0, NJ // 2) as i:
                        for b in range(2):
                            n, F = dense0 + 2 + 3 * b, 2 * i + b + 1
                            gate_up(n, F, i, hTh, hTl, NT, F - 1)
                            pe.wait_ge(actT_done, F)
                            deep(n + 2, i, actTh, actTl, 0, NT, False, False)
                            if b == 0:
                                mod_columns(SEG + i)
                    turn_product(NJ - 1, NT)
                    pe.wait_ge(actT_done, NJ)
                    deep(dense0 + 3 * NJ - 1, 0, actTh, actTl, 0, NT, False, True)
                    broadcast_gate(1)
                    mod_columns(2 * SEG - 1)

            pe.wait_ge(hT_done, 16)
            pe.wait_ge(r_landed, 32)
            for t in range(NT):
                for k in range(KD):
                    ins = pe.matmul(B[2][:, t * EXPERTS:(t + 1) * EXPERTS], hT[:, k, t * P:t * P + P], rw[:, k], start=(k == 0), stop=(k == KD - 1), skip_group_check=True)
            ins.then_inc(lg_ps, 1)
            pe.wait_ge(mask_done, 1)
            mk = rt[:, 32:48]
            pe.matmul(B[2][:, 16:24], strict[:], mk[:, 0:8], start=True, stop=True, skip_group_check=True)
            pe.matmul(B[2][:, 24:32], strict[:], mk[:, 8:16], start=True, stop=False, skip_group_check=True)
            pe.matmul(B[2][:, 24:32], ones[:], mk[:, 0:8], start=False, stop=True, skip_group_check=True)
            pe.matmul(B[2][:, 32:40], ones[:], mk[:, 0:8], start=True, stop=False, skip_group_check=True)
            pe.matmul(B[2][:, 32:40], ones[:], mk[:, 8:16], start=False, stop=True, skip_group_check=True).then_inc(pos_ps, 1)
            pe.wait_ge(table_done, 1)
            pairs = pe.value_load(table[0:1, 0:1], min_val=4, max_val=6)

            def gather(job):
                pe.wait_ge(pick_done, job + 1)
                if not isinstance(job, int):
                    pe.wait_ge(scat_done, 2 * job + 1)
                    pe.wait_ge(jobh_done, job)
                for k in range(KD):
                    for t in range(NT):
                        pe.matmul(B[6 + k // 4][:, k % 4 * P:k % 4 * P + P], xn[:, t, k * P:k * P + P], pick[:, t], start=(t == 0), stop=(t == NT - 1), skip_group_check=True)
                for t in range(NT):
                    ins = pe.transpose(B[3][:, t * P:t * P + P], pick[:, t], ident[:])
                ins.then_inc(gather_ps, 1)

            def scatter(job, b, t):
                if t == 0:
                    pe.wait_ge(yl_done, job + 2)
                    pe.wait_ge(h32_done, job + 2)
                pe.wait_ge(scat_done, 2 * job + t + 3)
                for half in range(2):
                    for n, w in enumerate((yh, yl)):
                        ins = pe.matmul(B[6 + half][:], put[b][:, t], w[:, half * 512:half * 512 + 512], start=(n == 0), stop=(n == 1), skip_group_check=True)
                ins.then_inc(scat_ps, 1)

            def moe_iter(n, F, turn, xb, start=False, last=False, incoming=None, ended=None):
                gate_up(n, F, turn, jobh[xb], jobl[xb], 1, F - 1, incoming)
                if ended is not None:
                    scatter(ended, 1 - xb, 0)
                pe.wait_ge(actT_done, F)
                deep(n + 2, turn, actTh, actTl, 0, 1, start, last)
                if ended is not None:
                    scatter(ended, 1 - xb, 1)

            gather(0)
            clear_acc(1)
            pe.wait_ge(jobl_done, 1)
            gate_up(moe0, NJ, 0, jobh[0], jobl[0], 1, None)
            with pe.Fori(0, pairs) as m:
                for b in range(2):
                    job, n0, F0, turn = 2 * m + b, moe0 + 2 + 33 * b, NJ + 22 * m + NJ * b, NJ * m
                    moe_iter(n0, F0 + 1, turn, b, start=True, ended=job - 1)
                    moe_iter(n0 + 3, F0 + 2, turn, b, incoming=job + 1)
                    n0 += 6
                    with pe.Fori(0, 4) as i:
                        for c in range(2):
                            moe_iter(n0 + 3 * c, F0 + 2 * i + c + 3, turn + i, b)
                    pe.wait_ge(jobl_done, job + 2)
                    moe_iter(n0 + 24, F0 + NJ, turn, 1 - b, last=True)
            for t in range(NT):
                scatter(2 * pairs - 1, 1, t)
            broadcast_gate(3)

        @block.vector
        def _(dve):
            o = Order(dve, dve_order)
            link, step = o.link, o.step

            def lo(n, turn=0):
                dve.wait_ge(hi_done, n + 1 + RING * turn)
                h, l = pair_of(n)
                dve.tensor_tensor(l, raw[:, n % RING], h.bitcast(F32), ALU.subtract).then_inc(split_done, 1)

            def ada(layer, seg, k):
                a = 8 * (SEG * layer + seg) + k
                half = 4 * (SEG * layer + seg) + k // 2
                dve.wait_ge(ada_landed[k % 2], 16 * half + 16)
                if k == 0:
                    if not (isinstance(a, int) and a == 0):
                        dve.wait_ge(mod_ps, SEG * layer + seg)
                    dve.tensor_scalar(acc[:], adaw[:, 0], cond[:, 0:1], None, ALU.mult).then_inc(ada_used, 1)
                else:
                    dve.wait_ge(ada_used, a)
                    dve.scalar_tensor_tensor(acc[:], adaw[:, k % 2], cond[:, k:k + 1], acc[:], ALU.mult, ALU.add).then_inc(ada_used, 1)

            def mod_evac(layer, seg):
                s = SEG * layer + seg
                dve.wait_ge(mod_ps, s + 1)
                dve.tensor_tensor(mod[:, bass.ds(s, 1)].rearrange("p a k -> p (a k)"), B[3][:, 0:KD], abcol[:, layer, bass.ds(seg * KD, KD)], ALU.add).then_inc(mod_done, 1)

            def normalise(n):
                dve.wait_ge(rms_done, n + 1)
                link(dve.reciprocal(ss[:, 2:4], ss[:, 2:4]))
                for t in range(NT):
                    ins = dve.tensor_scalar(xn[:, t], x[:, t], ss[:, 2 + t:3 + t], None, ALU.mult)
                    if t < NT - 1:
                        step(ins)
                ins.then_inc(xn_ready, 1)

            def modulate(n, layer, shift, scale, low=True):
                dve.wait_ge(mod_done, SEG * layer + scale + 1)
                link(dve.tensor_scalar(mod[:, SEG * layer + scale], mod[:, SEG * layer + scale], 1.0, None, ALU.add))
                for b in range(4):
                    dve.wait_ge(xT_ps, 4 * n + b + 1)
                    for kk in range(2):
                        k = 2 * b + kk
                        ins = dve.tensor_scalar(hT[:, k], B[4 + b][:, kk * SEQ:kk * SEQ + SEQ], mod[:, SEG * layer + scale, k:k + 1],
                                                mod[:, SEG * layer + shift, k:k + 1], ALU.mult, ALU.add)
                    ins.then_inc(hT_done, 1)
                if low:
                    for b in range(4):
                        dve.wait_ge(hTh_done, 4 * n + b + 1)
                        dve.tensor_tensor(hTl[:, 2 * b:2 * b + 2], hT[:, 2 * b:2 * b + 2], hTh[:, 2 * b:2 * b + 2].bitcast(F32), ALU.subtract).then_inc(hTl_done, 1)

            def make_diag(n, layer, seg):
                dve.wait_ge(mod_done, SEG * layer + seg + 1)
                for k in range(KD):
                    ins = dve.tensor_scalar(diag[:, k], ident[:], mod[:, SEG * layer + seg, k:k + 1], None, ALU.mult)
                ins.then_inc(diag_done, 1)

            def residual(n, source, tmp):
                dve.wait_ge(gb_done, n + 1)
                for q in range(4):
                    t, half = divmod(q, 2)
                    link(dve.scalar_tensor_tensor(tmp(q), gbc[:, half * 512:half * 512 + 512], 1.0, source(q), ALU.add, ALU.mult))
                    ins = dve.tensor_tensor(x[:, t, half * 512:half * 512 + 512], x[:, t, half * 512:half * 512 + 512], tmp(q), ALU.add)
                    if q < 3:
                        step(ins)
                ins.then_inc(x_done, 1)

            def scratch(q):
                return diag[:, 4 * (q % 2):4 * (q % 2) + 4].rearrange("p k n -> p (k n)")

            dve.wait_ge(consts, 1)
            for i in range(2 * LAYERS):
                dve.wait_ge(small_ps, i + 1)
                layer, b = divmod(i, 2)
                if b == 0:
                    dve.tensor_copy(pcol[:, layer], B[2][:, 0:SMALL]).then_inc(small_used, 1)
                else:
                    dve.tensor_copy(abcol[:, layer], B[2][:, 0:SEG * KD]).then_inc(small_used, 1)
            dve.wait_ge(cond_ready, 1)
            for seg in (SH1, SC1):
                for k in range(KD):
                    ada(0, seg, k)
                if seg == SH1:
                    normalise(0)
                mod_evac(0, seg)

            norm = 0
            for layer in range(LAYERS):
                if layer:
                    normalise(2 * layer)
                for b in range(2):
                    dve.wait_ge(wsT_ps, 2 * layer + b + 1)
                    ins = dve.tensor_tensor(wsT[:, 4 * b:4 * b + 4], B[b][:].rearrange("p (h t) -> p h t", h=4), upper[:].unsqueeze(1).broadcast_to([P, 4, P]), ALU.mult)
                ins.then_inc(wsT_done, 1)
                modulate(2 * layer, layer, SH1, SC1)
                dve.wait_ge(dt_ps, layer + 1)
                dve.wait_ge(hv_landed, 48 * (layer + 1))
                T = [dtt[:, n] for n in range(10)]
                link(dve.tensor_tensor(T[0].rearrange("p (c h) -> p c h", c=NT), B[2][:, 0:NT * HEADS].rearrange("p (c h) -> p c h", c=NT),
                                       hv[:, 0].unsqueeze(1).broadcast_to([P, NT, HEADS]), ALU.add))
                link(dve.tensor_scalar(T[1], T[0], -1.0, None, ALU.mult))
                dve.tensor_tensor(T[1], T[0], T[1], ALU.max).then_inc(dt_abs, 1)
                g0 = first_win[layer]
                dve.wait_ge(dt_exp, 2 * layer + 2)
                link(dve.tensor_scalar(T[3], T[1], 2.0, None, ALU.add))
                link(dve.reciprocal(T[3], T[3]))
                link(dve.tensor_tensor(T[3], T[3], T[1], ALU.mult))
                link(dve.tensor_tensor(T[4], T[3], T[3], ALU.mult))
                link(dve.tensor_scalar(T[5], T[4], 1.0 / 15, 1.0 / 13, ALU.mult, ALU.add))
                for c in (11, 9, 7, 5, 3, 1):
                    link(dve.tensor_tensor(T[5], T[5], T[4], ALU.mult))
                    link(dve.tensor_scalar(T[5], T[5], 1.0 / c, None, ALU.add))
                link(dve.scalar_tensor_tensor(T[3], T[3], 2.0, T[5], ALU.mult, ALU.mult))
                link(dve.tensor_scalar(T[0], T[0], 0.0, None, ALU.max))
                link(dve.tensor_tensor(T[0], T[0], T[3], ALU.add))
                dve.scalar_tensor_tensor(T[2].rearrange("p (c h) -> p c h", c=NT), T[0].rearrange("p (c h) -> p c h", c=NT), -1.0,
                                         hv[:, 1].unsqueeze(1).broadcast_to([P, NT, HEADS]), ALU.mult, ALU.mult).then_inc(dA_done, 1)
                lo(g0)
                lo(g0 + 1)
                conv = 0
                for i in range(WIN):
                    if i + 2 < WIN:
                        lo(g0 + i + 2)
                    if layer == 0 and i < 16:
                        ada(0, 2 + 2 * i // KD, 2 * i % KD)
                        ada(0, 2 + 2 * i // KD, 2 * i % KD + 1)
                    if layer == 0 and i in (5, 9, 13, 17):
                        mod_evac(0, G1 + (i - 5) // 4)
                    if i == 5:
                        dve.wait_ge(acs_ps, layer + 1)
                        link(dve.tensor_copy(T[4], B[2][:, 0:NT * HEADS]))
                        step(dve.tensor_tensor(T[5][:, 0:HEADS], B[2][:, 2 * HEADS:3 * HEADS], T[4][:, 0:HEADS], ALU.subtract))
                        dve.tensor_copy(T[5][:, HEADS:2 * HEADS], T[4][:, HEADS:2 * HEADS]).then_inc(acs_done, 1)
                    if 3 <= i < 3 + CX:
                        c = i - 3
                        dve.wait_ge(proj_evac, WIN * layer + c // 2 + 1)
                        wc = pcol[:, layer]
                        link(dve.tensor_scalar(xbc[:, c], padded[:, c, 0:SEQ], wc[:, c:c + 1], None, ALU.mult))
                        for j in range(1, CONV_K):
                            ins = dve.scalar_tensor_tensor(xbc[:, c], padded[:, c, j:j + SEQ], wc[:, j * CX + c:j * CX + c + 1], xbc[:, c], ALU.mult, ALU.add)
                            if j < CONV_K - 1:
                                link(ins)
                        ins.then_inc(conv_done, 1)
                dve.wait_ge(v_sq, layer + 1)
                dve.tensor_reduce(vs[:], sq[:].rearrange("p a (h d) -> p (a h) d", d=P), AX_X, ALU.add).then_inc(v_sum, 1)
                dve.wait_ge(v_ms, layer + 1)
                link(dve.reciprocal(vs[:], vs[:]))
                vh = v[:].rearrange("p t (h d) -> p (t h) d", d=P)
                dve.tensor_tensor(vh, vh, vs[:].unsqueeze(2).broadcast_to([P, NT * GH, P]), ALU.mult).then_inc(v_done, 1)
                for c in range(NT):
                    dve.wait_ge(cb_ps, 2 * layer + c + 1)
                    dve.tensor_tensor(cbm[:, c], B[2 + c][:].rearrange("p (g q) -> p g q", g=GROUPS), upper[:].unsqueeze(1).broadcast_to([P, GROUPS, P]), ALU.mult).then_inc(cb_done, 1)
                dve.wait_ge(bs_landed, 16 * (layer + 1))
                for h in range(GH):
                    if h % 2 == 0:
                        dve.wait_ge(sv_ps, 4 * layer + h // 2 + 1)
                    tmp = gtmp[:, h % 2].rearrange("p (c t) -> p c t", c=NT)
                    link(dve.scalar_tensor_tensor(tmp, B[4 + h // 2][:, h % 2 * SEQ:h % 2 * SEQ + SEQ].rearrange("p (c t) -> p c t", c=NT),
                                                  pcol[:, layer, VNW + h:VNW + h + 1], bsb[:, h].unsqueeze(1).broadcast_to([P, NT, P]), ALU.mult, ALU.add))
                    ins = dve.tensor_tensor(u[:, h].rearrange("p (c t) -> p c t", c=NT), u[:, h].rearrange("p (c t) -> p c t", c=NT), tmp, ALU.mult)
                    if h % 2:
                        ins.then_inc(gate_done, 1)
                    else:
                        step(ins)
                dve.wait_ge(grms_done, layer + 1)
                link(dve.reciprocal(rroot[:], B[0][:, 0:SEQ]))
                dve.tensor_tensor(u[:], u[:], rroot[:].unsqueeze(1).broadcast_to([P, KD, SEQ]), ALU.mult).then_inc(u_done, 1)
                for h in range(GH):
                    dve.wait_ge(mgh_done, GH * layer + h + 1)
                    if h == 0:
                        dve.wait_ge(u_done, layer + 1)
                    ins = dve.scalar_tensor_tensor(mgl[:, h], u[:, h], pcol[:, layer, ONW + h:ONW + h + 1], mgh[:, h].bitcast(F32), ALU.mult, ALU.subtract)
                ins.then_inc(mgl_done, 1)
                dve.wait_ge(xs_done, layer + 1)
                dve.wait_ge(skip_done, layer + 1)
                dve.wait_ge(acs_exp, layer + 1)
                for t in range(NT):
                    xt = xs[:, t].rearrange("p (h d) -> p h d", h=HEADS)
                    link(dve.tensor_tensor(xt, xt, T[0][:, t * HEADS:(t + 1) * HEADS].unsqueeze(2).broadcast_to([P, HEADS, HD]), ALU.mult))
                dve.tensor_tensor(xdec[:].rearrange("p (h d) -> p h d", h=HEADS), xs[:, 0].rearrange("p (h d) -> p h d", h=HEADS),
                                  T[5][:, 0:HEADS].unsqueeze(2).broadcast_to([P, HEADS, HD]), ALU.mult).then_inc(xdt_done, 1)

                def gather_y(i):
                    c, g = divmod(i, GROUPS)
                    yt = y[:, c, g * 256:g * 256 + 256]
                    dve.wait_ge(yd_ps, 8 * layer + (i | 1) + 1)
                    link(dve.tensor_tensor(yt, yt, B[4 + i // 2][:, i % 2 * 256:i % 2 * 256 + 256], ALU.add))
                    if c:
                        dve.wait_ge(yo_ps, layer + 1)
                        link(dve.tensor_tensor(yoff[:].rearrange("p (e d) -> p e d", e=HPG), B[2 + g // 2][:, g % 2 * 256:g % 2 * 256 + 256].rearrange("p (e d) -> p e d", e=HPG),
                                               T[5][:, HEADS + g * HPG:HEADS + (g + 1) * HPG].unsqueeze(2).broadcast_to([P, HPG, HD]), ALU.mult))
                        step(dve.tensor_tensor(yt, yt, yoff[:], ALU.add))

                def segment(i):
                    c, g = divmod(i, GROUPS)
                    dve.wait_ge(seg_ps, 8 * layer + i + 1)
                    if i >= 2:
                        dve.wait_ge(yd_ps, 8 * layer + i - 1)
                    for e in range(HPG):
                        h = c * HEADS + g * HPG + e
                        ins = dve.tensor_scalar(dec[:, i % 2, e], B[i % 2][:, e * P:e * P + P], T[4][:, h:h + 1], 0.0, ALU.subtract, ALU.min)
                    ins.then_inc(seg_done, 1)

                segment(0)
                for i in range(2 * GROUPS):
                    c, g = divmod(i, GROUPS)
                    if i + 1 < 2 * GROUPS:
                        segment(i + 1)
                    if i % 2 == 0 and i:
                        gather_y(i - 2)
                        gather_y(i - 1)
                    dve.wait_ge(decay_done, 8 * layer + i + 1)
                    dve.tensor_tensor(dec[:, i % 2], dec[:, i % 2], cbm[:, c, g].unsqueeze(1).broadcast_to([P, HPG, P]), ALU.mult).then_inc(wdec_done, 1)
                gather_y(6)
                gather_y(7)
                dve.wait_ge(dve_order, o.n)
                dve.wait_ge(proj_evac, WIN * (layer + 1))
                for t in range(NT):
                    ins = dve.tensor_tensor(y[:, t], y[:, t], z[:, t], ALU.mult)
                    if t < NT - 1:
                        step(ins)
                ins.then_inc(yz_done, 1)
                dve.wait_ge(yms_done, layer + 1)
                link(dve.reciprocal(ss[:, 6:8], ss[:, 6:8]))
                for t in range(NT):
                    ins = dve.tensor_scalar(y[:, t], y[:, t], ss[:, 6 + t:7 + t], None, ALU.mult)
                    if t < NT - 1:
                        step(ins)
                ins.then_inc(yn_done, 1)
                make_diag(2 * layer, layer, G1)
                for k in range(KD):
                    dve.wait_ge(msh_done, KD * layer + k // 2 * 2 + 2)
                    ins = dve.scalar_tensor_tensor(msl[:, k], B[4 + k // 2][:, k % 2 * SEQ:k % 2 * SEQ + SEQ], pcol[:, layer, SSDW + k:SSDW + k + 1],
                                                   msh[:, k].bitcast(F32), ALU.mult, ALU.subtract)
                ins.then_inc(msl_done, 1)
                for i in range(WOUT):
                    lo(first_wout[layer] + i)
                    if layer == 0 and i >= 4:
                        ada(1, 0, i - 4)
                dve.wait_ge(gemm_done, first_wout[layer] + WOUT)
                residual(2 * layer, lambda q: B[4 + q][:], scratch)
                normalise(2 * layer + 1)
                modulate(2 * layer + 1, layer, SH2, SC2, low=(layer == 0))

                def product(n, F, turn, nt):
                    dve.wait_ge(sg_done, F + 1)
                    dve.wait_ge(gemm_done, n + RING * turn)
                    dve.tensor_tensor(actn[:, 0:nt], gate[:, 0:nt], B[1][:].rearrange("p (t n) -> p t n", t=NT)[:, 0:nt], ALU.mult).then_inc(act_done, 1)

                def turned_low(F, nt):
                    dve.wait_ge(actTh_done, F + 1)
                    dve.tensor_tensor(actTl[:, :, 0:nt * P], B[2][:].rearrange("p (k t) -> p k t", k=KK)[:, :, 0:nt * P],
                                      actTh[:, :, 0:nt * P].bitcast(F32), ALU.subtract).then_inc(actT_done, 1)

                if layer == 0:
                    lo(dense0)
                    lo(dense0 + 1)
                    with dve.Fori(0, NJ // 2) as i:
                        for b in range(2):
                            n, F = dense0 + 2 + 3 * b, 2 * i + b + 1
                            lo(n, i)
                            for k in range(2):
                                ada(1, i + b, 4 * (1 - b) + k)
                            lo(n + 1, i)
                            product(n, F - 1, i, NT)
                            ada(1, i + b, 4 * (1 - b) + 2)
                            lo(n + 2, i)
                            turned_low(F - 1, NT)
                            ada(1, i + b, 4 * (1 - b) + 3)
                            if b == 0:
                                mod_evac(1, i)
                    product(dense0 + 3 * NJ - 1, NJ - 1, 0, NT)
                    lo(dense0 + 3 * NJ - 1)
                    turned_low(NJ - 1, NT)
                    make_diag(1, 0, G2)
                    for k in range(4, KD):
                        ada(1, SEG - 1, k)
                    mod_evac(1, SEG - 1)
                    dve.wait_ge(gemm_done, dense0 + 3 * NJ)
                    residual(1, lambda q: B[4 + q][:], scratch)

            DIFF, P1, MX, MASK, GATE, OH, POS, CNT, RANK, SEL = (rt[:, 0:2], rt[:, 2:4], rt[:, 16:32], rt[:, 32:48], rt[:, 48:64],
                                                               rt[:, 64:80], rt[:, 80:96], rt[:, 96:104], rt[:, 104:112], rt[:, 112:120])
            LG, IX, JP, JG, JE, CUR, TMP8, NOV = (rt[:, 120:136], rt[:, 136:152], rt[:, 152:180], rt[:, 180:208], rt[:, 208:224],
                                                  rt[:, 224:228], rt[:, 228:236], rt[:, 236:240])

            def v3(a):
                return a.rearrange("p (t e) -> p t e", t=NT)

            lo(moe0)
            lo(moe0 + 1)
            link(dve.memset(rt[:], 0.0))
            dve.wait_ge(lg_ps, 1)
            link(dve.tensor_tensor(v3(LG), B[2][:, 0:16].rearrange("p (t e) -> p t e", t=NT), rb[:].unsqueeze(1).broadcast_to([P, NT, EXPERTS]), ALU.add))
            for t in range(NT):
                link(dve.max(MX[:, 8 * t:8 * t + 8], LG[:, 8 * t:8 * t + 8]))
                link(dve.max_index(tix[:, t], MX[:, 8 * t:8 * t + 8], LG[:, 8 * t:8 * t + 8]))
            link(dve.tensor_copy(v3(IX), tix[:]))
            dve.tensor_tensor(DIFF, v3(MX)[:, :, 1], v3(MX)[:, :, 0], ALU.subtract).then_inc(rdiff, 1)
            dve.wait_ge(rexp, 1)
            link(dve.tensor_scalar(P1, DIFF, 1.0, None, ALU.add))
            link(dve.reciprocal(P1, P1))
            link(dve.tensor_tensor(DIFF, DIFF, P1, ALU.mult))
            for t in range(NT):
                e8 = slice(8 * t, 8 * t + 8)
                link(dve.tensor_scalar(MASK[:, e8], i8[:], IX[:, 8 * t:8 * t + 1], None, ALU.is_equal))
                link(dve.tensor_scalar(OH[:, e8], i8[:], IX[:, 8 * t + 1:8 * t + 2], None, ALU.is_equal))
                link(dve.tensor_scalar(GATE[:, e8], MASK[:, e8], P1[:, t:t + 1], None, ALU.mult))
                link(dve.scalar_tensor_tensor(GATE[:, e8], OH[:, e8], DIFF[:, t:t + 1], GATE[:, e8], ALU.mult, ALU.add))
                ins = dve.tensor_tensor(MASK[:, e8], MASK[:, e8], OH[:, e8], ALU.add)
                if t < NT - 1:
                    link(ins)
            ins.then_inc(mask_done, 1)
            dve.wait_ge(mask_done, 1)
            link(dve.memset(JP, -1.0))
            dve.wait_ge(pos_ps, 1)
            link(dve.scalar_tensor_tensor(POS, B[2][:, 16:32], 1.0, MASK, ALU.add, ALU.mult))
            link(dve.tensor_scalar(POS, POS, -1.0, None, ALU.add))
            link(dve.tensor_scalar(CNT, B[2][:, 32:40], float(P), None, ALU.is_gt))
            for e in range(1, EXPERTS):
                link(dve.tensor_tensor(RANK[:, e:e + 1], RANK[:, e - 1:e], CNT[:, e - 1:e], ALU.add))
            link(dve.tensor_tensor(NOV[:, 0:1], RANK[:, 7:8], CNT[:, 7:8], ALU.add))
            link(dve.tensor_scalar(NOV[:, 1:2], NOV[:, 0:1], 1.0, None, ALU.is_ge))
            link(dve.tensor_scalar(NOV[:, 2:3], NOV[:, 0:1], 3.0, 4.0, ALU.is_ge, ALU.add))
            link(dve.tensor_tensor(JE[:, 0:1], NOV[:, 1:2], NOV[:, 2:3], ALU.add))
            link(dve.tensor_copy(JE[:, 1:9], i8[:]))
            JP3, JG3 = (a.rearrange("p (t j) -> p t j", t=NT) for a in (JP, JG))
            link(dve.tensor_copy(JP3[:, :, 0:8], v3(POS)))
            link(dve.tensor_copy(JG3[:, :, 1:9], v3(GATE)))
            for k in range(4):
                link(dve.scalar_tensor_tensor(SEL, RANK, float(k), CNT, ALU.is_equal, ALU.mult))
                link(dve.scalar_tensor_tensor(TMP8, i8[:], 0.0, SEL, ALU.add, ALU.mult))
                link(dve.tensor_reduce(JE[:, 9 + k:10 + k], TMP8, AX_X, ALU.add))
                for t in range(NT):
                    e8 = slice(8 * t, 8 * t + 8)
                    link(dve.scalar_tensor_tensor(TMP8, POS[:, e8], 1.0 - P, SEL, ALU.add, ALU.mult))
                    link(dve.tensor_reduce(JP3[:, t, 8 + k:9 + k], TMP8, AX_X, ALU.add))
                    link(dve.tensor_scalar(JP3[:, t, 8 + k:9 + k], JP3[:, t, 8 + k:9 + k], -1.0, None, ALU.add))
                    link(dve.tensor_tensor(TMP8, GATE[:, e8], SEL, ALU.mult))
                    link(dve.tensor_reduce(JG3[:, t, 9 + k:10 + k], TMP8, AX_X, ALU.add))
            dve.memset(put[1][:].bitcast(F32), 0.0).then_inc(put_cleared, 1)
            dve.memset(mixed[:], 0.0).then_inc(scat_done, 1)
            dve.wait_ge(scat_done, 1)
            dve.wait_ge(put_cleared, 1)
            dve.tensor_copy(table[:, 0:16], JE).then_inc(table_done, 1)
            dve.wait_ge(table_done, 1)
            pairs = dve.value_load(table[0:1, 0:1], min_val=4, max_val=6)

            def make_pick(job):
                link(dve.tensor_copy(CUR[:, 0:2].unsqueeze(2), JP3[:, :, bass.ds(job, 1)]))
                for t in range(NT):
                    ins = dve.tensor_scalar(pick[:, t], slots[:], CUR[:, t:t + 1], None, ALU.is_equal)
                    if t < NT - 1:
                        step(ins)
                ins.then_inc(pick_done, 1)

            def job_in(job, b):
                dve.wait_ge(jobh_done, job + 1)
                dve.tensor_tensor(jobl[b][:], h32[:], jobh[b][:].bitcast(F32), ALU.subtract).then_inc(jobl_done, 1)

            def job_out(job):
                dve.wait_ge(yh_done, job + 2)
                for half in range(2):
                    ins = dve.tensor_tensor(yl[:, half * 512:half * 512 + 512], B[4 + half][:], yh[:, half * 512:half * 512 + 512].bitcast(F32), ALU.subtract)
                ins.then_inc(yl_done, 1)
                link(dve.tensor_copy(CUR[:, 2:4].unsqueeze(2), JG3[:, :, bass.ds(job + 1, 1)]))

            def add_rows(job, t):
                dve.wait_ge(scat_ps, 2 * job + t + 3)
                for half in range(2):
                    m_ = mixed[:, t, half * 512:half * 512 + 512]
                    ins = dve.scalar_tensor_tensor(m_, B[6 + half][:], CUR[:, 2 + t:3 + t], m_, ALU.mult, ALU.add)
                ins.then_inc(scat_done, 1)

            def moe_iter(n, F, turn, ended=None, ended_before=None, incoming=None):
                lo(n, turn)
                lo(n + 1, turn)
                product(n, F - 1, turn, 1)
                if ended_before is not None:
                    add_rows(ended_before, 1)
                    make_pick(incoming)
                if ended is not None:
                    job_out(ended)
                lo(n + 2, turn)
                turned_low(F - 1, 1)
                if ended is not None:
                    add_rows(ended, 0)

            IN, OUT = 2, 1
            make_pick(0)
            job_in(0, 0)
            done = o.n
            with dve.Fori(0, pairs) as m:
                o.n = done + 2 * (IN + OUT) * m
                for b in range(2):
                    job, n0, F0, turn = 2 * m + b, moe0 + 2 + 33 * b, NJ + 22 * m + NJ * b, NJ * m
                    moe_iter(n0, F0 + 1, turn, ended=job - 1)
                    moe_iter(n0 + 3, F0 + 2, turn, ended_before=job - 1, incoming=job + 1)
                    job_in(job + 1, 1 - b)
                    n0 += 6
                    with dve.Fori(0, 4) as i:
                        for c in range(2):
                            moe_iter(n0 + 3 * c, F0 + 2 * i + c + 3, turn + i)
                    moe_iter(n0 + 24, F0 + NJ, turn)
            o.n = done + 2 * (IN + OUT) * pairs
            job_out(2 * pairs - 1)
            for t in range(NT):
                add_rows(2 * pairs - 1, t)
            make_diag(3, 1, G2)
            residual(3, lambda q: mixed[:, q // 2, q % 2 * 512:q % 2 * 512 + 512], scratch)
            dve.wait_ge(fn_landed, 16)
            dve.wait_ge(rms_done, 5)
            link(dve.reciprocal(ss[:, 2:4], ss[:, 2:4]))
            for t in range(NT):
                dve.scalar_tensor_tensor(xn[:, t], x[:, t], ss[:, 2 + t:3 + t], fnw[:], ALU.mult, ALU.mult).then_inc(out_done, 1)


_INS = ["x", "c", "ada_w", "ada_b", "w_in", "conv_w", "conv_b", "dt_bias", "a_log", "d_skip", "ssd_norm_w",
        "gmlp_v_norm_w", "gmlp_ws", "gmlp_bs", "gmlp_out_norm_w", "w_out", "dense_w_gate", "dense_w_up",
        "dense_w_down", "router_w", "router_b", "moe_w_gate", "moe_w_up", "moe_w_down", "final_norm_w"]


def kernel(**inputs):
    import numpy as np
    import concourse.bacc as bacc
    from concourse.bass_utils import run_bass_kernel_spmd

    nc = bacc.Bacc("TRN2", target_bir_lowering=False, num_devices=1)
    arrays, args = {}, []
    for name in _INS:
        a = np.ascontiguousarray(inputs[name])
        arrays[f"in_{name}"] = a
        args.append(nc.dram_tensor(f"in_{name}", a.shape, mybir.dt.from_np(a.dtype), kind="ExternalInput").ap())
    out = nc.dram_tensor("out", (1, SEQ, D), F32, kind="ExternalOutput").ap()
    hybrid_trunk(nc, *args, out)
    r = run_bass_kernel_spmd(nc, [arrays], core_ids=[0])
    return r.results[0]["out"]
```

```python
from contextlib import ExitStack

import concourse.bass as bass
from concourse import mybir

F32 = mybir.dt.float32
F32R = mybir.dt.float32r
BF16 = mybir.dt.bfloat16
I32 = mybir.dt.int32
U32 = mybir.dt.uint32
ALU = mybir.AluOpType
ACT = mybir.ActivationFunctionType
AX_X = mybir.AxisListType.X

P = 128
D = 1024
KD = D // P
SEQ = 256
NT = SEQ // P
LAYERS = 2
HEADS = 16
HD = 64
GROUPS = 4
HPG = HEADS // GROUPS
STATE = 128
CONV_K = 4
PAD = CONV_K - 1
XBC = D + 2 * GROUPS * STATE
CX = XBC // P
GH = 8
FF = 2816
EXPERTS = 8
EPS = 1e-6
D_IN = 2 * D + 2 * GROUPS * STATE + HEADS + 2 * D
COL_Z, COL_XBC = 0, D
COL_DT = COL_XBC + XBC
COL_U = COL_DT + HEADS
COL_V = COL_U + D

UNIT = 2048
PANEL = UNIT // KD
RING = 6
LEAD = 3
AHEAD = 2
START = KD
NJ = FF // PANEL
KK = UNIT // D
SEG = 6
JOBS = 14
SMALL = 104
CONVB, SSDW, VNW, ONW = 64, 80, 88, 96
SH1, SC1, G1, SH2, SC2, G2 = range(6)
WIN = 4 * (D // PANEL) + (XBC - D) // PANEL
WOUT = 2 * D // (KK * P)
SCAN = 12
SPATIAL_AFTER = (15, 17, 18, 19)


class Order:

    def __init__(self, eng, sem):
        self.eng, self.sem, self.n = eng, sem, 0

    def step(self, ins):
        ins.then_inc(self.sem, 1)
        self.n = self.n + 1

    def link(self, ins):
        self.step(ins)
        self.eng.wait_ge(self.sem, self.n)


def hybrid_trunk(nc, x_in, c_in, ada_w, ada_b, w_in, conv_w, conv_b, dt_bias, a_log, d_skip, ssd_norm_w,
                 gmlp_v_norm_w, gmlp_ws, gmlp_bs, gmlp_out_norm_w, w_out, dense_w_gate, dense_w_up,
                 dense_w_down, router_w, router_b, moe_w_gate, moe_w_up, moe_w_down, final_norm_w, out):
    with ExitStack() as ctx:
        free = [(nc.sbuf_base + 63) // 64 * 64]

        def place(name, shape, dt=F32, at=None):
            size = 1
            for s in shape[1:]:
                size *= s
            size = (size * (2 if dt == BF16 else 4) + 31) // 32 * 32
            if at is None:
                at = free[0]
                free[0] += size
                assert free[0] <= nc.sbuf_usable_end, (name, free[0])
            return nc.alloc_sbuf_tensor_at(name, shape, dt, offset=at), at

        raw, _ = place("raw", [P, RING, UNIT])
        wh, _ = place("wh", [P, 2, UNIT], F32R)
        wl, _ = place("wl", [P, 2, UNIT], F32R)
        adaw, _ = place("adaw", [P, 2, D])
        acc, _ = place("acc", [P, D])
        x, _ = place("x", [P, NT, D])
        xn, at_xn = place("xn", [P, NT, D])
        y, _ = place("y", [P, NT, D], at=at_xn)
        hTh, at_hTh = place("hTh", [P, KD, SEQ], F32R)
        hTl, at_hTl = place("hTl", [P, KD, SEQ], F32R)
        z, at_z = place("z", [P, NT, D])
        v, at_v = place("v", [P, NT, D])
        u, at_u = place("u", [P, KD, SEQ])
        padded, at_pad = place("padded", [P, CX, PAD + SEQ])
        xbc, at_xbc = place("xbc", [P, CX, SEQ])
        bmN, _ = place("bmN", [P, GROUPS, STATE])
        dec_in, at_a = place("dec_in", [P, 2, HPG, P])
        dec, at_e = place("dec", [P, 2, HPG, P])
        wsT, at_wsT = place("wsT", [P, GH, P])
        bsb, _ = place("bsb", [P, GH, P])
        xs, _ = place("xs", [P, NT, D], at=at_pad)
        wsraw, _ = place("wsraw", [P, GH, P], at=at_a)
        vsq, _ = place("vsq", [P, NT, D], at=at_z)
        usq, _ = place("usq", [P, KD, SEQ], at=at_xbc + KD * SEQ * 4)
        gbc, _ = place("gbc", [P, D], at=at_a)
        diag, _ = place("diag", [P, KD, P], at=at_e)
        state, _ = place("state", [P, GROUPS, HPG * HD], at=at_xbc)
        xdec, _ = place("xdec", [P, D], at=at_xbc + D * 4)
        mgh, _ = place("mgh", [P, KD, SEQ], F32R, at=at_hTh)
        mgl, _ = place("mgl", [P, KD, SEQ], F32R, at=at_hTl)
        msh, _ = place("msh", [P, KD, SEQ], F32R, at=at_xbc)
        msl, _ = place("msl", [P, KD, SEQ], F32R, at=at_xbc + KD * SEQ * 4)
        hT, _ = place("hT", [P, KD, SEQ], at=at_xbc)
        at_bc = at_pad + KD * (PAD + SEQ) * 4
        cbm, _ = place("cbm", [P, NT, GROUPS, P], at=at_bc)
        yoff, _ = place("yoff", [P, HPG * HD], at=at_bc + 4096)
        rroot, _ = place("rroot", [P, SEQ], at=at_bc + 5120)
        gtmp, _ = place("gtmp", [P, 2, SEQ], at=at_bc + 6144)
        gate, _ = place("gate", [P, NT, PANEL], at=at_u)
        actn, _ = place("actn", [P, NT, PANEL], at=at_u + 2048)
        actTh, _ = place("actTh", [P, KK, SEQ], F32R, at=at_u + 4096)
        actTl, _ = place("actTl", [P, KK, SEQ], F32R, at=at_u + 6144)
        mixed, _ = place("mixed", [P, NT, D], at=at_z)
        yh, _ = place("yh", [P, D], F32R, at=at_v)
        yl, _ = place("yl", [P, D], F32R, at=at_v + 4096)
        jobh = [place(f"jobh{b}", [P, KD, P], F32R, at=a)[0] for b, a in enumerate((at_hTh, at_hTl))]
        jobl = [place(f"jobl{b}", [P, KD, P], F32R, at=a + 4096)[0] for b, a in enumerate((at_hTh, at_hTl))]
        wh2, _ = place("wh2", [P, UNIT], F32R, at=at_xbc)
        wl2, _ = place("wl2", [P, UNIT], F32R, at=at_xbc + UNIT * 4)
        h32, _ = place("h32", [P, KD, P], at=at_pad + 8192)
        pick, _ = place("pick", [P, NT, P], at=at_pad)
        put = [place(f"put{b}", [P, NT, P], F32R, at=at_pad + 1024 * (1 + b))[0] for b in range(2)]
        rt, _ = place("rt", [P, 256], at=at_pad + 3072)
        table, _ = place("table", [P, 16], I32, at=at_pad + 4096)
        tix, _ = place("tix", [P, NT, 8], U32, at=at_pad + 4160)
        fnw, _ = place("fnw", [P, D], at=at_wsT)

        acc0, _ = place("acc0", [P, UNIT], at=at_z)
        prows, _ = place("prows", [P, 2 * LAYERS, P], at=at_v)
        crows, _ = place("crows", [KD, P], at=at_v + 2 * LAYERS * P * 4)

        ident, _ = place("ident", [P, P])
        upper, _ = place("upper", [P, P])
        strict, _ = place("strict", [P, P])
        ones, _ = place("ones", [P, P])
        slots, _ = place("slots", [P, P])
        pcol, _ = place("pcol", [P, LAYERS, SMALL])
        abcol, _ = place("abcol", [P, LAYERS * SEG * KD])
        mod, _ = place("mod", [P, LAYERS * SEG, KD])
        cond, _ = place("cond", [P, KD])
        hv, _ = place("hv", [P, 3, HEADS])
        dtw, _ = place("dtw", [P, KD, HEADS])
        rw, _ = place("rw", [P, KD, EXPERTS])
        rb, _ = place("rb", [P, EXPERTS])
        i8, _ = place("i8", [P, EXPERTS])
        epsb, _ = place("epsb", [P, 1])
        ss, _ = place("ss", [P, 8])
        table_load, _ = place("table_load", [P, 1])
        vs, _ = place("vs", [P, NT * GH])
        dtt, _ = place("dtt", [P, 6, NT * HEADS])
        zeros, _ = place("zeros", [P, 512], BF16)

        B = [ctx.enter_context(nc.psum_tensor(f"bank{b}", [P, 512], F32)) for b in range(8)]

        def sem(name):
            return ctx.enter_context(nc.semaphore(name))

        landed = [sem(f"landed{s}") for s in range(RING)]
        ada_landed = [sem(f"ada_landed{s}") for s in range(2)]
        (hi_done, split_done, gemm_done, ada_used, mod_ps, mod_done, consts, c_landed, c_ps, small_landed, small_ps, small_used,
         cond_ready, x_landed, rms_done, xn_ready, xT_ps, hT_done, hTh_done, hTl_done, ws_landed, wsT_ps,
         wsT_done, dtw_landed, hv_landed, dt_ps, dt_abs, dt_exp, dA_done, acs_ps, acs_done, acs_exp, proj_evac,
         conv_done, silu_done, bs_landed, v_sq, v_sum, v_ms, v_done, sv_ps, gate_done, gsq_done, gss_ps, grms_done, u_done,
         mgh_done, mgl_done, xs_ps, xs_done, cb_ps, cb_done, skip_done, xdt_done, xdt1_done, bm_done, st_ps, st_done, decin_done,
         seg_ps, seg_done, decay_done, wdec_done, yd_ps, yo_ps, y_done, yz_done, yms_done, yn_done, yT_ps,
         msh_done, msl_done, diag_done, gb_ps, gb_done, x_tile, tile_done, x_done, act_order, dve_order, pool_order,
         sg_done, act_done, tp_ps, actTh_done, actT_done, r_landed, lg_ps, rdiff, rexp, mask_done, pos_ps,
         put_cleared, table_done, pick_done, gather_ps, h32_done, jobh_done, jobl_done, yh_done, yl_done, scat_ps, scat_done,
         fn_landed, out_done, stored) = [sem(n) for n in (
            "hi_done split_done gemm_done ada_used mod_ps mod_done consts c_landed c_ps small_landed small_ps small_used "
            "cond_ready x_landed rms_done xn_ready xT_ps hT_done hTh_done hTl_done ws_landed wsT_ps "
            "wsT_done dtw_landed hv_landed dt_ps dt_abs dt_exp dA_done acs_ps acs_done acs_exp proj_evac "
            "conv_done silu_done bs_landed v_sq v_sum v_ms v_done sv_ps gate_done gsq_done gss_ps grms_done u_done "
            "mgh_done mgl_done xs_ps xs_done cb_ps cb_done skip_done xdt_done xdt1_done bm_done st_ps st_done decin_done "
            "seg_ps seg_done decay_done wdec_done yd_ps yo_ps y_done yz_done yms_done yn_done yT_ps "
            "msh_done msl_done diag_done gb_ps gb_done x_tile tile_done x_done act_order dve_order pool_order "
            "sg_done act_done tp_ps actTh_done actT_done r_landed lg_ps rdiff rexp mask_done pos_ps "
            "put_cleared table_done pick_done gather_ps h32_done jobh_done jobl_done yh_done yl_done scat_ps scat_done "
            "fn_landed out_done stored").split()]

        def slot(n):
            return (START + n) % RING

        first_win = [0, WIN + WOUT + 3 * NJ]
        first_wout = [f + WIN for f in first_win]
        dense0 = first_wout[0] + WOUT
        moe0 = first_wout[1] + WOUT

        def splits(n):
            return 3 if dense0 <= n < dense0 + 3 * NJ or n >= moe0 else 2

        def first_of(n):
            return max(f for f in (first_win[0], dense0, first_win[1], moe0) if f <= n)

        def pair_number(n):
            return (n - first_of(n)) % splits(n)

        def pair_of(n):
            pair = pair_number(n)
            return (wh2[:], wl2[:]) if pair == 2 else (wh[:, pair], wl[:, pair])

        def last_in_pair(n):
            return max((m for m in range(n) if pair_number(m) == pair_number(n)), default=None)

        def chunks(i):
            c = (2 * i + KD) % CX
            return c, c + 1

        def win_col(i):
            if i < CX // 2:
                return COL_XBC + chunks(i)[0] * P
            part, i = divmod(i - CX // 2, D // PANEL)
            return (COL_V, COL_U, COL_Z)[part] + i * PANEL

        def early_ada(layer, i):
            if layer == 0 and 0 <= i < KD:
                return [(0, G1, i)]
            if layer == 1 and 0 <= i < 4:
                return [(1, SC2, 4 + i)]
            return [(layer, (SH2, G2)[layer], k) for k in {9: (0, 1), 10: (2, 3), 11: (4, 5), 13: (6,), 14: (7,)}.get(i, ())]

        def late_ada(i):
            seg, first, last = {2: (SC2, 0, 1), 3: (SC2, 1, 2), 4: (SC2, 2, 4), 5: (SC2, 4, 6), 6: (SC2, 6, 8), 7: (G2, 0, 2)}.get(i, (0, 0, 0))
            return [(0, seg, k) for k in range(first, last)]

        def panel(w, col):
            return w[:, bass.ds(col, PANEL)].rearrange("(k p) n -> p k n", p=P)

        def rows(w, row):
            return w[bass.ds(row, KK * P), :].rearrange("(k p) n -> p k n", p=P)

        block = ctx.enter_context(nc.Block())

        @block.sync
        def _(sp):
            def load(n, src, k, turn=0):
                if not (isinstance(turn, int) and START + n + RING * turn < RING):
                    sp.wait_ge(split_done, START + n + RING * turn - RING + 1)
                sp.dma_start(raw[:, slot(n)].rearrange("p (k n) -> p k n", k=k), src).then_inc(landed[slot(n)], 16)

            def load_ada(layer, seg, k):
                a = 8 * (SEG * layer + seg - 2) + k
                if not (isinstance(a, int) and a < 2):
                    sp.wait_ge(ada_used, a - 1)
                sp.dma_start(adaw[:, k % 2], ada_w[layer, k * P:(k + 1) * P, bass.ds(seg * D, D)]).then_inc(ada_landed[k % 2], 16)

            def load_rows(layer, first):
                if first:
                    for w, row in ((conv_w[layer].rearrange("j (c p) -> (j c) p", p=P), 0),
                                   (conv_b[layer].rearrange("(c p) -> c p", p=P), CONVB),
                                   (ssd_norm_w[layer].rearrange("(c p) -> c p", p=P), SSDW),
                                   (gmlp_v_norm_w[layer].rearrange("(c p) -> c p", p=P), VNW),
                                   (gmlp_out_norm_w[layer].rearrange("(c p) -> c p", p=P), ONW)):
                        sp.dma_start(prows[row:row + w.shape[0], 2 * layer], w).then_inc(small_landed, 16)
                else:
                    sp.dma_start(prows[0:SEG * KD, 2 * layer + 1], ada_b[layer].rearrange("(c p) -> c p", p=P)).then_inc(small_landed, 16)

            sp.dma_start(crows[:], c_in[0].rearrange("(c p) -> c p", p=P)).then_inc(c_landed, 16)
            for k in range(START):
                load(k - START, ada_w[0, k * P:(k + 1) * P, 0:UNIT].unsqueeze(1), 1)
                if k == 1:
                    for t in range(NT):
                        sp.dma_start(x[:, t], x_in[0, t * P:(t + 1) * P, :]).then_inc(x_landed, 16)
                if k == 5:
                    for layer in range(LAYERS):
                        load_rows(layer, True)
                        load_rows(layer, False)

            for layer in range(LAYERS):
                for i in range(AHEAD):
                    load(first_win[layer] + i, panel(w_in[layer], win_col(i)), KD)
                if layer:
                    sp.wait_ge(x_done, 2)
                sp.dma_start(wsraw[:], gmlp_ws[layer].rearrange("h t s -> t h s")).then_inc(ws_landed, 16)
                sp.dma_start(dtw[:], w_in[layer, :, COL_DT:COL_DT + HEADS].rearrange("(k p) n -> p k n", p=P)).then_inc(dtw_landed, 16)
                for n, w in enumerate((dt_bias, a_log, d_skip)):
                    sp.dma_start(hv[:, n], w[layer].partition_broadcast(P)).then_inc(hv_landed, 16)
                sp.dma_start(bsb[:].rearrange("p h t -> p (h t)"), gmlp_bs[layer].rearrange("h t -> (h t)").partition_broadcast(P)).then_inc(bs_landed, 16)
                for i in range(WIN + LEAD):
                    if AHEAD <= i < WIN:
                        load(first_win[layer] + i, panel(w_in[layer], win_col(i)), KD)
                    for part in early_ada(layer, i - LEAD):
                        load_ada(*part)
                for i in range(WOUT + LEAD):
                    if i < WOUT:
                        load(first_wout[layer] + i, rows(w_out[layer], D * (1 - i // 4) + KK * P * (i % 4)), KK)
                    if layer == 0:
                        for part in late_ada(i - LEAD):
                            load_ada(*part)
                if layer == 0:
                    g, up, dn = dense_w_gate[0], dense_w_up[0], dense_w_down[0]
                    load(dense0, panel(g, 0), KD)
                    load(dense0 + 1, panel(up, 0), KD)
                    for k in range(2, 4):
                        load_ada(0, G2, k)

                    def load_pair(i, seg_of):
                        for b in range(2):
                            n = dense0 + 2 + 3 * b
                            load(n, panel(g, (2 * i + b + 1) * PANEL), KD, i)
                            load(n + 1, panel(up, (2 * i + b + 1) * PANEL), KD, i)
                            load(n + 2, rows(dn, (2 * i + b) * PANEL), KK, i)
                            for k in range(4):
                                load_ada(*seg_of(b), 4 * (1 - b) + k)

                    load_pair(0, lambda b: ((0, G2), (1, SH1))[b])
                    with sp.Fori(1, NJ // 2) as i:
                        load_pair(i, lambda b: (1, i - 1 + b))
                    load(dense0 + 3 * NJ - 1, rows(dn, (NJ - 1) * PANEL), KK)

            sp.dma_start(rw[:], router_w[0].rearrange("(k p) e -> p k e", p=P)).then_inc(r_landed, 16)
            sp.dma_start(rb[:], router_b[0].partition_broadcast(P)).then_inc(r_landed, 16)

            def expert(e):
                return [w[0, bass.ds(e, 1)].rearrange("e k n -> (e k) n") for w in (moe_w_gate, moe_w_up, moe_w_down)]

            def expert_of(job):
                return expert(sp.value_load(table[0:1, bass.ds(job + 1, 1)], min_val=0, max_val=EXPERTS - 1))

            def load_iter(n, turn, gate_up_of, down_of, F):
                col = F % NJ * PANEL if isinstance(F, int) else F * PANEL
                load(n, panel(gate_up_of[0], col), KD, turn)
                load(n + 1, panel(gate_up_of[1], col), KD, turn)
                load(n + 2, rows(down_of[2], (F - 1) * PANEL), KK, turn)

            w0 = expert(0)
            load(moe0, panel(w0[0], 0), KD)
            load(moe0 + 1, panel(w0[1], 0), KD)
            load_iter(moe0 + 2, 0, w0, w0, 1)
            sp.dma_start(fnw[:], final_norm_w.partition_broadcast(P)).then_inc(fn_landed, 16)
            sp.wait_ge(table_done, 1)
            pairs = sp.value_load(table[0:1, 0:1], min_val=4, max_val=6)
            with sp.Fori(0, pairs) as m:
                n0, turn = moe0 + 5, NJ * m
                w0 = expert_of(2 * m)
                load_iter(n0, turn, w0, w0, 2)
                n0 += 3
                with sp.Fori(0, 4) as i:
                    for b in range(2):
                        load_iter(n0 + 3 * b, turn + i, w0, w0, 2 * i + b + 3)
                n0 += 24
                w1 = expert_of(2 * m + 1)
                load_iter(n0, turn, w1, w0, NJ)
                n0 += 3
                with sp.Fori(0, 5) as i:
                    for b in range(2):
                        load_iter(n0 + 3 * b, turn + i, w1, w1, 2 * i + b + 1)
                n0 += 30
                w2 = expert_of(2 * m + 2)
                load_iter(n0, turn, w2, w1, NJ)
                n0 += 3
                load_iter(n0, turn, w2, w2, 1)
            for n in range(moe0 + 68, moe0 + 71):
                sp.wait_ge(landed[slot(n)], 16 * ((START + n) // RING + 1) + 16 * NJ * (pairs - 1))
            for t in range(NT):
                sp.wait_ge(out_done, t + 1)
                sp.dma_start(out[0, t * P:(t + 1) * P, :], xn[:, t]).then_inc(stored, 16)
            sp.wait_ge(stored, 16 * NT)

        @block.gpsimd
        def _(pool):
            o = Order(pool, pool_order)
            o.step(pool.memset(ones[:], 1.0))
            o.step(pool.memset(zeros[:], 0.0))
            o.step(pool.memset(epsb[:], EPS))
            o.step(pool.memset(ident[:], 0.0))
            o.step(pool.iota(slots[:], pattern=[[1, P]], base=0, channel_multiplier=0, allow_small_or_imprecise_dtypes=True))
            o.link(pool.iota(i8[:], pattern=[[1, EXPERTS]], base=0, channel_multiplier=0, allow_small_or_imprecise_dtypes=True))
            o.step(pool.affine_select(out=ident[:], in_=ident[:], compare_op=ALU.not_equal, fill=1.0, base=0,
                                      pattern=[[-1, P]], channel_multiplier=1))
            o.step(pool.affine_select(out=upper[:], in_=ones[:], compare_op=ALU.is_ge, fill=0.0, base=0,
                                      pattern=[[1, P]], channel_multiplier=-1))
            pool.affine_select(out=strict[:], in_=ones[:], compare_op=ALU.is_gt, fill=0.0, base=0,
                               pattern=[[1, P]], channel_multiplier=-1).then_inc(consts, 1)
            for layer in range(LAYERS):
                if layer:
                    pool.wait_ge(mgl_done, GH * layer)
                    pool.wait_ge(x_done, 2 * layer)
                pool.memset(padded[:, :, 0:PAD], 0.0).then_inc(consts, 1)

                def decay_in(i):
                    c, g = divmod(i, GROUPS)
                    if i >= 2:
                        pool.wait_ge(seg_ps, 8 * layer + i - 1)
                    pool.tensor_tensor(dec_in[:, i % 2], upper[:].unsqueeze(1).broadcast_to([P, HPG, P]),
                                       dtt[:, 2, c * HEADS + HPG * g:c * HEADS + HPG * (g + 1)].unsqueeze(2).broadcast_to([P, HPG, P]),
                                       ALU.mult).then_inc(decin_done, 1)

                pool.wait_ge(dA_done, layer + 1)
                pool.wait_ge(wsT_done, layer + 1)
                decay_in(0)
                decay_in(1)
                pool.wait_ge(xs_done, layer + 1)
                pool.wait_ge(hv_landed, 48 * (layer + 1))
                for t in range(NT):
                    ins = pool.tensor_tensor(y[:, t].rearrange("p (h d) -> p h d", h=HEADS), xs[:, t].rearrange("p (h d) -> p h d", h=HEADS),
                                             hv[:, 2].unsqueeze(2).broadcast_to([P, HEADS, HD]), ALU.mult)
                    ins.then_inc(skip_done, 1)
                pool.wait_ge(skip_done, NT * (layer + 1))
                pool.tensor_tensor(xs[:, 1].rearrange("p (h d) -> p h d", h=HEADS), xs[:, 1].rearrange("p (h d) -> p h d", h=HEADS),
                                   dtt[:, 0, HEADS:2 * HEADS].unsqueeze(2).broadcast_to([P, HEADS, HD]), ALU.mult).then_inc(xdt1_done, 1)
                for i in range(2 * GROUPS):
                    c, g = divmod(i, GROUPS)
                    pool.wait_ge(decay_done, 8 * layer + i + 1)
                    pool.tensor_tensor(dec[:, i % 2], dec[:, i % 2], cbm[:, c, g].unsqueeze(1).broadcast_to([P, HPG, P]), ALU.mult).then_inc(wdec_done, 1)
                    if i + 2 < 2 * GROUPS:
                        decay_in(i + 2)
            pool.wait_ge(x_done, 3)
            pool.memset(put[1][:].bitcast(F32), 0.0).then_inc(put_cleared, 1)
            pool.memset(mixed[:], 0.0).then_inc(scat_done, 1)

        @block.scalar
        def _(act):
            o = Order(act, act_order)

            def hi(n, turn=0):
                act.wait_ge(landed[slot(n)], 16 * ((START + n) // RING + 1) + 16 * turn)
                if isinstance(turn, int):
                    if last_in_pair(n) is not None:
                        act.wait_ge(gemm_done, last_in_pair(n) + 1)
                else:
                    act.wait_ge(gemm_done, n + 1 - splits(n) + RING * turn)
                if n == dense0 + 2:
                    act.wait_ge(hTl_done, 8)
                elif n == moe0 + 2:
                    act.wait_ge(lg_ps, 1)
                act.activation(pair_of(n)[0], raw[:, slot(n)], ACT.Copy).then_inc(hi_done, 1)

            def root_mean(n):
                act.activation(table_load[:], epsb[:], ACT.Sqrt)
                for t in range(NT):
                    if n:
                        act.wait_ge((x_tile, x_done)[t], n)
                    o.link(act.activation(xn[:, t], x[:, t], ACT.Square, accum_out=ss[:, t:t + 1]))
                    act.activation(ss[:, 2 + t:3 + t], ss[:, t:t + 1], ACT.Sqrt, bias=epsb[:, 0:1], scale=1.0 / D).then_inc(rms_done, 1)

            def turned_hi(n):
                for b in range(4):
                    act.wait_ge(hT_done, 4 * n + b + 1)
                    act.activation(hTh[:, 2 * b:2 * b + 2], hT[:, 2 * b:2 * b + 2], ACT.Copy).then_inc(hTh_done, 1)

            def gb_evac(n):
                act.wait_ge(gb_ps, n + 1)
                for half in range(2):
                    ins = act.activation(gbc[:, half * 512:half * 512 + 512], B[half][:], ACT.Copy)
                ins.then_inc(gb_done, 1)

            act.wait_ge(c_ps, 1)
            act.activation(cond[:], B[3][:, 0:KD], ACT.Silu).then_inc(cond_ready, 1)
            act.wait_ge(consts, 1)
            act.wait_ge(x_landed, 16 * NT)
            for layer in range(LAYERS):
                g0 = first_win[layer]
                if layer:
                    hi(g0)
                    hi(g0 + 1)
                root_mean(2 * layer)
                if layer == 0:
                    hi(g0)
                    hi(g0 + 1)
                turned_hi(2 * layer)

                def square(b):
                    act.wait_ge(yo_ps, layer + 1)
                    act.wait_ge(gate_done, 4 * layer + b + 1)
                    act.activation(usq[:, 2 * b:2 * b + 2], u[:, 2 * b:2 * b + 2], ACT.Square).then_inc(gsq_done, 1)

                for i in range(WIN):
                    act.wait_ge(gemm_done, g0 + i + 1)
                    ps = B[i % 2]
                    if i < 8:
                        c = chunks(i)[0]
                        if i == 0:
                            act.wait_ge(consts, 2 + layer)
                        for b in range(2):
                            w3 = (CONV_K - 1) * CX + c + b
                            act.activation(xbc[:, c + b], ps[:, b * SEQ:b * SEQ + SEQ], ACT.Copy, scale=pcol[:, layer, w3:w3 + 1])
                        ins = act.activation(padded[:, c:c + 2, PAD:PAD + SEQ], ps[:].rearrange("p (c t) -> p c t", c=2), ACT.Copy)
                    elif i < 12:
                        ins = act.activation(v[:, :, PANEL * (i - 8):PANEL * (i - 7)], ps[:].rearrange("p (t n) -> p t n", t=NT), ACT.Gelu_apprx_tanh)
                    elif i < 16:
                        ins = act.activation(u[:, 2 * (i - 12):2 * (i - 12) + 2], ps[:].rearrange("p (c t) -> p c t", c=2), ACT.Gelu_apprx_tanh)
                    else:
                        ins = act.activation(z[:, :, PANEL * (i - 16):PANEL * (i - 15)], ps[:].rearrange("p (t n) -> p t n", t=NT), ACT.Silu)
                    ins.then_inc(proj_evac, 1)
                    if i < WIN - 1:
                        hi(g0 + i + 2)
                    if i == 1:
                        act.wait_ge(dt_abs, layer + 1)
                        act.activation(dtt[:, 1], dtt[:, 1], ACT.Exp, scale=-1.0).then_inc(dt_exp, 1)
                        act.wait_ge(hv_landed, 48 * (layer + 1))
                        act.activation(hv[:, 1], hv[:, 1], ACT.Exp).then_inc(dt_exp, 1)
                    if i == 11:
                        act.wait_ge(acs_done, layer + 1)
                        act.activation(dtt[:, 5], dtt[:, 5], ACT.Exp).then_inc(acs_exp, 1)
                    if 2 <= i <= 9:
                        act.wait_ge(conv_done, CX * layer + 2 * (i - 1))
                        for c in chunks(i - 2):
                            act.activation(xbc[:, c], xbc[:, c], ACT.Silu, bias=pcol[:, layer, CONVB + c:CONVB + c + 1]).then_inc(silu_done, 1)
                    if i == 10:
                        for n in range(4):
                            act.wait_ge(xs_ps, 5 * layer + n + 1)
                            t, half = divmod(n, 2)
                            ins = act.activation(xs[:, t, half * 512:half * 512 + 512], B[4 + n][:], ACT.Copy)
                        ins.then_inc(xs_done, 1)
                    if i == 11:
                        act.wait_ge(xs_ps, 5 * layer + 5)
                        act.activation(bmN[:].rearrange("p g n -> p (g n)"), B[2][:], ACT.Copy).then_inc(bm_done, 1)
                    if i == 12:
                        act.wait_ge(proj_evac, WIN * layer + 12)
                        act.activation(vsq[:].rearrange("p a b -> p (a b)"), v[:].rearrange("p a b -> p (a b)"), ACT.Square).then_inc(v_sq, 1)
                    if i >= SCAN:
                        act.wait_ge(seg_done, 8 * layer + i - SCAN + 1)
                        act.activation(dec[:, i % 2], dec[:, i % 2], ACT.Exp).then_inc(decay_done, 1)
                    if i == 13:
                        act.wait_ge(v_sum, layer + 1)
                        act.activation(vs[:], vs[:], ACT.Sqrt, bias=epsb[:, 0:1], scale=1.0 / P).then_inc(v_ms, 1)
                    if i == 14:
                        act.wait_ge(st_ps, layer + 1)
                        for b in range(2):
                            ins = act.activation(state[:, 2 * b:2 * b + 2].rearrange("p g n -> p (g n)"), B[6 + b][:], ACT.Copy)
                        ins.then_inc(st_done, 1)
                    if i >= 17:
                        square(i - 17)
                square(3)
                act.wait_ge(gss_ps, layer + 1)
                act.activation(B[0][:, 0:SEQ], B[0][:, 0:SEQ], ACT.Sqrt, bias=epsb[:, 0:1], scale=1.0 / D).then_inc(grms_done, 1)
                for h in range(GH):
                    act.wait_ge(u_done, 4 * layer + h // 2 + 1)
                    act.activation(mgh[:, h], u[:, h], ACT.Copy, scale=pcol[:, layer, ONW + h:ONW + h + 1]).then_inc(mgh_done, 1)
                hi(first_wout[layer] + 1)
                act.wait_ge(yz_done, layer + 1)
                for t in range(NT):
                    o.step(act.activation(z[:, t], y[:, t], ACT.Square, accum_out=ss[:, 4 + t:5 + t]))
                act.wait_ge(act_order, o.n)
                act.activation(ss[:, 6:8], ss[:, 4:6], ACT.Sqrt, bias=epsb[:, 0:1], scale=1.0 / D).then_inc(yms_done, 1)
                for i in range(2, WOUT):
                    hi(first_wout[layer] + i)
                    if i == 3:
                        for k in range(KD):
                            act.wait_ge(yT_ps, 4 * layer + k // 2 + 1)
                            act.activation(msh[:, k], B[k // 2][:, k % 2 * SEQ:k % 2 * SEQ + SEQ], ACT.Copy,
                                           scale=pcol[:, layer, SSDW + k:SSDW + k + 1]).then_inc(msh_done, 1)
                    if i == 5:
                        gb_evac(2 * layer)
                after = dense0 if layer == 0 else moe0
                hi(after)
                root_mean(2 * layer + 1)
                hi(after + 1)
                if layer == 0:
                    turned_hi(1)

                def silu_gate(n, F, turn, nt):
                    act.wait_ge(gemm_done, n + 1 + RING * turn)
                    act.wait_ge(act_done, F)
                    act.activation(gate[:, 0:nt], B[0][:].rearrange("p (t n) -> p t n", t=NT)[:, 0:nt], ACT.Silu).then_inc(sg_done, 1)

                def turned_product(F, nt):
                    act.wait_ge(tp_ps, F + 1)
                    act.activation(actTh[:, :, 0:nt * P], B[2][:].rearrange("p (k t) -> p k t", k=KK)[:, :, 0:nt * P], ACT.Copy).then_inc(actTh_done, 1)

                if layer == 0:
                    silu_gate(dense0, 0, 0, NT)
                    with act.Fori(0, NJ // 2) as i:
                        for b in range(2):
                            n, F = dense0 + 2 + 3 * b, 2 * i + b + 1
                            hi(n, i)
                            hi(n + 1, i)
                            hi(n + 2, i)
                            silu_gate(n, F, i, NT)
                            turned_product(F - 1, NT)
                    hi(dense0 + 3 * NJ - 1)
                    turned_product(NJ - 1, NT)
                    gb_evac(1)
            gb_evac(3)
            act.wait_ge(rdiff, 1)
            act.activation(rt[:, 0:2], rt[:, 0:2], ACT.Exp).then_inc(rexp, 1)
            def job_in(job, b):
                act.wait_ge(gather_ps, job + 1)
                if not isinstance(job, int):
                    act.wait_ge(jobl_done, job)
                act.activation(put[b][:].rearrange("p t n -> p (t n)"), B[3][:, 0:SEQ], ACT.Copy)
                for k in range(KD):
                    ins = act.activation(h32[:, k], B[6 + k // 4][:, k % 4 * P:k % 4 * P + P], ACT.Identity, scale=mod[:, SEG + SC2, k:k + 1], bias=mod[:, SEG + SH2, k:k + 1])
                ins.then_inc(h32_done, 1)
                act.wait_ge(h32_done, job + 1)
                act.activation(jobh[b][:], h32[:], ACT.Copy).then_inc(jobh_done, 1)

            def job_out(job, n, turn):
                act.wait_ge(gemm_done, n + RING * turn)
                act.wait_ge(scat_done, 2 * job + 3)
                for half in range(2):
                    ins = act.activation(yh[:, half * 512:half * 512 + 512], B[4 + half][:], ACT.Copy)
                ins.then_inc(yh_done, 1)

            def moe_iter(n, F, turn, ended=None, begun=False):
                if not begun:
                    hi(n, turn)
                hi(n + 1, turn)
                if ended is not None:
                    job_out(ended, n, turn)
                hi(n + 2, turn)
                silu_gate(n, F, turn, 1)
                turned_product(F - 1, 1)

            job_in(0, 0)
            act.wait_ge(table_done, 1)
            pairs = act.value_load(table[0:1, 0:1], min_val=4, max_val=6)
            silu_gate(moe0, NJ, 0, 1)
            with act.Fori(0, pairs) as m:
                for b in range(2):
                    job, n0, F0, turn = 2 * m + b, moe0 + 2 + 33 * b, NJ + 22 * m + NJ * b, NJ * m
                    moe_iter(n0, F0 + 1, turn, job - 1)
                    moe_iter(n0 + 3, F0 + 2, turn)
                    n0 += 6
                    hi(n0, turn)
                    job_in(job + 1, 1 - b)
                    moe_iter(n0, F0 + 3, turn, begun=True)
                    n0 += 3
                    with act.Fori(0, 3) as i:
                        for c in range(2):
                            moe_iter(n0 + 3 * c, F0 + 2 * i + c + 4, turn + i)
                    moe_iter(n0 + 18, F0 + NJ - 1, turn)
                    moe_iter(n0 + 21, F0 + NJ, turn)
            job_out(2 * pairs - 1, moe0 + 68, NJ * (pairs - 1))
            root_mean(4)

        @block.tensor
        def _(pe):
            def three(ps, k, last, ah, al, bh, bl):
                pe.matmul(ps, ah, bh, start=(k == 0), stop=False, skip_group_check=True)
                pe.matmul(ps, ah, bl, start=False, stop=False, skip_group_check=True)
                return pe.matmul(ps, al, bh, start=False, stop=last, skip_group_check=True)

            def unit(n, turn):
                pe.wait_ge(split_done, START + n + 1 + RING * turn)

            def whl(n, k):
                return (w.rearrange("p (k n) -> p k n", k=k) for w in pair_of(n))

            def natural(n, turn, ps_of, xh, xl, nt, ready=None):
                unit(n, turn)
                h, l = whl(n, KD)
                for t in range(nt):
                    for k in range(KD):
                        if ready is not None and t == 0:
                            ready(k)
                        ins = three(ps_of(t), k, k == KD - 1, xh[:, k, t * P:t * P + P], xl[:, k, t * P:t * P + P], h[:, k], l[:, k])
                ins.then_inc(gemm_done, 1)

            def turned(n, ps, ready=None):
                unit(n, 0)
                h, l = whl(n, KD)
                for c in range(2):
                    for k in range(KD):
                        if ready is not None and c == 0:
                            ready(k)
                        ins = three(ps[:, c * SEQ:c * SEQ + SEQ], k, k == KD - 1, h[:, k, c * P:c * P + P], l[:, k, c * P:c * P + P], hTh[:, k], hTl[:, k])
                ins.then_inc(gemm_done, 1)

            def deep(n, turn, xh, xl, k0, nt, start, last):
                unit(n, turn)
                h, l = whl(n, KK)
                by_tile = last and nt == NT
                for o in range(NT * KK if by_tile else KK):
                    for t in (o // KK,) if by_tile else range(nt):
                        kk = o % KK
                        for half in range(2):
                            ps = B[4 + 2 * t + half][:]
                            ins = three(ps, 0 if start and kk == 0 else 1, last and kk == KK - 1, xh[:, k0 + kk, t * P:t * P + P],
                                        xl[:, k0 + kk, t * P:t * P + P], h[:, kk, half * 512:half * 512 + 512], l[:, kk, half * 512:half * 512 + 512])
                    if by_tile and o == KK - 1:
                        ins.then_inc(tile_done, 1)
                ins.then_inc(gemm_done, 1)

            def h_ready(before):
                def wait(k):
                    if k % 2 == 0:
                        pe.wait_ge(hTl_done, before + k // 2 + 1)
                return wait

            def clear_acc(nt):
                for b in range(2 * nt):
                    pe.matmul(B[4 + b][:], zeros[0:1, 0:P], zeros[0:1, :], start=True, stop=False, skip_group_check=True)

            def mod_columns(s):
                pe.wait_ge(ada_used, 8 * (s - 1))
                pe.wait_ge(mod_done, s)
                for k in range(KD):
                    ins = pe.matmul(B[3][:, k:k + 1], acc[:, k * P:k * P + P], ones[:, 0:1], start=True, stop=True, skip_group_check=True)
                ins.then_inc(mod_ps, 1)

            def turn_x(n):
                for t in range(NT):
                    pe.wait_ge(xn_ready, NT * n + t + 1)
                    for k in range(KD):
                        ins = pe.transpose(B[4 + k // 2][:, (k % 2 * NT + t) * P:(k % 2 * NT + t + 1) * P], xn[:, t, k * P:k * P + P], ident[:])
                        if t == NT - 1 and k % 2:
                            ins.then_inc(xT_ps, 1)

            def broadcast_gate(n):
                pe.wait_ge(diag_done, n + 1)
                for half in range(2):
                    ins = pe.matmul(B[half][:], ones[:], diag[:, 4 * half:4 * half + 4].rearrange("p k n -> p (k n)"), start=True, stop=True, skip_group_check=True)
                ins.then_inc(gb_ps, 1)

            pe.wait_ge(consts, 1)
            pe.wait_ge(c_landed, 16)
            pe.transpose(B[3][:, 0:KD], crows[:], ident[0:KD, 0:KD]).then_inc(c_ps, 1)
            pe.wait_ge(small_landed, 16 * 6 * LAYERS)
            for i in range(2 * LAYERS):
                rows_n = (SMALL, SEG * KD)[i % 2]
                ins = pe.transpose(B[2][:, i * P:i * P + rows_n], prows[0:rows_n, i], ident[0:rows_n, 0:rows_n])
            ins.then_inc(small_ps, 1)
            turn_x(0)
            pe.wait_ge(split_done, START)
            pe.wait_ge(cond_ready, 1)
            for k in range(2 * KD):
                ins = pe.matmul(B[3][:, k:k + 1], acc0[:, k * P:k * P + P], ones[:, 0:1], start=True, stop=True, skip_group_check=True)
            ins.then_inc(mod_ps, 2)

            for layer in range(LAYERS):
                if layer:
                    turn_x(2 * layer)
                g0 = first_win[layer]

                def segments(i):
                    pe.wait_ge(decin_done, 8 * layer + i + 1)
                    if i:
                        pe.wait_ge(seg_done, 8 * layer + i)
                    else:
                        pe.wait_ge(bm_done, layer + 1)
                    pe.matmul(B[2][:], ones[:], dec_in[:, i % 2].rearrange("p e q -> p (e q)"), start=True, stop=True, skip_group_check=True).then_inc(seg_ps, 1)

                def within(i):
                    c, g = divmod(i, GROUPS)
                    pe.wait_ge(wdec_done, 8 * layer + i + 1)
                    pe.wait_ge((xdt_done, xdt1_done)[c], layer + 1)
                    if i >= 4:
                        pe.wait_ge(y_done, 4 * layer + i // 2 - 1)
                    for e in range(HPG):
                        h = g * HPG + e
                        ins = pe.matmul(B[4 + i // 2 % 2][:, (i % 2 * HPG + e) * HD:(i % 2 * HPG + e + 1) * HD], dec[:, i % 2, e],
                                        xs[:, c, h * HD:(h + 1) * HD], start=True, stop=True, skip_group_check=True)
                    ins.then_inc(yd_ps, 1)

                def spatial(b):
                    pe.wait_ge(v_done, layer + 1)
                    pe.wait_ge(mod_done, (G1, SEG + SC2)[layer] + 1 + (b > 0))
                    if b:
                        pe.wait_ge(gate_done, 4 * layer + b)
                    for h in (2 * b, 2 * b + 1):
                        for c in range(NT):
                            ins = pe.matmul(B[3][:, (h % 2 * 2 + c) * P:(h % 2 * 2 + c + 1) * P], v[:, c, h * P:h * P + P], wsT[:, h], start=True, stop=True, skip_group_check=True)
                    ins.then_inc(sv_ps, 1)

                def square_sums(b):
                    pe.wait_ge(gsq_done, 4 * layer + b + 1)
                    for h in (2 * b, 2 * b + 1):
                        ins = pe.matmul(B[0][:, 0:SEQ], ones[:], usq[:, h], start=(h == 0), stop=(h == GH - 1), skip_group_check=True)
                    if b == 3:
                        ins.then_inc(gss_ps, 1)

                for i in range(WIN):
                    if i >= 2:
                        pe.wait_ge(proj_evac, WIN * layer + i - 1)
                    if i < 8 or 12 <= i < 16:
                        turned(g0 + i, B[i % 2], h_ready(8 * layer) if i == 0 else None)
                    else:
                        natural(g0 + i, 0, lambda t: B[i % 2][:, t * PANEL:(t + 1) * PANEL], hTh, hTl, NT)
                    if i == 0:
                        pe.wait_ge(dtw_landed, 16 * (layer + 1))
                        if layer == 0:
                            pe.wait_ge(small_used, LAYERS)
                        for t in range(NT):
                            for k in range(KD):
                                ins = pe.matmul(B[2][:, t * HEADS:(t + 1) * HEADS], hT[:, k, t * P:t * P + P], dtw[:, k], start=(k == 0), stop=(k == KD - 1), skip_group_check=True)
                        ins.then_inc(dt_ps, 1)
                    if i == 2:
                        pe.wait_ge(ws_landed, 16 * (layer + 1))
                        for h in range(GH):
                            ins = pe.transpose(B[4 + h // 4][:, h % 4 * P:h % 4 * P + P], wsraw[:, h], ident[:])
                            if h % 4 == 3:
                                ins.then_inc(wsT_ps, 1)
                    if i == 10:
                        pe.wait_ge(dA_done, layer + 1)
                        for c in range(NT):
                            pe.matmul(B[2][:, c * HEADS:(c + 1) * HEADS], upper[:], dtt[:, 2, c * HEADS:(c + 1) * HEADS], start=True, stop=True, skip_group_check=True)
                        pe.matmul(B[2][:, 2 * HEADS:3 * HEADS], ones[:], dtt[:, 2, 0:HEADS], start=True, stop=True, skip_group_check=True).then_inc(acs_ps, 1)
                    if i == 7:
                        pe.wait_ge(silu_done, CX * layer + KD)
                        for c in range(NT):
                            for g in range(GROUPS):
                                ins = pe.matmul(B[6 + c][:, g * P:g * P + P], xbc[:, KD + g, c * P:c * P + P], xbc[:, KD + GROUPS + g, c * P:c * P + P], start=True, stop=True, skip_group_check=True)
                            ins.then_inc(cb_ps, 1)
                    if i == 10:
                        pe.wait_ge(silu_done, CX * (layer + 1))
                        pe.wait_ge(cb_done, 2 * (layer + 1))
                        pe.wait_ge(wsT_done, layer + 1)
                        for n in range(4):
                            t, half = divmod(n, 2)
                            for c in range(4):
                                ins = pe.transpose(B[4 + n][:, c * P:c * P + P], xbc[:, 4 * half + c, t * P:t * P + P], ident[:])
                            ins.then_inc(xs_ps, 1)
                    if i == 11:
                        pe.wait_ge(acs_done, layer + 1)
                        for g in range(GROUPS):
                            ins = pe.transpose(B[2][:, g * P:g * P + P], xbc[:, KD + g, 0:P], ident[:])
                        ins.then_inc(xs_ps, 1)
                    if i >= SCAN:
                        segments(i - SCAN)
                    if i > SCAN:
                        within(i - SCAN - 1)
                    if i == 14:
                        pe.wait_ge(bm_done, layer + 1)
                        for g in range(GROUPS):
                            ins = pe.matmul(B[6 + g // 2][:, g % 2 * 256:g % 2 * 256 + 256], bmN[:, g], xdec[:, g * 256:g * 256 + 256], start=True, stop=True, skip_group_check=True)
                        ins.then_inc(st_ps, 1)
                    if i == 16:
                        pe.wait_ge(st_done, layer + 1)
                        for g in range(GROUPS):
                            ins = pe.matmul(B[6 + g // 2][:, g % 2 * 256:g % 2 * 256 + 256], xbc[:, KD + GROUPS + g, P:2 * P], state[:, g], start=True, stop=True, skip_group_check=True)
                        ins.then_inc(yo_ps, 1)
                    if i in SPATIAL_AFTER:
                        spatial(SPATIAL_AFTER.index(i))
                    if i == 9:
                        mod_columns((G1, SEG + SC2)[layer])
                    if i == 16:
                        pe.wait_ge(gate_done, 4 * layer + 1)
                        mod_columns((SH2, SEG + G2)[layer])
                pe.wait_ge(proj_evac, WIN * layer + 19)
                square_sums(0)
                square_sums(1)
                within(7)
                square_sums(2)
                square_sums(3)
                pe.wait_ge(y_done, 4 * (layer + 1))
                for i in range(WOUT):
                    if i < 4:
                        pe.wait_ge(mgl_done, GH * layer + KK * (i + 1))
                    sh, sl = (mgh, mgl) if i < 4 else (msh, msl)
                    deep(first_wout[layer] + i, 0, sh, sl, KK * (i % 4), NT, i == 0, i == WOUT - 1)
                    if i == 1:
                        pe.wait_ge(yn_done, layer + 1)
                        for b in range(4):
                            for c in range(4):
                                k, t = 2 * b + c // 2, c % 2
                                ins = pe.transpose(B[b][:, c * P:c * P + P], y[:, t, k * P:k * P + P], ident[:])
                            ins.then_inc(yT_ps, 1)
                    if i == 3:
                        pe.wait_ge(msl_done, layer + 1)
                        broadcast_gate(2 * layer)
                    if layer == 0 and i == 6:
                        mod_columns(SC2)
                turn_x(2 * layer + 1)

                def turn_product(F, nt):
                    pe.wait_ge(act_done, F + 1)
                    if not (isinstance(F, int) and F == 0):
                        pe.wait_ge(actT_done, F)
                    for kk in range(KK):
                        for t in range(nt):
                            ins = pe.transpose(B[2][:, kk * SEQ + t * P:kk * SEQ + t * P + P], actn[:, t, kk * P:kk * P + P], ident[:])
                    ins.then_inc(tp_ps, 1)

                def gate_up(n, F, turn, xh, xl, nt, between, incoming=None, ready=None):
                    pe.wait_ge(sg_done, F)
                    natural(n, turn, lambda t: B[0][:, t * PANEL:(t + 1) * PANEL], xh, xl, nt, ready)
                    if between is not None:
                        turn_product(between, nt)
                    if incoming is not None:
                        gather(incoming)
                    pe.wait_ge(act_done, F)
                    natural(n + 1, turn, lambda t: B[1][:, t * PANEL:(t + 1) * PANEL], xh, xl, nt)

                if layer == 0:
                    gate_up(dense0, 0, 0, hTh, hTl, NT, None, None, h_ready(4))
                    clear_acc(NT)
                    with pe.Fori(0, NJ // 2) as i:
                        for b in range(2):
                            n, F = dense0 + 2 + 3 * b, 2 * i + b + 1
                            gate_up(n, F, i, hTh, hTl, NT, F - 1)
                            pe.wait_ge(actT_done, F)
                            deep(n + 2, i, actTh, actTl, 0, NT, False, False)
                            if b == 0:
                                mod_columns(SEG - 1 + i)
                    turn_product(NJ - 1, NT)
                    pe.wait_ge(sg_done, NJ)
                    pe.wait_ge(act_done, NJ)
                    broadcast_gate(1)
                    pe.wait_ge(actT_done, NJ)
                    deep(dense0 + 3 * NJ - 1, 0, actTh, actTl, 0, NT, False, True)

            pe.wait_ge(hT_done, 16)
            pe.wait_ge(r_landed, 32)
            for t in range(NT):
                for k in range(KD):
                    ins = pe.matmul(B[2][:, t * EXPERTS:(t + 1) * EXPERTS], hT[:, k, t * P:t * P + P], rw[:, k], start=(k == 0), stop=(k == KD - 1), skip_group_check=True)
            ins.then_inc(lg_ps, 1)
            broadcast_gate(3)
            pe.wait_ge(mask_done, 1)
            mk = rt[:, 32:48]
            pe.matmul(B[2][:, 16:24], strict[:], mk[:, 0:8], start=True, stop=True, skip_group_check=True)
            pe.matmul(B[2][:, 24:32], strict[:], mk[:, 8:16], start=True, stop=False, skip_group_check=True)
            pe.matmul(B[2][:, 24:32], ones[:], mk[:, 0:8], start=False, stop=True, skip_group_check=True)
            pe.matmul(B[2][:, 32:40], ones[:], mk[:, 0:8], start=True, stop=False, skip_group_check=True)
            pe.matmul(B[2][:, 32:40], ones[:], mk[:, 8:16], start=False, stop=True, skip_group_check=True).then_inc(pos_ps, 1)
            def gather(job):
                pe.wait_ge(pick_done, job + 1)
                if not isinstance(job, int):
                    pe.wait_ge(scat_done, 2 * job + 1)
                    pe.wait_ge(jobh_done, job)
                for k in range(KD):
                    for t in range(NT):
                        pe.matmul(B[6 + k // 4][:, k % 4 * P:k % 4 * P + P], xn[:, t, k * P:k * P + P], pick[:, t], start=(t == 0), stop=(t == NT - 1), skip_group_check=True)
                for t in range(NT):
                    ins = pe.transpose(B[3][:, t * P:t * P + P], pick[:, t], ident[:])
                ins.then_inc(gather_ps, 1)

            def scatter(job, b, t):
                if t == 0:
                    pe.wait_ge(yl_done, job + 2)
                    pe.wait_ge(h32_done, job + 2)
                pe.wait_ge(scat_done, 2 * job + t + 3)
                for half in range(2):
                    for n, w in enumerate((yh, yl)):
                        ins = pe.matmul(B[6 + half][:], put[b][:, t], w[:, half * 512:half * 512 + 512], start=(n == 0), stop=(n == 1), skip_group_check=True)
                ins.then_inc(scat_ps, 1)

            def moe_iter(n, F, turn, xb, start=False, last=False, incoming=None, ended=None):
                gate_up(n, F, turn, jobh[xb], jobl[xb], 1, F - 1, incoming)
                if ended is not None:
                    scatter(ended, 1 - xb, 0)
                pe.wait_ge(actT_done, F)
                deep(n + 2, turn, actTh, actTl, 0, 1, start, last)
                if ended is not None:
                    scatter(ended, 1 - xb, 1)

            gather(0)
            clear_acc(1)
            pe.wait_ge(table_done, 1)
            pairs = pe.value_load(table[0:1, 0:1], min_val=4, max_val=6)

            pe.wait_ge(jobl_done, 1)
            gate_up(moe0, NJ, 0, jobh[0], jobl[0], 1, None)
            with pe.Fori(0, pairs) as m:
                for b in range(2):
                    job, n0, F0, turn = 2 * m + b, moe0 + 2 + 33 * b, NJ + 22 * m + NJ * b, NJ * m
                    moe_iter(n0, F0 + 1, turn, b, start=True, ended=job - 1)
                    moe_iter(n0 + 3, F0 + 2, turn, b, incoming=job + 1)
                    n0 += 6
                    with pe.Fori(0, 4) as i:
                        for c in range(2):
                            moe_iter(n0 + 3 * c, F0 + 2 * i + c + 3, turn + i, b)
                    pe.wait_ge(jobl_done, job + 2)
                    moe_iter(n0 + 24, F0 + NJ, turn, 1 - b, last=True)
            for t in range(NT):
                scatter(2 * pairs - 1, 1, t)

        @block.vector
        def _(dve):
            o = Order(dve, dve_order)
            link, step = o.link, o.step

            def lo(n, turn=0):
                dve.wait_ge(hi_done, n + 1 + RING * turn)
                h, l = pair_of(n)
                dve.tensor_tensor(l, raw[:, slot(n)], h.bitcast(F32), ALU.subtract).then_inc(split_done, 1)

            def ada(layer, seg, k):
                a = 8 * (SEG * layer + seg - 2) + k
                half = 4 * (SEG * layer + seg - 2) + k // 2
                dve.wait_ge(ada_landed[k % 2], 16 * half + 16)
                if k == 0:
                    dve.wait_ge(mod_ps, SEG * layer + seg)
                    dve.tensor_scalar(acc[:], adaw[:, 0], cond[:, 0:1], None, ALU.mult).then_inc(ada_used, 1)
                else:
                    dve.wait_ge(ada_used, a)
                    dve.scalar_tensor_tensor(acc[:], adaw[:, k % 2], cond[:, k:k + 1], acc[:], ALU.mult, ALU.add).then_inc(ada_used, 1)

            def mod_evac(s):
                dve.wait_ge(mod_ps, s + 1)
                dve.tensor_tensor(mod[:, bass.ds(s, 1)].rearrange("p a k -> p (a k)"), B[3][:, 0:KD], abcol[:, bass.ds(s * KD, KD)], ALU.add).then_inc(mod_done, 1)

            def normalise(n, t):
                dve.wait_ge(rms_done, NT * n + t + 1)
                link(dve.reciprocal(ss[:, 2 + t:3 + t], ss[:, 2 + t:3 + t]))
                dve.tensor_scalar(xn[:, t], x[:, t], ss[:, 2 + t:3 + t], None, ALU.mult).then_inc(xn_ready, 1)

            def modulate(n, layer, shift, scale, low=True):
                dve.wait_ge(mod_done, SEG * layer + scale + 1)
                link(dve.tensor_scalar(mod[:, SEG * layer + scale], mod[:, SEG * layer + scale], 1.0, None, ALU.add))

                def low_part(b):
                    dve.wait_ge(hTh_done, 4 * n + b + 1)
                    dve.tensor_tensor(hTl[:, 2 * b:2 * b + 2], hT[:, 2 * b:2 * b + 2], hTh[:, 2 * b:2 * b + 2].bitcast(F32), ALU.subtract).then_inc(hTl_done, 1)

                for b in range(4):
                    dve.wait_ge(xT_ps, 4 * n + b + 1)
                    for kk in range(2):
                        k = 2 * b + kk
                        ins = dve.tensor_scalar(hT[:, k], B[4 + b][:, kk * SEQ:kk * SEQ + SEQ], mod[:, SEG * layer + scale, k:k + 1],
                                                mod[:, SEG * layer + shift, k:k + 1], ALU.mult, ALU.add)
                    ins.then_inc(hT_done, 1)
                    if low and b:
                        low_part(b - 1)
                if low:
                    low_part(3)

            def make_diag(n, layer, seg):
                dve.wait_ge(mod_done, SEG * layer + seg + 1)
                for k in range(KD):
                    ins = dve.tensor_scalar(diag[:, k], ident[:], mod[:, SEG * layer + seg, k:k + 1], None, ALU.mult)
                ins.then_inc(diag_done, 1)

            def residual(n, source, tmp, ended=None, between=None):
                dve.wait_ge(gb_done, n + 1)
                for q in range(4):
                    t, half = divmod(q, 2)
                    if ended is not None and q == 0:
                        dve.wait_ge(tile_done, n + 1)
                    if ended is not None and q == 2:
                        dve.wait_ge(gemm_done, ended)
                    if between is not None and q == 2:
                        between()
                        dve.wait_ge(scat_done, 4 * pairs + 3)
                    if q == 3:
                        dve.wait_ge(x_tile, n + 1)
                    link(dve.scalar_tensor_tensor(tmp(q), gbc[:, half * 512:half * 512 + 512], 1.0, source(q), ALU.add, ALU.mult))
                    if q == 3 and n < 3:
                        normalise(n + 1, 0)
                    ins = dve.tensor_tensor(x[:, t, half * 512:half * 512 + 512], x[:, t, half * 512:half * 512 + 512], tmp(q), ALU.add)
                    if q % 2:
                        ins.then_inc((x_tile, x_done)[t], 1)
                    else:
                        step(ins)

            def scratch(q):
                return diag[:, 4 * (q % 2):4 * (q % 2) + 4].rearrange("p k n -> p (k n)")

            dve.wait_ge(consts, 1)
            dve.wait_ge(cond_ready, 1)
            for k in range(START):
                dve.wait_ge(landed[k % RING], 16 * (k // RING + 1))
                if k == 0:
                    dve.tensor_scalar(acc0[:], raw[:, 0], cond[:, 0:1], None, ALU.mult).then_inc(split_done, 1)
                else:
                    dve.wait_ge(split_done, k)
                    dve.scalar_tensor_tensor(acc0[:], raw[:, k % RING], cond[:, k:k + 1], acc0[:], ALU.mult, ALU.add).then_inc(split_done, 1)
                if k == 5:
                    normalise(0, 0)
                    normalise(0, 1)
            dve.wait_ge(small_ps, 1)
            for layer in range(LAYERS):
                dve.tensor_copy(pcol[:, layer], B[2][:, 2 * layer * P:2 * layer * P + SMALL])
                dve.tensor_copy(abcol[:, layer * SEG * KD:(layer + 1) * SEG * KD], B[2][:, (2 * layer + 1) * P:(2 * layer + 1) * P + SEG * KD]).then_inc(small_used, 1)
            dve.wait_ge(small_used, LAYERS)
            lo(first_win[0])
            dve.wait_ge(mod_ps, 2)
            dve.tensor_tensor(mod[:, 0:2].rearrange("p a k -> p (a k)"), B[3][:, 0:2 * KD], abcol[:, 0:2 * KD], ALU.add).then_inc(mod_done, 2)

            for layer in range(LAYERS):
                g0 = first_win[layer]
                if layer:
                    normalise(2 * layer, 1)
                    lo(g0)
                modulate(2 * layer, layer, SH1, SC1)
                lo(g0 + 1)
                T = [dtt[:, n] for n in range(6)]

                def gather_y(i):
                    c, g = divmod(i, GROUPS)
                    yt = y[:, c, g * 256:g * 256 + 256]
                    dve.wait_ge(yd_ps, 8 * layer + (i | 1) + 1)
                    ins = dve.tensor_tensor(yt, yt, B[4 + i // 2 % 2][:, i % 2 * 256:i % 2 * 256 + 256], ALU.add)
                    if c:
                        link(ins)
                        dve.wait_ge(yo_ps, layer + 1)
                        link(dve.tensor_tensor(yoff[:].rearrange("p (e d) -> p e d", e=HPG), B[6 + g // 2][:, g % 2 * 256:g % 2 * 256 + 256].rearrange("p (e d) -> p e d", e=HPG),
                                               T[5][:, HEADS + g * HPG:HEADS + (g + 1) * HPG].unsqueeze(2).broadcast_to([P, HPG, HD]), ALU.mult))
                        ins = dve.tensor_tensor(yt, yt, yoff[:], ALU.add)
                    if i % 2:
                        ins.then_inc(y_done, 1)
                    else:
                        step(ins)

                def segment(i):
                    dve.wait_ge(seg_ps, 8 * layer + i + 1)
                    if i >= 2:
                        dve.wait_ge(yd_ps, 8 * layer + i - 1)
                    for e in range(HPG):
                        h = i // GROUPS * HEADS + i % GROUPS * HPG + e
                        ins = dve.tensor_scalar(dec[:, i % 2, e], B[2][:, e * P:e * P + P], T[4][:, h:h + 1], 0.0, ALU.subtract, ALU.min)
                    ins.then_inc(seg_done, 1)

                def gate_heads(b):
                    dve.wait_ge(bs_landed, 16 * (layer + 1))
                    dve.wait_ge(sv_ps, 4 * layer + b + 1)
                    dve.wait_ge(proj_evac, WIN * layer + 13 + b)
                    for h in (2 * b, 2 * b + 1):
                        tmp = gtmp[:, h % 2].rearrange("p (c t) -> p c t", c=NT)
                        link(dve.scalar_tensor_tensor(tmp, B[3][:, h % 2 * SEQ:h % 2 * SEQ + SEQ].rearrange("p (c t) -> p c t", c=NT),
                                                      pcol[:, layer, VNW + h:VNW + h + 1], bsb[:, h].unsqueeze(1).broadcast_to([P, NT, P]), ALU.mult, ALU.add))
                        ins = dve.tensor_tensor(u[:, h].rearrange("p (c t) -> p c t", c=NT), u[:, h].rearrange("p (c t) -> p c t", c=NT), tmp, ALU.mult)
                        if h % 2:
                            ins.then_inc(gate_done, 1)
                        else:
                            step(ins)

                for i in range(WIN):
                    if i < WIN - 1:
                        lo(g0 + i + 2)
                    if i == 1:
                        dve.wait_ge(dt_ps, layer + 1)
                        dve.wait_ge(hv_landed, 48 * (layer + 1))
                        link(dve.tensor_tensor(T[0].rearrange("p (c h) -> p c h", c=NT), B[2][:, 0:NT * HEADS].rearrange("p (c h) -> p c h", c=NT),
                                               hv[:, 0].unsqueeze(1).broadcast_to([P, NT, HEADS]), ALU.add))
                        link(dve.tensor_scalar(T[1], T[0], -1.0, None, ALU.mult))
                        dve.tensor_tensor(T[1], T[0], T[1], ALU.max).then_inc(dt_abs, 1)
                    if i == 8:
                        dve.wait_ge(dt_exp, 2 * layer + 2)
                        link(dve.tensor_scalar(T[3], T[1], 2.0, None, ALU.add))
                        link(dve.reciprocal(T[3], T[3]))
                        link(dve.tensor_tensor(T[3], T[3], T[1], ALU.mult))
                        link(dve.tensor_tensor(T[4], T[3], T[3], ALU.mult))
                        link(dve.tensor_scalar(T[5], T[4], 1.0 / 15, 1.0 / 13, ALU.mult, ALU.add))
                    if i == 4:
                        for b in range(2):
                            dve.wait_ge(wsT_ps, 2 * layer + b + 1)
                            ins = dve.tensor_tensor(wsT[:, 4 * b:4 * b + 4], B[4 + b][:].rearrange("p (h t) -> p h t", h=4), upper[:].unsqueeze(1).broadcast_to([P, 4, P]), ALU.mult)
                        ins.then_inc(wsT_done, 1)
                    if i in (8, 9):
                        for c in ((11, 9, 7), (5, 3, 1))[i - 8]:
                            link(dve.tensor_tensor(T[5], T[5], T[4], ALU.mult))
                            link(dve.tensor_scalar(T[5], T[5], 1.0 / c, None, ALU.add))
                    if i == 9:
                        link(dve.scalar_tensor_tensor(T[3], T[3], 2.0, T[5], ALU.mult, ALU.mult))
                        link(dve.tensor_scalar(T[0], T[0], 0.0, None, ALU.max))
                        link(dve.tensor_tensor(T[0], T[0], T[3], ALU.add))
                        dve.scalar_tensor_tensor(T[2].rearrange("p (c h) -> p c h", c=NT), T[0].rearrange("p (c h) -> p c h", c=NT), -1.0,
                                                 hv[:, 1].unsqueeze(1).broadcast_to([P, NT, HEADS]), ALU.mult, ALU.mult).then_inc(dA_done, 1)
                    if i in (9, 16):
                        mod_evac((G1, SEG + SC2)[layer] + i // 16)
                    for part in early_ada(layer, i):
                        ada(*part)
                    if i == 10:
                        dve.wait_ge(acs_ps, layer + 1)
                        link(dve.tensor_copy(T[4], B[2][:, 0:NT * HEADS]))
                        step(dve.tensor_tensor(T[5][:, 0:HEADS], B[2][:, 2 * HEADS:3 * HEADS], T[4][:, 0:HEADS], ALU.subtract))
                        dve.tensor_copy(T[5][:, HEADS:2 * HEADS], T[4][:, HEADS:2 * HEADS]).then_inc(acs_done, 1)
                    if i < CX // 2:
                        dve.wait_ge(proj_evac, WIN * layer + i + 1)
                        wc, (c0, c1) = pcol[:, layer], chunks(i)
                        for j in range(CONV_K - 1):
                            for c in (c0, c1):
                                if j:
                                    dve.wait_ge(dve_order, o.n if j == CONV_K - 2 and c == c1 else o.n - 1)
                                ins = dve.scalar_tensor_tensor(xbc[:, c], padded[:, c, j:j + SEQ], wc[:, j * CX + c:j * CX + c + 1], xbc[:, c], ALU.mult, ALU.add)
                                if j < CONV_K - 2:
                                    step(ins)
                                else:
                                    ins.then_inc(conv_done, 1)
                    if i == 8:
                        for c in range(NT):
                            dve.wait_ge(cb_ps, 2 * layer + c + 1)
                            dve.tensor_tensor(cbm[:, c], B[6 + c][:].rearrange("p (g q) -> p g q", g=GROUPS), upper[:].unsqueeze(1).broadcast_to([P, GROUPS, P]), ALU.mult).then_inc(cb_done, 1)
                    if i >= SCAN:
                        segment(i - SCAN)
                    if i == 12:
                        dve.wait_ge(acs_exp, layer + 1)
                        dve.wait_ge(xs_done, layer + 1)
                        dve.wait_ge(skip_done, NT * layer + 1)
                        xt = xs[:, 0].rearrange("p (h d) -> p h d", h=HEADS)
                        link(dve.tensor_tensor(xt, xt, T[0][:, 0:HEADS].unsqueeze(2).broadcast_to([P, HEADS, HD]), ALU.mult))
                        dve.tensor_tensor(xdec[:].rearrange("p (h d) -> p h d", h=HEADS), xs[:, 0].rearrange("p (h d) -> p h d", h=HEADS),
                                          T[5][:, 0:HEADS].unsqueeze(2).broadcast_to([P, HEADS, HD]), ALU.mult).then_inc(xdt_done, 1)
                    if i == 13:
                        dve.wait_ge(v_sq, layer + 1)
                        dve.tensor_reduce(vs[:], vsq[:].rearrange("p a (h d) -> p (a h) d", d=P), AX_X, ALU.add).then_inc(v_sum, 1)
                    if i == 14:
                        dve.wait_ge(v_ms, layer + 1)
                        link(dve.reciprocal(vs[:], vs[:]))
                        vh = v[:].rearrange("p t (h d) -> p (t h) d", d=P)
                        dve.tensor_tensor(vh, vh, vs[:].unsqueeze(2).broadcast_to([P, NT * GH, P]), ALU.mult).then_inc(v_done, 1)
                    if i in SPATIAL_AFTER:
                        gate_heads(SPATIAL_AFTER.index(i))
                    if i in (15, 17, 19):
                        gather_y(i - 15)
                        gather_y(i - 14)
                gather_y(6)
                gather_y(7)
                dve.wait_ge(grms_done, layer + 1)
                link(dve.reciprocal(rroot[:], B[0][:, 0:SEQ]))

                def gated_low(h):
                    dve.wait_ge(mgh_done, GH * layer + h + 1)
                    dve.wait_ge(u_done, 4 * layer + h // 2 + 1)
                    dve.scalar_tensor_tensor(mgl[:, h], u[:, h], pcol[:, layer, ONW + h:ONW + h + 1], mgh[:, h].bitcast(F32), ALU.mult, ALU.subtract).then_inc(mgl_done, 1)

                for b in range(4):
                    dve.tensor_tensor(u[:, 2 * b:2 * b + 2], u[:, 2 * b:2 * b + 2], rroot[:].unsqueeze(1).broadcast_to([P, 2, SEQ]), ALU.mult).then_inc(u_done, 1)
                    if b:
                        gated_low(2 * b - 2)
                        gated_low(2 * b - 1)
                gated_low(6)
                gated_low(7)
                lo(first_wout[layer] + 1)
                dve.wait_ge(y_done, 4 * (layer + 1))
                dve.wait_ge(proj_evac, WIN * (layer + 1))
                for t in range(NT):
                    ins = dve.tensor_tensor(y[:, t], y[:, t], z[:, t], ALU.mult)
                    if t < NT - 1:
                        step(ins)
                ins.then_inc(yz_done, 1)
                dve.wait_ge(yms_done, layer + 1)
                link(dve.reciprocal(ss[:, 6:8], ss[:, 6:8]))
                for t in range(NT):
                    ins = dve.tensor_scalar(y[:, t], y[:, t], ss[:, 6 + t:7 + t], None, ALU.mult)
                    if t < NT - 1:
                        step(ins)
                ins.then_inc(yn_done, 1)
                for i in range(WOUT):
                    if i >= 2:
                        lo(first_wout[layer] + i)
                    if i == 3:
                        for k in range(KD):
                            dve.wait_ge(msh_done, KD * layer + k // 2 * 2 + 2)
                            ins = dve.scalar_tensor_tensor(msl[:, k], B[k // 2][:, k % 2 * SEQ:k % 2 * SEQ + SEQ], pcol[:, layer, SSDW + k:SSDW + k + 1],
                                                           msh[:, k].bitcast(F32), ALU.mult, ALU.subtract)
                        ins.then_inc(msl_done, 1)
                        make_diag(2 * layer, layer, G1)
                    if layer == 0:
                        if i == 7:
                            mod_evac(SC2)
                        for part in late_ada(i):
                            ada(*part)
                after = dense0 if layer == 0 else moe0
                residual(2 * layer, lambda q: B[4 + q][:], scratch, first_wout[layer] + WOUT)
                normalise(2 * layer + 1, 1)
                lo(after)
                modulate(2 * layer + 1, layer, SH2, SC2, low=(layer == 0))
                lo(after + 1)
                if layer:
                    dve.wait_ge(x_done, 3)
                    make_diag(3, 1, G2)
                if layer == 0:
                    for k in range(2, 4):
                        ada(0, G2, k)

                def product(n, F, turn, nt):
                    dve.wait_ge(sg_done, F + 1)
                    dve.wait_ge(gemm_done, n + RING * turn)
                    dve.tensor_tensor(actn[:, 0:nt], gate[:, 0:nt], B[1][:].rearrange("p (t n) -> p t n", t=NT)[:, 0:nt], ALU.mult).then_inc(act_done, 1)

                def turned_low(F, nt):
                    dve.wait_ge(actTh_done, F + 1)
                    dve.tensor_tensor(actTl[:, :, 0:nt * P], B[2][:].rearrange("p (k t) -> p k t", k=KK)[:, :, 0:nt * P],
                                      actTh[:, :, 0:nt * P].bitcast(F32), ALU.subtract).then_inc(actT_done, 1)

                if layer == 0:
                    with dve.Fori(0, NJ // 2) as i:
                        for b in range(2):
                            n, F = dense0 + 2 + 3 * b, 2 * i + b + 1
                            lo(n, i)
                            if b == 1:
                                mod_evac(SEG - 1 + i)
                            ada(0, SEG - 1 + i + b, 4 * (1 - b))
                            ada(0, SEG - 1 + i + b, 4 * (1 - b) + 1)
                            lo(n + 1, i)
                            product(n, F - 1, i, NT)
                            ada(0, SEG - 1 + i + b, 4 * (1 - b) + 2)
                            lo(n + 2, i)
                            turned_low(F - 1, NT)
                            ada(0, SEG - 1 + i + b, 4 * (1 - b) + 3)
                    make_diag(1, 0, G2)
                    product(dense0 + 3 * NJ - 1, NJ - 1, 0, NT)
                    lo(dense0 + 3 * NJ - 1)
                    turned_low(NJ - 1, NT)
                    residual(1, lambda q: B[4 + q][:], scratch, dense0 + 3 * NJ)

            DIFF, P1, MX, MASK, GATE, OH, POS, CNT, RANK, SEL = (rt[:, 0:2], rt[:, 2:4], rt[:, 16:32], rt[:, 32:48], rt[:, 48:64],
                                                               rt[:, 64:80], rt[:, 80:96], rt[:, 96:104], rt[:, 104:112], rt[:, 112:120])
            LG, IX, JP, JG, JE, CUR, TMP8, NOV, TMP = (rt[:, 120:136], rt[:, 136:152], rt[:, 152:180], rt[:, 180:208], rt[:, 208:224],
                                                  rt[:, 224:228], rt[:, 228:236], rt[:, 236:240], rt[:, 240:256])

            def v3(a):
                return a.rearrange("p (t e) -> p t e", t=NT)

            link(dve.memset(rt[:], 0.0))
            link(dve.memset(JP, -1.0))
            dve.wait_ge(lg_ps, 1)
            link(dve.tensor_tensor(v3(LG), B[2][:, 0:16].rearrange("p (t e) -> p t e", t=NT), rb[:].unsqueeze(1).broadcast_to([P, NT, EXPERTS]), ALU.add))
            for t in range(NT):
                link(dve.max(MX[:, 8 * t:8 * t + 8], LG[:, 8 * t:8 * t + 8]))
                link(dve.max_index(tix[:, t], MX[:, 8 * t:8 * t + 8], LG[:, 8 * t:8 * t + 8]))
            link(dve.tensor_copy(v3(IX), tix[:]))
            dve.tensor_tensor(DIFF, v3(MX)[:, :, 1], v3(MX)[:, :, 0], ALU.subtract).then_inc(rdiff, 1)
            dve.wait_ge(rexp, 1)
            link(dve.tensor_scalar(P1, DIFF, 1.0, None, ALU.add))
            link(dve.reciprocal(P1, P1))
            link(dve.tensor_tensor(DIFF, DIFF, P1, ALU.mult))
            i8b = i8[:].unsqueeze(1).broadcast_to([P, NT, EXPERTS])

            def over_experts(a):
                return a.unsqueeze(2).broadcast_to([P, NT, EXPERTS])

            link(dve.tensor_tensor(v3(MASK), i8b, over_experts(v3(IX)[:, :, 0]), ALU.is_equal))
            step(dve.tensor_tensor(v3(OH), i8b, over_experts(v3(IX)[:, :, 1]), ALU.is_equal))
            link(dve.tensor_tensor(v3(GATE), v3(MASK), over_experts(P1), ALU.mult))
            step(dve.tensor_tensor(v3(TMP), v3(OH), over_experts(DIFF), ALU.mult))
            dve.tensor_tensor(MASK, MASK, OH, ALU.add).then_inc(mask_done, 1)
            dve.wait_ge(dve_order, o.n)
            link(dve.tensor_tensor(GATE, GATE, TMP, ALU.add))
            dve.wait_ge(mask_done, 1)
            dve.wait_ge(pos_ps, 1)
            link(dve.scalar_tensor_tensor(POS, B[2][:, 16:32], 1.0, MASK, ALU.add, ALU.mult))
            link(dve.tensor_scalar(POS, POS, -1.0, None, ALU.add))
            JP3, JG3 = (a.rearrange("p (t j) -> p t j", t=NT) for a in (JP, JG))
            link(dve.tensor_copy(JP3[:, :, 0:8], v3(POS)))

            def make_pick(job):
                link(dve.tensor_copy(CUR[:, 0:2].unsqueeze(2), JP3[:, :, bass.ds(job, 1)]))
                for t in range(NT):
                    ins = dve.tensor_scalar(pick[:, t], slots[:], CUR[:, t:t + 1], None, ALU.is_equal)
                    if t < NT - 1:
                        step(ins)
                ins.then_inc(pick_done, 1)

            make_pick(0)
            link(dve.tensor_scalar(CNT, B[2][:, 32:40], float(P), None, ALU.is_gt))
            for e in range(1, EXPERTS):
                link(dve.tensor_tensor(RANK[:, e:e + 1], RANK[:, e - 1:e], CNT[:, e - 1:e], ALU.add))
            link(dve.tensor_tensor(NOV[:, 0:1], RANK[:, 7:8], CNT[:, 7:8], ALU.add))
            link(dve.tensor_scalar(NOV[:, 1:2], NOV[:, 0:1], 1.0, None, ALU.is_ge))
            link(dve.tensor_scalar(NOV[:, 2:3], NOV[:, 0:1], 3.0, 4.0, ALU.is_ge, ALU.add))
            link(dve.tensor_tensor(JE[:, 0:1], NOV[:, 1:2], NOV[:, 2:3], ALU.add))
            link(dve.tensor_copy(JE[:, 1:9], i8[:]))
            link(dve.tensor_copy(JG3[:, :, 1:9], v3(GATE)))
            for k in range(4):
                link(dve.scalar_tensor_tensor(SEL, RANK, float(k), CNT, ALU.is_equal, ALU.mult))
                link(dve.tensor_tensor(TMP8, i8[:], SEL, ALU.mult))
                link(dve.tensor_reduce(JE[:, 9 + k:10 + k], TMP8, AX_X, ALU.add))
            dve.wait_ge(scat_done, 1)
            dve.wait_ge(put_cleared, 1)
            dve.tensor_copy(table[:, 0:16], JE).then_inc(table_done, 1)
            dve.wait_ge(table_done, 1)
            pairs = dve.value_load(table[0:1, 0:1], min_val=4, max_val=6)

            def job_in(job, b):
                dve.wait_ge(jobh_done, job + 1)
                dve.tensor_tensor(jobl[b][:], h32[:], jobh[b][:].bitcast(F32), ALU.subtract).then_inc(jobl_done, 1)

            def job_out(job):
                dve.wait_ge(yh_done, job + 2)
                for half in range(2):
                    ins = dve.tensor_tensor(yl[:, half * 512:half * 512 + 512], B[4 + half][:], yh[:, half * 512:half * 512 + 512].bitcast(F32), ALU.subtract)
                ins.then_inc(yl_done, 1)
                link(dve.tensor_copy(CUR[:, 2:4].unsqueeze(2), JG3[:, :, bass.ds(job + 1, 1)]))

            def add_rows(job, t):
                dve.wait_ge(scat_ps, 2 * job + t + 3)
                for half in range(2):
                    m_ = mixed[:, t, half * 512:half * 512 + 512]
                    ins = dve.scalar_tensor_tensor(m_, B[6 + half][:], CUR[:, 2 + t:3 + t], m_, ALU.mult, ALU.add)
                ins.then_inc(scat_done, 1)

            def moe_iter(n, F, turn, ended=None, ended_before=None, incoming=None, begun=False):
                if not begun:
                    lo(n, turn)
                if ended_before is None:
                    lo(n + 1, turn)
                    product(n, F - 1, turn, 1)
                else:
                    product(n, F - 1, turn, 1)
                    add_rows(ended_before, 1)
                    make_pick(incoming)
                    lo(n + 1, turn)
                if ended is not None:
                    job_out(ended)
                lo(n + 2, turn)
                turned_low(F - 1, 1)
                if ended is not None:
                    add_rows(ended, 0)

            IN, OUT = 2, 1
            job_in(0, 0)
            for k in range(4):
                link(dve.scalar_tensor_tensor(SEL, RANK, float(k), CNT, ALU.is_equal, ALU.mult))
                selected = SEL.unsqueeze(1).broadcast_to([P, NT, EXPERTS])
                link(dve.scalar_tensor_tensor(v3(TMP), v3(POS), 1.0 - P, selected, ALU.add, ALU.mult))
                link(dve.tensor_reduce(JP3[:, :, 8 + k], v3(TMP), AX_X, ALU.add))
                link(dve.tensor_scalar(JP3[:, :, 8 + k], JP3[:, :, 8 + k], -1.0, None, ALU.add))
                link(dve.tensor_tensor(v3(TMP), v3(GATE), selected, ALU.mult))
                link(dve.tensor_reduce(JG3[:, :, 9 + k], v3(TMP), AX_X, ALU.add))
            done = o.n
            with dve.Fori(0, pairs) as m:
                o.n = done + 2 * (IN + OUT) * m
                for b in range(2):
                    job, n0, F0, turn = 2 * m + b, moe0 + 2 + 33 * b, NJ + 22 * m + NJ * b, NJ * m
                    moe_iter(n0, F0 + 1, turn, ended=job - 1)
                    moe_iter(n0 + 3, F0 + 2, turn, ended_before=job - 1, incoming=job + 1)
                    n0 += 6
                    lo(n0, turn)
                    job_in(job + 1, 1 - b)
                    moe_iter(n0, F0 + 3, turn, begun=True)
                    n0 += 3
                    with dve.Fori(0, 3) as i:
                        for c in range(2):
                            moe_iter(n0 + 3 * c, F0 + 2 * i + c + 4, turn + i)
                    moe_iter(n0 + 18, F0 + NJ - 1, turn)
                    moe_iter(n0 + 21, F0 + NJ, turn)
            o.n = done + 2 * (IN + OUT) * pairs
            job_out(2 * pairs - 1)
            add_rows(2 * pairs - 1, 0)
            dve.wait_ge(scat_done, 4 * pairs + 2)
            residual(3, lambda q: mixed[:, q // 2, q % 2 * 512:q % 2 * 512 + 512], scratch,
                     between=lambda: add_rows(2 * pairs - 1, 1))
            dve.wait_ge(fn_landed, 16)
            for t in range(NT):
                dve.wait_ge(rms_done, 4 * NT + t + 1)
                link(dve.reciprocal(ss[:, 2 + t:3 + t], ss[:, 2 + t:3 + t]))
                dve.scalar_tensor_tensor(xn[:, t], x[:, t], ss[:, 2 + t:3 + t], fnw[:], ALU.mult, ALU.mult).then_inc(out_done, 1)


_INS = ["x", "c", "ada_w", "ada_b", "w_in", "conv_w", "conv_b", "dt_bias", "a_log", "d_skip", "ssd_norm_w",
        "gmlp_v_norm_w", "gmlp_ws", "gmlp_bs", "gmlp_out_norm_w", "w_out", "dense_w_gate", "dense_w_up",
        "dense_w_down", "router_w", "router_b", "moe_w_gate", "moe_w_up", "moe_w_down", "final_norm_w"]


def kernel(**inputs):
    import numpy as np
    import concourse.bacc as bacc
    from concourse.bass_utils import run_bass_kernel_spmd

    nc = bacc.Bacc("TRN2", target_bir_lowering=False, num_devices=1)
    arrays, args = {}, []
    for name in _INS:
        a = np.ascontiguousarray(inputs[name])
        arrays[f"in_{name}"] = a
        args.append(nc.dram_tensor(f"in_{name}", a.shape, mybir.dt.from_np(a.dtype), kind="ExternalInput").ap())
    out = nc.dram_tensor("out", (1, SEQ, D), F32, kind="ExternalOutput").ap()
    hybrid_trunk(nc, *args, out)
    r = run_bass_kernel_spmd(nc, [arrays], core_ids=[0])
    return r.results[0]["out"]
```
